# Optimizing a Trainium2 kernel written in Bass

```python
import jax, jax.numpy as jnp
from jax import lax
import numpy as np

D_MODEL = 1024
BATCH = 1
SEQ = 256
DEPTH = 2

N_MIXERS = 2
N_ATTN_LAYERS = (DEPTH + 1) // 2
N_SGU_LAYERS = DEPTH // 2

N_HEADS = 16
N_KV_HEADS = 4
HEAD_DIM = 64
Q_PER_KV = N_HEADS // N_KV_HEADS
WINDOW = 128
BLOCK = 128
Q_DIM = N_HEADS * HEAD_DIM
KV_DIM = N_KV_HEADS * HEAD_DIM
QKV_DIM = Q_DIM + 2 * KV_DIM
ALIBI_MAX_BIAS = 8.0

CHUNK = 128
SGU_HALF = 3 * D_MODEL
N_SGU_GROUPS = 8
SGU_GROUP_DIM = SGU_HALF // N_SGU_GROUPS

D_FF = 2816
CONV_WIDTH = 3

EPS = 1e-6


def rms_norm(x, g):
    xf = x.astype(jnp.float32)
    y = xf * lax.rsqrt(jnp.mean(xf * xf, axis=-1, keepdims=True) + EPS)
    return (y * g.astype(jnp.float32)).astype(x.dtype)

def layer_norm(x, g, b):
    xf = x.astype(jnp.float32)
    mu = jnp.mean(xf, axis=-1, keepdims=True)
    xc = xf - mu
    y = xc * lax.rsqrt(jnp.mean(xc * xc, axis=-1, keepdims=True) + EPS)
    return (y * g.astype(jnp.float32) + b.astype(jnp.float32)).astype(x.dtype)

def alibi_slopes():
    h = jnp.arange(1, N_HEADS + 1, dtype=jnp.float32)
    return jnp.exp2(-ALIBI_MAX_BIAS * h / N_HEADS)

def sliding_window_attention(h, w_qkv, b_qkv, sinks, w_o, b_o):
    B, S, _ = h.shape
    nb = S // BLOCK
    qkv = h @ w_qkv + b_qkv
    q, k, v = jnp.split(qkv, [Q_DIM, Q_DIM + KV_DIM], axis=-1)
    q = q.reshape(B, nb, BLOCK, N_KV_HEADS, Q_PER_KV, HEAD_DIM)
    k = k.reshape(B, nb, BLOCK, N_KV_HEADS, HEAD_DIM)
    v = v.reshape(B, nb, BLOCK, N_KV_HEADS, HEAD_DIM)

    def with_prev(t):
        prev = jnp.concatenate([jnp.zeros_like(t[:, :1]), t[:, :-1]], axis=1)
        return jnp.concatenate([prev, t], axis=2)

    kb, vb = with_prev(k), with_prev(v)
    scores = jnp.einsum("bnqgrd,bnkgd->bngrqk", q, kb).astype(jnp.float32) * (HEAD_DIM ** -0.5)

    qi = jnp.arange(BLOCK)[:, None]
    kj = jnp.arange(2 * BLOCK)[None, :]
    dist = qi + BLOCK - kj
    key_pos = jnp.arange(nb)[:, None, None] * BLOCK - BLOCK + kj[None]
    valid = (dist >= 0)[None] & (dist < WINDOW)[None] & (key_pos >= 0)

    slopes = alibi_slopes().reshape(N_KV_HEADS, Q_PER_KV)
    scores = scores - slopes[:, :, None, None] * dist.astype(jnp.float32)
    scores = jnp.where(valid[None, :, None, None], scores, -jnp.inf)

    sink = sinks.astype(jnp.float32).reshape(N_KV_HEADS, Q_PER_KV)[None, None, :, :, None, None]
    m = jnp.maximum(jnp.max(scores, axis=-1, keepdims=True), sink)
    p = jnp.exp(scores - m)
    probs = p / (jnp.sum(p, axis=-1, keepdims=True) + jnp.exp(sink - m))

    out = jnp.einsum("bngrqk,bnkgd->bnqgrd", probs.astype(h.dtype), vb)
    return out.reshape(B, S, Q_DIM) @ w_o + b_o

def chunked_sgu(h, w_in, ln_g, ln_b, w_s, b_s, w_out):
    B, S, _ = h.shape
    nc = S // CHUNK
    z = jax.nn.gelu(h @ w_in)
    u, v = jnp.split(z, 2, axis=-1)
    v = layer_norm(v, ln_g, ln_b)
    v = v.reshape(B, nc, CHUNK, N_SGU_GROUPS, SGU_GROUP_DIM)
    causal = jnp.tril(jnp.ones((CHUNK, CHUNK), dtype=bool))
    ws = jnp.where(causal[None], w_s, jnp.zeros_like(w_s))
    sv = jnp.einsum("gts,bcsgd->bctgd", ws, v) + b_s.T[None, None, :, :, None]
    return (u * sv.reshape(B, S, SGU_HALF)) @ w_out

def conv_gated_ffn(h, w_in, conv_w, conv_b, w_out):
    S = h.shape[1]
    g, u = jnp.split(h @ w_in, 2, axis=-1)
    gp = jnp.pad(g, ((0, 0), (CONV_WIDTH - 1, 0), (0, 0)))
    g = conv_b + sum(conv_w[k] * gp[:, k:k + S] for k in range(CONV_WIDTH))
    return (jax.nn.gelu(g) * u) @ w_out

def first_inputs(seed: int = 0) -> dict:
    key = jax.random.key(seed)
    ks = jax.random.split(key, 24)
    f32 = jnp.float32

    def nrm(k, shape, scale):
        return jax.random.normal(k, shape, f32) * scale

    nA, nB = N_ATTN_LAYERS, N_SGU_LAYERS
    return {
        "x": nrm(ks[0], (BATCH, SEQ, D_MODEL), 1.0),
        "attn_w_qkv": nrm(ks[1], (nA, D_MODEL, QKV_DIM), D_MODEL ** -0.5),
        "attn_b_qkv": nrm(ks[2], (nA, QKV_DIM), 0.02),
        "attn_sinks": nrm(ks[3], (nA, N_HEADS), 1.0),
        "attn_w_o": nrm(ks[4], (nA, Q_DIM, D_MODEL), Q_DIM ** -0.5),
        "attn_b_o": nrm(ks[5], (nA, D_MODEL), 0.02),
        "sgu_w_in": nrm(ks[6], (nB, D_MODEL, 2 * SGU_HALF), D_MODEL ** -0.5),
        "sgu_ln_g": 1.0 + nrm(ks[7], (nB, SGU_HALF), 0.05),
        "sgu_ln_b": nrm(ks[8], (nB, SGU_HALF), 0.02),
        "sgu_w_s": nrm(ks[9], (nB, N_SGU_GROUPS, CHUNK, CHUNK), CHUNK ** -0.5),
        "sgu_b_s": 1.0 + nrm(ks[10], (nB, N_SGU_GROUPS, CHUNK), 0.05),
        "sgu_w_out": nrm(ks[11], (nB, SGU_HALF, D_MODEL), SGU_HALF ** -0.5),
        "ffn_w_in": nrm(ks[12], (DEPTH, D_MODEL, 2 * D_FF), D_MODEL ** -0.5),
        "ffn_conv_w": nrm(ks[13], (DEPTH, CONV_WIDTH, D_FF), CONV_WIDTH ** -0.5),
        "ffn_conv_b": nrm(ks[14], (DEPTH, D_FF), 0.02),
        "ffn_w_out": nrm(ks[15], (DEPTH, D_FF, D_MODEL), D_FF ** -0.5),
        "norm_mix_pre": 1.0 + nrm(ks[16], (DEPTH, D_MODEL), 0.05),
        "norm_mix_post": 1.0 + nrm(ks[17], (DEPTH, D_MODEL), 0.05),
        "norm_ffn_pre": 1.0 + nrm(ks[18], (DEPTH, D_MODEL), 0.05),
        "norm_ffn_post": 1.0 + nrm(ks[19], (DEPTH, D_MODEL), 0.05),
    }

def first_block(x, attn_w_qkv, attn_b_qkv, attn_sinks, attn_w_o, attn_b_o,
              sgu_w_in, sgu_ln_g, sgu_ln_b, sgu_w_s, sgu_b_s, sgu_w_out,
              ffn_w_in, ffn_conv_w, ffn_conv_b, ffn_w_out,
              norm_mix_pre, norm_mix_post, norm_ffn_pre, norm_ffn_post):
    for i in range(DEPTH):
        j = i // N_MIXERS
        h = rms_norm(x, norm_mix_pre[i])
        if i % N_MIXERS == 0:
            h = sliding_window_attention(h, attn_w_qkv[j], attn_b_qkv[j], attn_sinks[j],
                                         attn_w_o[j], attn_b_o[j])
        else:
            h = chunked_sgu(h, sgu_w_in[j], sgu_ln_g[j], sgu_ln_b[j], sgu_w_s[j],
                            sgu_b_s[j], sgu_w_out[j])
        x = x + rms_norm(h, norm_mix_post[i])
        h = conv_gated_ffn(rms_norm(x, norm_ffn_pre[i]), ffn_w_in[i], ffn_conv_w[i],
                           ffn_conv_b[i], ffn_w_out[i])
        x = x + rms_norm(h, norm_ffn_post[i])
    return x


DEPTH_2 = 1

D_SSM = D_MODEL
SSM_HEAD_DIM = 64
SSM_HEADS = D_SSM // SSM_HEAD_DIM
SSM_GROUPS = 2
SSM_STATE = 128
CONV_WIDTH_2 = 5
D_XBC = D_SSM + 2 * SSM_GROUPS * SSM_STATE

ATTN_HEAD_DIM = 64
ATTN_HEADS = D_MODEL // ATTN_HEAD_DIM
ATTN_KV_HEADS = 4
D_ATTN = ATTN_HEADS * ATTN_HEAD_DIM
D_KV = ATTN_KV_HEADS * ATTN_HEAD_DIM

D_MIX = D_SSM + D_ATTN
D_FF_2 = 4 * D_MODEL

IN_SIZES = (D_SSM, D_XBC, 2 * SSM_HEADS, D_ATTN, D_KV, D_KV)
D_IN = sum(IN_SIZES)
IN_OFFSETS = tuple(int(o) for o in np.cumsum(IN_SIZES)[:-1])


def rmsnorm(x, w):
    xf = x.astype(jnp.float32)
    y = xf * lax.rsqrt(jnp.mean(xf * xf, axis=-1, keepdims=True) + EPS)
    return (y * w.astype(jnp.float32)).astype(x.dtype)

def depthwise_conv_centred(u, w, b):
    c = u.shape[-1]
    out = lax.conv_general_dilated(
        u, w[:, None, :].astype(u.dtype), window_strides=(1,),
        padding=[(CONV_WIDTH_2 // 2, CONV_WIDTH_2 // 2)],
        dimension_numbers=("NWC", "WIO", "NWC"), feature_group_count=c)
    return out + b.astype(u.dtype)

def ssd_scan(X, dt, A, B, C):
    b, l, h, p = X.shape
    g, n = B.shape[2], B.shape[3]
    r = h // g
    c = l // CHUNK
    Xd = (X.astype(jnp.float32) * dt[..., None]).reshape(b, c, CHUNK, g, r, p)
    dA = (dt * A).reshape(b, c, CHUNK, g, r).transpose(0, 3, 4, 1, 2)
    Bc = B.astype(jnp.float32).reshape(b, c, CHUNK, g, n)
    Cc = C.astype(jnp.float32).reshape(b, c, CHUNK, g, n)
    A_cs = jnp.cumsum(dA, axis=-1)
    tri = jnp.tril(jnp.ones((CHUNK, CHUNK), dtype=bool))
    Lmat = jnp.exp(jnp.where(tri, A_cs[..., :, None] - A_cs[..., None, :], -jnp.inf))
    CB = jnp.einsum("bclgn,bcsgn->bgcls", Cc, Bc)
    Y_diag = jnp.einsum("bgrcls,bcsgrp->bclgrp", CB[:, :, None] * Lmat, Xd)
    decay_states = jnp.exp(A_cs[..., -1:] - A_cs)
    states = jnp.einsum("bcsgn,bgrcs,bcsgrp->bcgrpn", Bc, decay_states, Xd)
    chunk_decay = jnp.exp(A_cs[..., -1])

    def step(carry, inp):
        s_c, dec_c = inp
        return carry * dec_c[..., None, None] + s_c, carry

    init = jnp.zeros_like(states[:, 0])
    _, prev = lax.scan(step, init, (states.transpose(1, 0, 2, 3, 4, 5),
                                    chunk_decay.transpose(3, 0, 1, 2)))
    Y_off = jnp.einsum("bclgn,cbgrpn,bgrcl->bclgrp", Cc, prev, jnp.exp(A_cs))
    return (Y_diag + Y_off).reshape(b, l, h, p)

def ssd_mixer(z, xbc, dt_raw, conv_w, conv_b, dt_bias, a_log, d_skip, norm_w):
    b, l, _ = xbc.shape
    xbc = jax.nn.silu(depthwise_conv_centred(xbc, conv_w, conv_b))
    xs, Bm, Cm = jnp.split(xbc, (D_SSM, D_SSM + SSM_GROUPS * SSM_STATE), axis=-1)
    X = xs.reshape(b, l, SSM_HEADS, SSM_HEAD_DIM)
    Bm = Bm.reshape(b, l, SSM_GROUPS, SSM_STATE)
    Cm = Cm.reshape(b, l, SSM_GROUPS, SSM_STATE)
    dt = jax.nn.softplus(dt_raw.astype(jnp.float32).reshape(b, l, 2, SSM_HEADS)
                         + dt_bias.astype(jnp.float32))
    A = -jnp.exp(a_log.astype(jnp.float32))
    flip = lambda t: jnp.flip(t, axis=1)
    y_f = ssd_scan(X, dt[:, :, 0], A[0], Bm, Cm)
    y_b = flip(ssd_scan(flip(X), flip(dt[:, :, 1]), A[1], flip(Bm), flip(Cm)))
    y = y_f + y_b + X.astype(jnp.float32) * d_skip.astype(jnp.float32)[:, None]
    y = y.reshape(b, l, D_SSM)
    return rmsnorm(y * jax.nn.silu(z.astype(jnp.float32)), norm_w)

def window_attention(q, k, v, sink):
    b, l, _ = q.shape
    nb = l // BLOCK
    G, R, Dh = ATTN_KV_HEADS, ATTN_HEADS // ATTN_KV_HEADS, ATTN_HEAD_DIM
    qb = q.reshape(b, nb, BLOCK, G, R, Dh)
    pad = ((0, 0), (WINDOW, WINDOW), (0, 0))
    kp = jnp.pad(k, pad).reshape(b, nb + 2, BLOCK, G, Dh)
    vp = jnp.pad(v, pad).reshape(b, nb + 2, BLOCK, G, Dh)
    kb = jnp.concatenate([kp[:, :-2], kp[:, 1:-1], kp[:, 2:]], axis=2)
    vb = jnp.concatenate([vp[:, :-2], vp[:, 1:-1], vp[:, 2:]], axis=2)
    s = jnp.einsum("bnqgrd,bnkgd->bgrnqk", qb, kb).astype(jnp.float32) * (Dh ** -0.5)
    qi = jnp.arange(BLOCK)[:, None]
    kj = jnp.arange(3 * BLOCK)[None, :]
    dist = kj - BLOCK - qi
    key_abs = jnp.arange(nb)[:, None, None] * BLOCK + (kj - BLOCK)[None]
    valid = (jnp.abs(dist) <= WINDOW)[None] & (key_abs >= 0) & (key_abs < l)
    slopes = 2.0 ** (-8.0 * jnp.arange(1, ATTN_HEADS + 1, dtype=jnp.float32) / ATTN_HEADS)
    slopes = slopes.reshape(G, R)[:, :, None, None, None]
    s = jnp.where(valid, s - slopes * jnp.abs(dist).astype(jnp.float32), -jnp.inf)
    sk = sink.astype(jnp.float32).reshape(G, R)[:, :, None, None, None]
    m = jnp.maximum(jnp.max(s, axis=-1, keepdims=True), sk)
    p = jnp.exp(s - m)
    probs = p / (jnp.sum(p, axis=-1, keepdims=True) + jnp.exp(sk - m))
    o = jnp.einsum("bgrnqk,bnkgd->bnqgrd", probs.astype(v.dtype), vb)
    return o.reshape(b, l, D_ATTN)

def second_inputs(seed: int = 0) -> dict:
    key = jax.random.key(seed)
    ks = jax.random.split(key, 18)
    f32 = jnp.float32
    nrm = lambda k, shape, scale: jax.random.normal(k, shape, f32) * scale
    gain = lambda k, shape: 1.0 + 0.05 * jax.random.normal(k, shape, f32)
    dt0 = jnp.exp(jax.random.uniform(ks[5], (DEPTH_2, 2, SSM_HEADS), f32,
                                     jnp.log(1e-3), jnp.log(1e-1)))
    dt_bias = dt0 + jnp.log(-jnp.expm1(-dt0))
    a_log = jnp.log(jax.random.uniform(ks[6], (DEPTH_2, 2, SSM_HEADS), f32, 1.0, 16.0))
    return {
        "x": nrm(ks[0], (BATCH, SEQ, D_MODEL), 1.0),
        "norm_mix_pre": gain(ks[1], (DEPTH_2, D_MODEL)),
        "w_in": nrm(ks[2], (DEPTH_2, D_MODEL, D_IN), D_MODEL ** -0.5),
        "conv_w": nrm(ks[3], (DEPTH_2, CONV_WIDTH_2, D_XBC), CONV_WIDTH_2 ** -0.5),
        "conv_b": nrm(ks[4], (DEPTH_2, D_XBC), 0.01),
        "dt_bias": dt_bias,
        "a_log": a_log,
        "d_skip": gain(ks[7], (DEPTH_2, SSM_HEADS)),
        "ssm_norm": gain(ks[8], (DEPTH_2, D_SSM)),
        "attn_sink": nrm(ks[9], (DEPTH_2, ATTN_HEADS), 0.5),
        "w_out": nrm(ks[10], (DEPTH_2, D_MIX, D_MODEL), D_MIX ** -0.5),
        "norm_mix_post": gain(ks[11], (DEPTH_2, D_MODEL)),
        "norm_mlp_pre": gain(ks[12], (DEPTH_2, D_MODEL)),
        "w_up": nrm(ks[13], (DEPTH_2, D_MODEL, D_FF_2), D_MODEL ** -0.5),
        "w_down": nrm(ks[14], (DEPTH_2, D_FF_2, D_MODEL), D_FF_2 ** -0.5),
        "norm_mlp_post": gain(ks[15], (DEPTH_2, D_MODEL)),
    }

def second_block(x, norm_mix_pre, w_in, conv_w, conv_b, dt_bias, a_log, d_skip, ssm_norm,
              attn_sink, w_out, norm_mix_post, norm_mlp_pre, w_up, w_down, norm_mlp_post):
    for i in range(DEPTH_2):
        h = rmsnorm(x, norm_mix_pre[i])
        proj = h @ w_in[i]
        z, xbc, dt_raw, q, k, v = jnp.split(proj, IN_OFFSETS, axis=-1)
        y_ssm = ssd_mixer(z, xbc, dt_raw, conv_w[i], conv_b[i], dt_bias[i], a_log[i],
                          d_skip[i], ssm_norm[i])
        y_attn = window_attention(q, k, v, attn_sink[i])
        mix = jnp.concatenate([y_ssm.astype(x.dtype), y_attn.astype(x.dtype)], axis=-1) @ w_out[i]
        x = x + rmsnorm(mix, norm_mix_post[i])
        h = rmsnorm(x, norm_mlp_pre[i])
        f = jnp.square(jax.nn.relu(h @ w_up[i])) @ w_down[i]
        x = x + rmsnorm(f, norm_mlp_post[i])
    return x


def setup_inputs(seed=0):
    out = dict(first_inputs(seed))
    for name, value in second_inputs(seed + 1).items():
        if name != "x":
            out[name + "_2"] = value
    return out


def reference(
    x, attn_w_qkv, attn_b_qkv, attn_sinks, attn_w_o, attn_b_o, sgu_w_in, sgu_ln_g, sgu_ln_b,
    sgu_w_s, sgu_b_s, sgu_w_out, ffn_w_in, ffn_conv_w, ffn_conv_b, ffn_w_out, norm_mix_pre,
    norm_mix_post, norm_ffn_pre, norm_ffn_post, norm_mix_pre_2, w_in_2, conv_w_2, conv_b_2,
    dt_bias_2, a_log_2, d_skip_2, ssm_norm_2, attn_sink_2, w_out_2, norm_mix_post_2,
    norm_mlp_pre_2, w_up_2, w_down_2, norm_mlp_post_2,
):
    x = first_block(
        x, attn_w_qkv, attn_b_qkv, attn_sinks, attn_w_o, attn_b_o, sgu_w_in, sgu_ln_g, sgu_ln_b,
        sgu_w_s, sgu_b_s, sgu_w_out, ffn_w_in, ffn_conv_w, ffn_conv_b, ffn_w_out, norm_mix_pre,
        norm_mix_post, norm_ffn_pre, norm_ffn_post,
    )
    return second_block(
        x, norm_mix_pre_2, w_in_2, conv_w_2, conv_b_2, dt_bias_2, a_log_2, d_skip_2, ssm_norm_2,
        attn_sink_2, w_out_2, norm_mix_post_2, norm_mlp_pre_2, w_up_2, w_down_2,
        norm_mlp_post_2,
    )


_drawn_inputs = setup_inputs


def setup_inputs(seed=0):
    import zlib

    import numpy as np

    out = dict(_drawn_inputs(seed))
    spreads = {}
    factors = {'sgu_ln_g': 3.365,
     'sgu_ln_b': 8.0,
     'ffn_conv_b': 3.192,
     'conv_b_2': 8.0,
     'd_skip_2': 5.5,
     'ssm_norm_2': 2.898,
     'attn_sink_2': 8.0,
     'norm_mlp_post_2': 3.059}
    for name, (base, spread) in spreads.items():
        noise = np.random.default_rng([zlib.crc32(name.encode()), seed]).standard_normal(out[name].shape)
        drawn = base * np.exp(spread * noise) if base else spread * noise
        out[name] = __import__('jax').numpy.asarray(drawn.astype(out[name].dtype))
    for name, factor in factors.items():
        out[name] = (out[name] * factor).astype(out[name].dtype)
    return out
```

```python
import math
from collections import namedtuple

import concourse.bass as bass
import numpy as np
from concourse import mybir

F32 = mybir.dt.float32
F32R = mybir.dt.float32r
ACT = mybir.ActivationFunctionType
ALU = mybir.AluOpType
AX = mybir.AxisListType

P = 128
SEQ = 256
TT = SEQ // P
D = 1024
KT = D // P
EPS = 1e-6

HEADS, KV_HEADS, DH = 16, 4, 64
REP = HEADS // KV_HEADS
QT = HEADS * DH // P
KVT = KV_HEADS * DH // P
SLOPE = [2.0 ** (-8.0 * (h + 1) / HEADS) for h in range(HEADS)]

FT = 2816 // P
SG = 3072
SGT = SG // P
SGC = SG // 512
GROUPS = 8
XT = 1536 // P
MT = 4096 // P

RING = 6
UNIT = 1024

N_QKV1 = 0
N_WO1 = N_QKV1 + QT + KVT + 2
N_FFN0 = N_WO1 + KT
N_SGV = N_FFN0 + 3 * FT
N_SGU = N_SGV + 4 * SGC
N_SGO = N_SGU + SGT
N_FFN1 = N_SGO + SGT
N_XBC = N_FFN1 + 3 * FT
N_QKV2 = N_XBC + XT
N_Z = N_QKV2 + QT + KVT + 2
N_WO2 = N_Z + KT
N_MLP = N_WO2 + 2 * KT
UNITS = N_MLP + 2 * MT
assert UNITS % RING == 0

C_GAIN = 0
C_BQK = C_GAIN + 7 * KT
C_CONV = C_BQK + QT + KVT
C_XBC = C_CONV + 2 * FT * 4
C_LN = C_XBC + XT * 6
COLS = C_LN + SGT * 2

M_SINK1, M_SINK2, M_BV, M_DTB, M_ALOG, M_SKIP, M_BS, MISC = np.cumsum(
    [0, HEADS, HEADS, KV_HEADS * DH, 2 * HEADS, 2 * HEADS, HEADS, GROUPS * P]).tolist()

T_ID, T_LE, T_GT, T_GE, T_LT, T_ONE, T_D1, T_D2, TABLES = np.cumsum(
    [0, P, P, P, P, P, P, 3 * P, 4 * P]).tolist()
FAR = 1e30


def build(nc, w, x_in, cols_in, misc_in, tables_in, rows_in, ws_in, wdt_in, out):
    def sb(name, shape, dt=F32):
        return nc.alloc_sbuf_tensor(name, shape, dt)

    def sem(name):
        return nc.alloc_semaphore(name)

    def signals(prefix, names):
        return namedtuple(prefix, names)(*(sem(f"{prefix}_{name}") for name in names.split()))

    raw = sb("raw", [P, RING, UNIT])
    w_hi = sb("w_hi", [P, RING, UNIT], F32R)
    w_lo = sb("w_lo", [P, RING, UNIT], F32R)
    x = sb("x", [P, TT, D])
    a_hi = sb("a_hi", [P, 2 * KT, SEQ], F32R)
    a_lo = sb("a_lo", [P, 2 * KT, SEQ], F32R)
    cols = sb("cols", [P, COLS])
    misc = sb("misc", [P, MISC])
    tab = sb("tab", [P, TABLES])
    row = sb("row", [P, 2, D])
    wdt = sb("wdt", [P, KT, 32])
    wdt_hi = sb("wdt_hi", [P, KT, 32], F32R)
    wdt_lo = sb("wdt_lo", [P, KT, 32], F32R)
    st = sb("st", [P, 96])
    pad = sb("pad", [P, 2, SEQ + 4])
    arena = sb("arena", [P, 16640])
    ps = nc.alloc_psum_tensor("ps", [P, 8, 512], F32)

    def cut(at, *shape):
        n = math.prod(shape)
        assert at + n <= 16640
        v = arena[:, at:at + n]
        if len(shape) == 1:
            return v
        names = "abcd"[:len(shape)]
        return v.rearrange(f"p ({' '.join(names)}) -> p {' '.join(names)}",
                           **{k: s for k, s in zip(names[1:], shape[1:])})

    ident, le, gt, ge, lt, one = (tab[:, o:o + P] for o in (T_ID, T_LE, T_GT, T_GE, T_LT, T_ONE))
    ybuf = cut(0, TT, D)
    junk = cut(2048, D)

    raw_loaded = [sem(f"raw_loaded{s}") for s in range(RING)]
    hi_done = sem("hi_done")
    lo_done = sem("lo_done")
    unit_used = sem("unit_used")
    x_loaded, ident_loaded, cols_loaded = sem("x_loaded"), sem("ident_loaded"), sem("cols_loaded")
    const_loaded, ws_loaded = sem("const_loaded"), sem("ws_loaded")
    row_loaded = [sem("row_loaded0"), sem("row_loaded1")]
    out_done, pad_ready = sem("out_done"), sem("pad_ready")

    def hi_of(act, n, i=0):
        s = n % RING
        act.wait_ge(raw_loaded[s], 16 * (n // RING + 1) + 16 * i)
        if n >= RING:
            act.wait_ge(unit_used, n - RING + 1 + RING * i)
        act.activation(w_hi[:, s, :], raw[:, s, :], ACT.Copy).then_inc(hi_done, 1)

    def lo_of(dve, n, i=0):
        s = n % RING
        dve.wait_ge(hi_done, n + 1 + RING * i)
        dve.tensor_tensor(w_lo[:, s, :], raw[:, s, :], w_hi[:, s, :].bitcast(F32),
                          ALU.subtract).then_inc(lo_done, 1)

    act_at, dve_at = [0], [0]

    def hi_to(act, n):
        while act_at[0] <= min(n, UNITS - 1):
            hi_of(act, act_at[0])
            act_at[0] += 1

    def lo_to(dve, n):
        while dve_at[0] <= min(n, UNITS - 1):
            lo_of(dve, dve_at[0])
            dve_at[0] += 1

    def three(pe, o, l_hi, l_lo, r_hi, r_lo, first, last):
        pe.matmul(o, l_hi, r_hi, start=first, stop=False)
        pe.matmul(o, l_hi, r_lo, start=False, stop=False)
        return pe.matmul(o, l_lo, r_hi, start=False, stop=last)

    def features(pe, n, o, i=0, pre=None):
        s = n % RING
        pe.wait_ge(lo_done, n + 1 + RING * i)
        for k in range(KT):
            if pre is not None:
                pe.wait_ge(pre.lo, KT * pre.n + k + 1)
            c = slice(k * P, (k + 1) * P)
            mm = three(pe, o, w_hi[:, s, c], w_lo[:, s, c], a_hi[:, k, :], a_lo[:, k, :],
                       k == 0, k == KT - 1)
        mm.then_inc(unit_used, 1)

    def tokens(pe, n, o, k0, nk, width, i=0, pre=None):
        s = n % RING
        pe.wait_ge(lo_done, n + 1 + RING * i)
        for k in range(nk):
            if pre is not None:
                pe.wait_ge(pre.lo, KT * pre.n + k0 + k + 1)
            c = slice(k * width, (k + 1) * width)
            for tt in range(TT):
                t = slice(tt * P, (tt + 1) * P)
                mm = three(pe, o[tt], a_hi[:, k0 + k, t], a_lo[:, k0 + k, t],
                           w_hi[:, s, c], w_lo[:, s, c], k0 + k == 0, k0 + k == KT - 1)
        mm.then_inc(unit_used, 1)

    def accumulate(pe, n, slot, first, last, i=0):
        s = n % RING
        pe.wait_ge(lo_done, n + 1 + RING * i)
        for tt in range(TT):
            t = slice(tt * P, (tt + 1) * P)
            for a, b, f, z in ((a_hi, w_hi, first, False), (a_hi, w_lo, False, False),
                               (a_lo, w_hi, False, last)):
                for c in range(2):
                    mm = pe.matmul(ps[:, 2 * tt + c, :], a[:, slot, t],
                                   b[:, s, c * 512:(c + 1) * 512], start=f, stop=z)
        mm.then_inc(unit_used, 1)

    pre_sems = signals("pre", "sum mean root inv scaled turned hi lo")
    post_sems = signals("post", "sum mean root inv scaled turned hi lo")
    add_sems = signals("update", "biased term added")

    Norm = namedtuple("Norm", "n sum mean root inv scaled turned hi lo")
    Update = namedtuple("Update", "n post pre biased term added")

    def turn_pe(pe, q):
        for tt in range(TT):
            pe.wait_ge(q.scaled, TT * q.n + tt + 1)
            for k in range(KT):
                o = turned(k)[:, tt * P:(tt + 1) * P]
                mm = pe.transpose(o, ybuf[:, tt, k * P:(k + 1) * P], ident)
            mm.then_inc(q.turned, 1)

    def norm_act(act, q, view, done, c0):
        for tt in range(TT):
            act.wait_ge(*done(tt))
            if tt:
                act.wait_ge(q.sum, TT * q.n + tt)
            act.activation(junk[:, :], view(tt), ACT.Square,
                           accum_out=st[:, c0 + tt:c0 + tt + 1]).then_inc(q.sum, 1)
        act.wait_ge(q.mean, q.n + 1)
        act.activation(st[:, c0 + 4:c0 + 6], st[:, c0 + 2:c0 + 4], ACT.Sqrt).then_inc(q.root, 1)

    def norm_dve(dve, q, c0, width=D):
        dve.wait_ge(q.sum, TT * (q.n + 1))
        dve.tensor_scalar(st[:, c0 + 2:c0 + 4], st[:, c0:c0 + 2], 1.0 / width, EPS,
                          ALU.mult, ALU.add).then_inc(q.mean, 1)
        dve.wait_ge(q.root, q.n + 1)
        dve.reciprocal(st[:, c0 + 6:c0 + 8], st[:, c0 + 4:c0 + 6]).then_inc(q.inv, 1)
        dve.wait_ge(q.inv, q.n + 1)

    def scale_dve(dve, q, c0, src):
        for tt in range(TT):
            dve.tensor_scalar(ybuf[:, tt, :], src[:, tt, :], st[:, c0 + 6 + tt:c0 + 7 + tt], None,
                              ALU.mult).then_inc(q.scaled, 1)

    def turned(k):
        return ps[:, 4 + k % 4, (k // 4) * SEQ:(k // 4 + 1) * SEQ]

    def gain(g, k):
        return cols[:, C_GAIN + g * KT + k:C_GAIN + g * KT + k + 1]

    def halves_act(act, q, g):
        act.wait_ge(q.turned, TT * (q.n + 1))
        for k in range(KT):
            if k >= 4:
                act.wait_ge(q.lo, KT * q.n + k - 3)
            act.activation(a_hi[:, k, :], turned(k), ACT.Copy, scale=gain(g, k)).then_inc(q.hi, 1)

    def halves_dve(dve, q, g):
        dve.wait_ge(q.turned, TT * (q.n + 1))
        for k in range(KT):
            dve.wait_ge(q.hi, KT * q.n + k + 1)
            dve.scalar_tensor_tensor(a_lo[:, k, :], turned(k), gain(g, k),
                                     a_hi[:, k, :].bitcast(F32), ALU.mult,
                                     ALU.subtract).then_inc(q.lo, 1)

    def update(n, pre):
        return Update(n, Norm(n, *post_sems), pre, *add_sems)

    acc = [ps[:, 2 * tt:2 * tt + 2, :].rearrange("p a b -> p (a b)") for tt in range(TT)]

    def update_act(act, u, n_last, g, bias):
        hi_to(act, n_last + RING - 1)
        if bias:
            norm_act(act, u.post, lambda tt: ybuf[:, tt, :], lambda tt: (u.biased, tt + 1), 0)
        else:
            norm_act(act, u.post, lambda tt: acc[tt],
                     lambda tt: (u.term, TT * u.n + 1) if tt else (unit_used, n_last + 1), 0)
        if g is None:
            return
        norm_act(act, u.pre, lambda tt: x[:, tt, :], lambda tt: (u.added, TT * u.n + tt + 1), 8)
        halves_act(act, u.pre, g)

    def update_dve(dve, u, n_last, g, r, bias):
        lo_to(dve, n_last + RING - 1)
        dve.wait_ge(row_loaded[r % 2], 16 * (r // 2 + 1))
        dve.wait_ge(unit_used, n_last + 1)
        if bias is not None:
            dve.wait_ge(row_loaded[bias % 2], 16 * (bias // 2 + 1))
            for tt in range(TT):
                dve.tensor_tensor(ybuf[:, tt, :], acc[tt], row[:, bias % 2, :],
                                  ALU.add).then_inc(u.biased, 1)
            for tt in range(TT):
                dve.wait_ge(u.post.sum, TT * u.n + tt + 1)
                dve.tensor_tensor(ybuf[:, tt, :], ybuf[:, tt, :], row[:, r % 2, :],
                                  ALU.mult).then_inc(u.term, 1)
        else:
            for n, tt in enumerate((1, 0)):
                if n:
                    dve.wait_ge(u.post.sum, TT * u.n + 1)
                dve.tensor_tensor(ybuf[:, tt, :], acc[tt], row[:, r % 2, :], ALU.mult).then_inc(u.term, 1)
        norm_dve(dve, u.post, 0)
        dve.wait_ge(u.term, TT * (u.n + 1))
        for tt in range(TT):
            dve.scalar_tensor_tensor(x[:, tt, :], ybuf[:, tt, :], st[:, 6 + tt:7 + tt], x[:, tt, :],
                                     ALU.mult, ALU.add).then_inc(u.added, 1)
        dve.wait_ge(u.added, TT * (u.n + 1))
        if g is None:
            return
        norm_dve(dve, u.pre, 8)
        scale_dve(dve, u.pre, 8, x)
        halves_dve(dve, u.pre, g)

    F_CV, F_GL, F_PR = cut(3072, 2, SEQ), cut(3584, 2, SEQ), cut(4096, 2, SEQ)

    def ffn_sems(name):
        return signals(name, "copied conv gelu product hi lo")

    def f_g(n0, t):
        return n0 + 3 * t - 1 if t else n0

    def f_out(n0, t):
        return n0 + 3 * FT - 1 if t == FT - 1 else n0 + 4 + 3 * t

    def ffn_in_pe(pe, f, n0, t, i=0, first=False):
        b = t % 2
        if not first:
            pe.wait_ge(f.product, t - 1 + 2 * i)
        features(pe, f_g(n0, t), ps[:, 4 + b, 0:SEQ], i)
        features(pe, f_g(n0, t) + 1, ps[:, 6 + b, 0:SEQ], i)

    def f_banks(t, i):
        return (0, 1) if t == 0 and isinstance(i, int) else (4 + t % 2, 6 + t % 2)

    def ready(pe, q):
        pe.wait_ge(q.lo, KT * (q.n + 1))

    def ffn_pe(pe, f, n0, pre):
        for n in range(2):
            features(pe, n0 + n, ps[:, n, 0:SEQ], pre=pre)
        ffn_in_pe(pe, f, n0, 1, first=True)
        pe.wait_ge(f.lo, 1)
        accumulate(pe, f_out(n0, 0), KT, True, False)
        with pe.Fori(0, (FT - 2) // 2) as i:
            for t in (2, 3):
                ffn_in_pe(pe, f, n0, t, i)
                pe.wait_ge(f.lo, t + 2 * i)
                accumulate(pe, f_out(n0, t - 1), KT + (t - 1) % 2, False, False, i)
        pe.wait_ge(f.lo, FT)
        accumulate(pe, f_out(n0, FT - 1), KT + (FT - 1) % 2, False, True)

    def ffn_act_step(act, f, n0, t, i, split):
        b = t % 2
        act.wait_ge(unit_used, f_g(n0, t) + 1 + RING * i)
        if t >= 2:
            act.wait_ge(f.conv, 3 * t - 3 + 6 * i)
        act.activation(pad[:, b, 2:2 + SEQ], ps[:, f_banks(t, i)[0], 0:SEQ], ACT.Copy).then_inc(f.copied, 1)
        split(0)
        act.wait_ge(f.conv, 3 * t + 3 + 6 * i)
        if t >= 2:
            act.wait_ge(f.product, t - 1 + 2 * i)
        act.activation(F_GL[:, b, :], F_CV[:, b, :], ACT.Gelu_apprx_tanh).then_inc(f.gelu, 1)
        split(1)
        act.wait_ge(f.product, t + 1 + 2 * i)
        if t >= 2:
            act.wait_ge(unit_used, f_out(n0, t - 2) + 1 + RING * i)
        act.activation(a_hi[:, KT + b, :], F_PR[:, b, :], ACT.Copy).then_inc(f.hi, 1)
        split(2)

    def ffn_dve_step(dve, f, n0, layer, t, i, split):
        b = t % 2
        c = C_CONV + (layer * FT + t) * 4

        def col(k):
            return cols[:, bass.ds(c + k + 8 * i, 1)] if not isinstance(i, int) else cols[:, c + k:c + k + 1]

        dve.wait_ge(f.copied, t + 1 + 2 * i)
        if t >= 2:
            dve.wait_ge(f.gelu, t - 1 + 2 * i)
        dve.tensor_scalar(F_CV[:, b, :], pad[:, b, 0:SEQ], col(0), col(3), ALU.mult,
                          ALU.add).then_inc(f.conv, 1)
        for k in (1, 2):
            dve.wait_ge(f.conv, 3 * t + k + 6 * i)
            dve.scalar_tensor_tensor(F_CV[:, b, :], pad[:, b, k:k + SEQ], col(k), F_CV[:, b, :],
                                     ALU.mult, ALU.add).then_inc(f.conv, 1)
        split(0)
        split(1)
        dve.wait_ge(f.gelu, t + 1 + 2 * i)
        dve.wait_ge(unit_used, f_g(n0, t) + 2 + RING * i)
        dve.tensor_tensor(F_PR[:, b, :], F_GL[:, b, :], ps[:, f_banks(t, i)[1], 0:SEQ],
                          ALU.mult).then_inc(f.product, 1)
        split(2)
        dve.wait_ge(f.hi, t + 1 + 2 * i)
        dve.tensor_tensor(a_lo[:, KT + b, :], F_PR[:, b, :], a_hi[:, KT + b, :].bitcast(F32),
                          ALU.subtract).then_inc(f.lo, 1)

    def ffn_run(eng, step, half_of, half_to, at, n0):
        half_to(eng, n0 + 5)
        step(0, 0, lambda j: half_to(eng, n0 + 6 + min(j, 1)))
        step(1, 0, lambda j: half_to(eng, n0 + 8 + j))
        with eng.Fori(0, (FT - 2) // 2) as i:
            for t in (2, 3):
                step(t, i, lambda j, t=t: half_of(eng, f_g(n0, t) + 6 + j, i))
        at[0] = n0 + 8 + 3 * (FT - 1)

    def ffn_act(act, f, n0):
        ffn_run(act, lambda t, i, s: ffn_act_step(act, f, n0, t, i, s), hi_of, hi_to, act_at, n0)

    def ffn_dve(dve, f, n0, layer):
        ffn_run(dve, lambda t, i, s: ffn_dve_step(dve, f, n0, layer, t, i, s), lo_of, lo_to, dve_at, n0)

    A_Q, A_K, A_V = cut(3072, QT, SEQ), cut(5120, KVT, SEQ), cut(5632, TT, KV_HEADS * DH)
    QKT = QT + KVT

    def qk_bank(j):
        return 4 + j % 4 if j else 0

    def qkv_pe(pe, n0, qk_out, pre=None):
        for j in range(QKT):
            if j >= 4:
                pe.wait_ge(qk_out, j - 3)
            features(pe, n0 + j, ps[:, qk_bank(j), 0:SEQ], pre=pre if j == 0 else None)
        for h in range(2):
            tokens(pe, n0 + QKT + h, [ps[:, 2, 0:256], ps[:, 3, 0:256]], 4 * h, 4, 256)

    def qkv_dve(dve, n0, qk_out, v_out, biased):
        for j in range(QKT):
            lo_to(dve, n0 + j + 5)
            dve.wait_ge(unit_used, n0 + j + 1)
            dst = A_Q[:, j, :] if j < QT else A_K[:, j - QT, :]
            scale = DH ** -0.5 if j < QT else 1.0
            bias = cols[:, C_BQK + j:C_BQK + j + 1] if biased else 0.0
            dve.tensor_scalar(dst, ps[:, qk_bank(j), 0:SEQ], bias, scale, ALU.add,
                              ALU.mult).then_inc(qk_out, 1)
        dve.wait_ge(unit_used, n0 + QKT + 2)
        for tt in range(TT):
            if biased:
                dve.tensor_tensor(A_V[:, tt, :], ps[:, 2 + tt, 0:256], misc[:, M_BV:M_BV + 256],
                                  ALU.add).then_inc(v_out, 1)
            else:
                dve.tensor_copy(A_V[:, tt, :], ps[:, 2 + tt, 0:256]).then_inc(v_out, 1)
        lo_to(dve, n0 + QKT + 1 + RING)

    A_S, A_PT = cut(6144, 2, REP, 512), cut(10240, 2, 512)

    def attn_plan(first):
        seen = [[0], [0, 1]] if first else [[0, 1], [0, 1]]
        at, off = [], 0
        for keys in seen:
            at.append(off)
            off += P * len(keys)
        return seen, at, off

    def attn_sems(name):
        return signals(name, "qk v scores biased stat exp norm turned out hi lo den copied_even copied_odd")

    def attn_pe(pe, q, first, busy=None):
        seen, at, width = attn_plan(first)

        def scores(g):
            half = slice(64 * (g % 2), 64 * (g % 2) + 64)
            for r in range(REP):
                if g >= 1:
                    pe.wait_ge(q.biased, REP * (g - 1) + r + 1)
                for b in range(TT):
                    keys = seen[b]
                    mm = pe.matmul(ps[:, r, at[b]:at[b] + P * len(keys)],
                                   A_Q[half, REP * (g // 2) + r, b * P:(b + 1) * P],
                                   A_K[half, g // 2, keys[0] * P:(keys[-1] + 1) * P],
                                   start=True, stop=True)
                mm.then_inc(q.scores, 1)

        def turn(g, r):
            h = REP * g + r
            pe.wait_ge(q.norm, g + 1)
            if h >= 2:
                pe.wait_ge((q.copied_even, q.copied_odd)[r % 2], h // 2)
            for j in range(width // P):
                mm = pe.transpose(ps[:, 4 + r % 2, j * P:(j + 1) * P],
                                  A_S[:, g % 2, r, j * P:(j + 1) * P], ident)
            mm.then_inc(q.turned, 1)

        def values(g, r):
            h = REP * g + r
            half = slice(64 * (g % 2), 64 * (g % 2) + 64)
            pe.wait_ge((q.copied_even, q.copied_odd)[r % 2], h // 2 + 1)
            if g >= 1 and r == 0:
                pe.wait_ge(q.lo, g)
            for b in range(TT):
                for j, kb in enumerate(seen[b]):
                    c = at[b] + j * P
                    o = (r % 2) * SEQ + b * P
                    mm = pe.matmul(ps[half, 6 + r // 2, o:o + P],
                                   A_V[:, kb, g * DH:(g + 1) * DH], A_PT[:, r % 2, c:c + P],
                                   start=(j == 0), stop=(j == len(seen[b]) - 1))
            if r == REP - 1:
                mm.then_inc(q.out, 1)

        pe.wait_ge(q.qk, QKT)
        pe.wait_ge(q.v, TT)
        scores(0)
        for g in range(KV_HEADS):
            if g + 1 < KV_HEADS:
                scores(g + 1)
            turn(g, 0)
            for r in range(REP):
                if r + 1 < REP:
                    turn(g, r + 1)
                values(g, r)

    stq = sb("stq", [P, 7, 2 * REP])

    def stat(k):
        return stq[:, k, :]

    def attn_act(act, q, first):
        seen, at, width = attn_plan(first)
        for g in range(KV_HEADS):
            act.wait_ge(q.stat, 5 * g + 5)
            if g:
                act.wait_ge(q.norm, g)
            for b in range(TT):
                for r in range(REP):
                    s = A_S[:, g % 2, r, at[b]:at[b] + P * len(seen[b])]
                    k = b * REP + r
                    act.activation(s, s, ACT.Exp, bias=stat(1)[:, k:k + 1],
                                   accum_out=stat(4)[:, k:k + 1]).then_inc(q.exp, 1)
            act.activation(stat(3), stat(2), ACT.Exp).then_inc(q.exp, 1)
            for r in (1, 3):
                act.wait_ge(q.turned, REP * g + r + 1)
                act.activation(A_PT[:, 1, 0:width], ps[:, 5, 0:width], ACT.Copy).then_inc(q.copied_odd, 1)
            act.wait_ge(q.out, g + 1)
            half = slice(64 * (g % 2), 64 * (g % 2) + 64)
            t = KT + REP * (g // 2)
            act.activation(a_hi[half, t:t + REP, :],
                           ps[half, 6:8, :].rearrange("p a (b c) -> p (a b) c", b=2),
                           ACT.Copy).then_inc(q.hi, 1)

    def attn_dve(dve, q, first, m_sink):
        seen, at, width = attn_plan(first)
        dist = tab[:, T_D1:T_D1 + width] if first else tab[:, T_D2:T_D2 + width]

        def maxima(g):
            for r in range(REP):
                h = REP * g + r
                dve.wait_ge(q.scores, h + 1)
                if g >= 2:
                    dve.wait_ge(q.turned, REP * (g - 1))
                dve.scalar_tensor_tensor(A_S[:, g % 2, r, 0:width], dist, -SLOPE[h],
                                         ps[:, r, 0:width], ALU.mult, ALU.add).then_inc(q.biased, 1)
            dve.wait_ge(q.biased, REP * (g + 1))
            if g:
                dve.wait_ge(q.exp, 9 * g)
            for b in range(TT):
                dve.tensor_reduce(stat(0)[:, b * REP:(b + 1) * REP],
                                  A_S[:, g % 2, :, at[b]:at[b] + P * len(seen[b])],
                                  AX.X, ALU.max).then_inc(q.stat, 1)
            dve.wait_ge(q.stat, 5 * g + 2)
            sink = misc[:, m_sink + REP * g:m_sink + REP * (g + 1)]
            both = sink.rearrange("p (a r) -> p a r", a=1).to_broadcast([P, TT, REP])
            two = lambda k: stat(k).rearrange("p (b r) -> p b r", b=TT)
            dve.tensor_tensor(two(0), two(0), both, ALU.max).then_inc(q.stat, 1)
            dve.wait_ge(q.stat, 5 * g + 3)
            dve.tensor_scalar(stat(1), stat(0), -1.0, None, ALU.mult).then_inc(q.stat, 1)
            dve.tensor_tensor(two(2), both, two(0), ALU.subtract).then_inc(q.stat, 1)

        def normalise(g):
            dve.wait_ge(q.exp, 9 * (g + 1))
            dve.tensor_tensor(stat(5), stat(4), stat(3), ALU.add).then_inc(q.den, 1)
            dve.wait_ge(q.den, 2 * g + 1)
            dve.reciprocal(stat(6), stat(5)).then_inc(q.den, 1)
            dve.wait_ge(q.den, 2 * g + 2)
            for b in range(TT):
                s = A_S[:, g % 2, :, at[b]:at[b] + P * len(seen[b])]
                inv = stat(6)[:, b * REP:(b + 1) * REP].rearrange("p (r a) -> p r a", a=1)
                op = dve.tensor_tensor(s, s, inv.to_broadcast([P, REP, P * len(seen[b])]), ALU.mult)
            op.then_inc(q.norm, 1)

        maxima(0)
        for g in range(KV_HEADS):
            normalise(g)
            if g + 1 < KV_HEADS:
                maxima(g + 1)
            for r in (0, 2):
                dve.wait_ge(q.turned, REP * g + r + 1)
                dve.tensor_copy(A_PT[:, 0, 0:width], ps[:, 4, 0:width]).then_inc(q.copied_even, 1)
            dve.wait_ge(q.hi, g + 1)
            half = slice(64 * (g % 2), 64 * (g % 2) + 64)
            t = KT + REP * (g // 2)
            dve.tensor_tensor(a_lo[half, t:t + REP, :],
                              ps[half, 6:8, :].rearrange("p a (b c) -> p (a b) c", b=2),
                              a_hi[half, t:t + REP, :].bitcast(F32), ALU.subtract).then_inc(q.lo, 1)

    G_V, G_U = cut(0, TT, SG), cut(TT * SG, SGT, SEQ)
    G_WS, G_R = cut(12288, GROUPS, P), cut(13312, GROUPS, P)
    G_VN, G_AFF, G_PR = cut(14336, 3, TT, P), cut(15104, 3, P), cut(15488, 3, SEQ)
    lns = sb("lns", [P, 40])
    L_SUM, L_SQ, L_TOT, L_NEG, L_VSUM, L_VAR, L_ROOT, L_INV, L_SHIFT = 0, 12, 24, 26, 28, 30, 32, 34, 36
    g_sem = signals("sgu", "v u masked rows rows_out stat square root vn mixed affine gated product hi lo")
    VB = (2, 4, 6)

    def sgu_v_pe(pe, c, first=False, pre=None):
        if not first:
            pe.wait_ge(g_sem.v, 2 * (c - 2))
        b = VB[c % 3]
        for k in range(4):
            tokens(pe, N_SGV + 4 * c + k, [ps[:, b, :], ps[:, b + 1, :]], 2 * k, 2, 512, pre=pre)

    def sgu_spatial(pe, j, i=0):
        pe.wait_ge(g_sem.vn, 2 * j + 2 + 12 * i)
        if j >= 3:
            pe.wait_ge(g_sem.gated, j - 2 + 6 * i)
        for c in range(TT):
            g = j // 3
            rhs = G_WS[:, g, :] if isinstance(i, int) else \
                G_WS[:, bass.ds(g + 2 * i, 1), :].rearrange("p a t -> p (a t)")
            mm = pe.matmul(ps[:, 4 + j % 3, c * P:(c + 1) * P], G_VN[:, j % 3, c, :], rhs,
                           start=True, stop=True)
        mm.then_inc(g_sem.mixed, 1)

    def sgu_pe(pe, pre):
        pe.wait_ge(g_sem.masked, 1)
        for h in range(2):
            mm = pe.matmul(ps[:, h, :], one, G_WS[:, 4 * h:4 * h + 4, :], start=True, stop=True)
        mm.then_inc(g_sem.rows, 1)
        for c in range(3):
            sgu_v_pe(pe, c, first=True, pre=None if c else pre)
        for c in range(3, 6):
            sgu_v_pe(pe, c)
        pe.wait_ge(g_sem.v, 2 * SGC)
        for p in range(3):
            for k in range(2):
                features(pe, N_SGU + 2 * p + k, ps[:, 4 + p, k * SEQ:(k + 1) * SEQ])
        with pe.Fori(0, SGT // 6 - 1) as i:
            for p in range(3, 6):
                pe.wait_ge(g_sem.u, p - 2 + 3 * i)
                for k in range(2):
                    features(pe, N_SGU + 2 * p + k, ps[:, 4 + p % 3, k * SEQ:(k + 1) * SEQ], i)
        pe.wait_ge(g_sem.u, SGT // 2)

        def out_tile(j, i=0):
            pe.wait_ge(g_sem.lo, j + 1 + 6 * i)
            accumulate(pe, N_SGO + j, KT + j % 3, j == 0, j == SGT - 1, i)

        for j in range(3):
            sgu_spatial(pe, j)
        out_tile(0)
        with pe.Fori(0, 3) as i:
            for j in range(1, 7):
                sgu_spatial(pe, j + 2, i)
                out_tile(j, i)
        for j in range(19, SGT):
            if j + 2 < SGT:
                sgu_spatial(pe, j + 2)
            out_tile(j)

    def sgu_act(act):
        act.wait_ge(g_sem.rows, 1)
        act.activation(G_R.rearrange("p a b -> p (a b)"), ps[:, 0:2, :].rearrange("p a b -> p (a b)"),
                       ACT.Copy).then_inc(g_sem.rows_out, 1)
        hi_to(act, N_SGV + 5)
        for c in range(SGC):
            hi_to(act, N_SGV + 4 * c + 8)
            for tt in range(TT):
                act.wait_ge(unit_used, N_SGV + 4 * c + 4)
                act.activation(G_V[:, tt, c * 512:(c + 1) * 512], ps[:, VB[c % 3] + tt, :],
                               ACT.Gelu_apprx_tanh,
                               accum_out=lns[:, L_SUM + 6 * tt + c:L_SUM + 6 * tt + c + 1]).then_inc(g_sem.v, 1)
            hi_to(act, N_SGV + 4 * c + 9)

        def moments():
            act.wait_ge(g_sem.stat, 2)
            for tt in range(TT):
                for c in range(SGC):
                    if tt or c:
                        act.wait_ge(g_sem.square, SGC * tt + c)
                    act.activation(G_PR[:, 0:2, :].rearrange("p a b -> p (a b)"), G_V[:, tt, c * 512:(c + 1) * 512],
                                   ACT.Square, bias=lns[:, L_NEG + tt:L_NEG + tt + 1],
                                   accum_out=lns[:, L_SQ + 6 * tt + c:L_SQ + 6 * tt + c + 1]).then_inc(g_sem.square, 1)
            act.wait_ge(g_sem.stat, 4)
            act.activation(lns[:, L_ROOT:L_ROOT + 2], lns[:, L_VAR:L_VAR + 2], ACT.Sqrt).then_inc(g_sem.root, 1)

        def pair(p, i, split):
            split(0)
            act.wait_ge(unit_used, N_SGU + 2 * p + 2 + 6 * i)
            dst = G_U[:, 2 * p:2 * p + 2, :] if isinstance(i, int) else G_U[:, bass.ds(2 * p + 6 * i, 2), :]
            act.activation(dst.rearrange("p a b -> p (a b)"), ps[:, 4 + p % 3, :],
                           ACT.Gelu_apprx_tanh).then_inc(g_sem.u, 1)
            split(1)

        for p in range(3):
            pair(p, 0, lambda j, p=p: hi_to(act, N_SGU + 2 * p + 6 + j))
        moments()
        with act.Fori(0, SGT // 6 - 1) as i:
            for p in range(3, 6):
                pair(p, i, lambda j, p=p: hi_of(act, N_SGU + 2 * p + 6 + j, i))
        act_at[0] = N_SGO + 6

        def vn(j, i=0):
            if j >= 3:
                act.wait_ge(g_sem.mixed, j - 2 + 6 * i)
            for tt in range(TT):
                src = G_V[:, tt, j * P:(j + 1) * P] if isinstance(i, int) else \
                    G_V[:, tt, bass.ds(j * P + 6 * P * i, P)]
                act.activation(G_VN[:, j % 3, tt, :], src, ACT.Identity,
                               bias=lns[:, L_SHIFT + tt:L_SHIFT + tt + 1],
                               scale=lns[:, L_INV + tt:L_INV + tt + 1]).then_inc(g_sem.vn, 1)

        def high(j, i=0):
            act.wait_ge(g_sem.product, j + 1 + 6 * i)
            if j >= 3:
                act.wait_ge(unit_used, N_SGO + j - 2 + 6 * i)
            act.activation(a_hi[:, KT + j % 3, :], G_PR[:, j % 3, :], ACT.Copy).then_inc(g_sem.hi, 1)

        act.wait_ge(g_sem.stat, 6)
        for j in range(4):
            if j == 3:
                high(0)
            vn(j)
        high(1)
        with act.Fori(0, 3) as i:
            for j in range(1, 7):
                vn(j + 3, i)
                high(j + 1, i)
                hi_of(act, N_SGO + j + 5, i)
        act_at[0] = N_SGO + 24
        for j in range(19, SGT):
            if j + 3 < SGT:
                vn(j + 3)
            if j + 1 < SGT:
                high(j + 1)
            hi_to(act, N_SGO + j + 5)

    def sgu_dve(dve):
        lo_to(dve, N_SGV + 4 * SGC - 1 + 6)
        dve.wait_ge(g_sem.v, 2 * SGC)
        dve.tensor_reduce(lns[:, L_TOT:L_TOT + 2], lns[:, L_SUM:L_SUM + 12].rearrange("p (a b) -> p a b", a=2),
                          AX.X, ALU.add).then_inc(g_sem.stat, 1)
        dve.wait_ge(g_sem.stat, 1)
        dve.tensor_scalar(lns[:, L_NEG:L_NEG + 2], lns[:, L_TOT:L_TOT + 2], -1.0 / SG, None,
                          ALU.mult).then_inc(g_sem.stat, 1)
        lo_to(dve, N_SGU + 11)
        dve.wait_ge(g_sem.square, 12)
        dve.tensor_reduce(lns[:, L_VSUM:L_VSUM + 2], lns[:, L_SQ:L_SQ + 12].rearrange("p (a b) -> p a b", a=2),
                          AX.X, ALU.add).then_inc(g_sem.stat, 1)
        dve.wait_ge(g_sem.stat, 3)
        dve.tensor_scalar(lns[:, L_VAR:L_VAR + 2], lns[:, L_VSUM:L_VSUM + 2], 1.0 / SG, EPS,
                          ALU.mult, ALU.add).then_inc(g_sem.stat, 1)
        dve.wait_ge(g_sem.root, 1)
        dve.reciprocal(lns[:, L_INV:L_INV + 2], lns[:, L_ROOT:L_ROOT + 2]).then_inc(g_sem.stat, 1)
        dve.wait_ge(g_sem.stat, 5)
        dve.tensor_tensor(lns[:, L_SHIFT:L_SHIFT + 2], lns[:, L_INV:L_INV + 2], lns[:, L_NEG:L_NEG + 2],
                          ALU.mult).then_inc(g_sem.stat, 1)
        with dve.Fori(0, SGT // 6 - 1) as i:
            for n in range(12, 18):
                lo_of(dve, N_SGU + n, i)
        dve_at[0] = N_SGO + 6

        def gate(j, i=0):
            b = j % 3
            c = C_LN + 2 * j
            g = cols[:, c:c + 1] if isinstance(i, int) else cols[:, bass.ds(c + 12 * i, 1)]
            u = G_U[:, j, :] if isinstance(i, int) else \
                G_U[:, bass.ds(j + 6 * i, 1), :].rearrange("p a t -> p (a t)")
            dve.wait_ge(g_sem.mixed, j + 1 + 6 * i)
            dve.wait_ge(g_sem.affine, 2 * j + 2 + 12 * i)
            if j >= 3:
                dve.wait_ge(g_sem.lo, j - 2 + 6 * i)
            dve.scalar_tensor_tensor(G_PR[:, b, :].rearrange("p (c t) -> p c t", c=TT),
                                     ps[:, 4 + b, 0:SEQ].rearrange("p (c t) -> p c t", c=TT), g,
                                     G_AFF[:, b:b + 1, :].to_broadcast([P, TT, P]), ALU.mult,
                                     ALU.add).then_inc(g_sem.gated, 1)
            dve.wait_ge(g_sem.gated, j + 1 + 6 * i)
            dve.tensor_tensor(G_PR[:, b, :], G_PR[:, b, :], u, ALU.mult).then_inc(g_sem.product, 1)

        def low(j, i=0):
            dve.wait_ge(g_sem.hi, j + 1 + 6 * i)
            dve.tensor_tensor(a_lo[:, KT + j % 3, :], G_PR[:, j % 3, :],
                              a_hi[:, KT + j % 3, :].bitcast(F32), ALU.subtract).then_inc(g_sem.lo, 1)

        gate(0)
        gate(1)
        low(0)
        gate(2)
        low(1)
        with dve.Fori(0, 3) as i:
            for j in range(1, 7):
                gate(j + 2, i)
                lo_of(dve, N_SGO + j + 5, i)
                low(j + 1, i)
        dve_at[0] = N_SGO + 24
        for j in range(19, SGT):
            if j + 2 < SGT:
                gate(j + 2)
            lo_to(dve, N_SGO + j + 5)
            if j + 1 < SGT:
                low(j + 1)

    def sgu_pool(pool):
        def affine(j):
            b, c, g = j % 3, C_LN + 2 * j + 1, j // 3
            if j >= 3:
                pool.wait_ge(g_sem.gated, j - 2)
            pool.tensor_tensor(G_AFF[:, b, :], G_R[:, g, :], cols[:, c:c + 1].to_broadcast([P, P]),
                               ALU.mult).then_inc(g_sem.affine, 1)
            pool.wait_ge(g_sem.affine, 2 * j + 1)
            pool.tensor_tensor(G_AFF[:, b, :], G_AFF[:, b, :], misc[:, M_BS + g * P:M_BS + (g + 1) * P],
                               ALU.add).then_inc(g_sem.affine, 1)

        pool.wait_ge(g_sem.rows_out, 1)
        for j in range(SGT):
            affine(j)

    S_X, S_B, S_F = cut(6144, TT, D), cut(8192, TT, 256), cut(8704, 4, SEQ)
    S_XD, S_XDD, S_ST = cut(9728, 2, 512), cut(10752, 512), cut(11264, 2, 512)
    S_E, S_LA, S_CB, S_T = cut(12288, 4, 512), cut(14336, 2, 512), cut(15360, 2, 2, P), cut(15872, 512)
    S_CV, S_SL = cut(12288, 2, SEQ), cut(12800, 2, SEQ)
    S_Z = cut(6144, TT, D)
    x_sem = signals("xbc", "copied conv silu turned moved")

    def xbc_dst(j):
        return S_SL[:, j % 2, :] if j < 8 else S_F[:, j - 8, :]

    def x_bank(j):
        return 4 + j % 2 if j else 0

    def xbc_pe(pe, pre):
        def turn(j):
            pe.wait_ge(x_sem.silu, j + 1)
            if j >= 2:
                pe.wait_ge(x_sem.moved, j - 1)
            for tt in range(TT):
                mm = pe.transpose(ps[:, 6 + j % 2, tt * P:(tt + 1) * P],
                                  xbc_dst(j)[:, tt * P:(tt + 1) * P], ident)
            mm.then_inc(x_sem.turned, 1)

        for j in range(XT):
            if j >= 2:
                pe.wait_ge(x_sem.copied, j - 1)
            features(pe, N_XBC + j, ps[:, x_bank(j), 0:SEQ], pre=None if j else pre)
            if j >= 2:
                turn(j - 2)
        pe.wait_ge(x_sem.copied, XT)

    def xbc_act(act):
        def move(j):
            act.wait_ge(x_sem.turned, j + 1)
            dst = S_X[:, :, j * P:(j + 1) * P] if j < 8 else S_B[:, :, (j - 8) * P:(j - 7) * P]
            act.activation(dst, ps[:, 6 + j % 2, 0:SEQ].rearrange("p (a b) -> p a b", a=TT),
                           ACT.Copy).then_inc(x_sem.moved, 1)

        for j in range(XT):
            hi_to(act, N_XBC + j + 5)
            act.wait_ge(unit_used, N_XBC + j + 1)
            if j >= 2:
                act.wait_ge(x_sem.conv, 5 * (j - 1))
            act.activation(pad[:, j % 2, 2:2 + SEQ], ps[:, x_bank(j), 0:SEQ], ACT.Copy).then_inc(x_sem.copied, 1)
            if j >= 3:
                move(j - 3)
            act.wait_ge(x_sem.conv, 5 * j + 5)
            if 2 <= j < 8:
                act.wait_ge(x_sem.turned, j - 1)
            act.activation(xbc_dst(j), S_CV[:, j % 2, :], ACT.Silu).then_inc(x_sem.silu, 1)
        move(XT - 3)

    def xbc_dve(dve):
        for j in range(XT):
            lo_to(dve, N_XBC + j + 5)
            c = C_XBC + 6 * j
            b = j % 2
            dve.wait_ge(x_sem.copied, j + 1)
            if j >= 2:
                dve.wait_ge(x_sem.silu, j - 1)
            dve.tensor_scalar(S_CV[:, b, :], pad[:, b, 0:SEQ], cols[:, c:c + 1], cols[:, c + 5:c + 6],
                              ALU.mult, ALU.add).then_inc(x_sem.conv, 1)
            for k in range(1, 5):
                dve.wait_ge(x_sem.conv, 5 * j + k)
                dve.scalar_tensor_tensor(S_CV[:, b, :], pad[:, b, k:k + SEQ], cols[:, c + k:c + k + 1],
                                         S_CV[:, b, :], ALU.mult, ALU.add).then_inc(x_sem.conv, 1)

    dts = sb("dts", [P, 12, 64])
    ex = sb("ex", [P, 4, HEADS])
    ea = sb("ea", [P, 32])
    d_sem = signals("dt", "w_loaded w_hi w_lo product step exp ln a sums decay")
    V_A, V_NEG, V_E, V_U, V_L, V_D, V_EQ, V_D2, V_RD, V_T, V_DT, V_DA = range(12)

    def dt_pe(pe):
        pe.wait_ge(d_sem.w_lo, 1)
        for tt in range(TT):
            t = slice(tt * P, (tt + 1) * P)
            for k in range(KT):
                mm = three(pe, ps[:, 1, 32 * tt:32 * tt + 32], a_hi[:, k, t], a_lo[:, k, t],
                           wdt_hi[:, k, :], wdt_lo[:, k, :], k == 0, k == KT - 1)
        mm.then_inc(d_sem.product, 1)

    def dt_sums_pe(pe):
        pe.wait_ge(d_sem.step, 12)
        da = dts[:, V_DA, :].rearrange("p (a b) -> p a b", a=TT)
        for n, (m, c, d) in enumerate(((gt, 0, 0), (lt, 1, 1), (ge, 0, 1), (le, 1, 0))):
            mm = pe.matmul(ps[:, 1, 128 + 16 * n:144 + 16 * n], m, da[:, c, 16 * d:16 * d + 16],
                           start=True, stop=True)
        mm.then_inc(d_sem.sums, 1)

    def dt_act(act):
        act.wait_ge(d_sem.step, 2)
        act.activation(dts[:, V_E, :], dts[:, V_NEG, :], ACT.Exp).then_inc(d_sem.exp, 1)
        act.activation(ea[:, :], misc[:, M_ALOG:M_ALOG + 32], ACT.Exp).then_inc(d_sem.exp, 1)
        act.wait_ge(d_sem.step, 3)
        act.activation(dts[:, V_L, :], dts[:, V_U, :], ACT.Ln).then_inc(d_sem.ln, 1)

    def decay_act(act):
        act.wait_ge(d_sem.sums, 1)
        act.activation(ex[:, :, :].rearrange("p a b -> p (a b)"), ps[:, 1, 128:192], ACT.Exp).then_inc(d_sem.decay, 1)

    def dt_dve(dve):
        v = lambda k: dts[:, k, :]
        two = lambda k: v(k).rearrange("p (a b) -> p a b", a=TT)
        row32 = lambda t, o: t[:, o:o + 32].rearrange("p (a b) -> p a b", a=1).to_broadcast([P, TT, 32])
        step = [0]

        def then(ins):
            ins.then_inc(d_sem.step, 1)
            step[0] += 1
            dve.wait_ge(d_sem.step, step[0])

        dve.wait_ge(d_sem.product, 1)
        then(dve.tensor_tensor(two(V_A), ps[:, 1, 0:64].rearrange("p (a b) -> p a b", a=TT), row32(misc, M_DTB), ALU.add))
        then(dve.scalar_tensor_tensor(v(V_NEG), v(V_A), -1.0, v(V_A), ALU.mult, ALU.min))
        dve.wait_ge(d_sem.exp, 2)
        then(dve.tensor_scalar(v(V_U), v(V_E), 1.0, None, ALU.add))
        then(dve.tensor_scalar(v(V_D), v(V_U), 1.0, None, ALU.subtract))
        then(dve.tensor_scalar(v(V_EQ), v(V_U), 1.0, None, ALU.is_equal))
        then(dve.tensor_tensor(v(V_D2), v(V_D), v(V_EQ), ALU.add))
        then(dve.reciprocal(v(V_RD), v(V_D2)))
        then(dve.tensor_tensor(v(V_T), v(V_E), v(V_RD), ALU.mult))
        dve.wait_ge(d_sem.ln, 1)
        then(dve.tensor_tensor(v(V_D), v(V_L), v(V_EQ), ALU.add))
        then(dve.tensor_tensor(v(V_T), v(V_T), v(V_D), ALU.mult))
        then(dve.scalar_tensor_tensor(v(V_DT), v(V_A), 0.0, v(V_T), ALU.max, ALU.add))
        then(dve.scalar_tensor_tensor(two(V_DA), two(V_DT), -1.0, row32(ea, 0), ALU.mult, ALU.mult))

    s_sem = signals("ssd", "la diff exp m cb cb_out xd y xdd state state_out off t comb")

    def heads_bc(v, n, width):
        return v.rearrange("p (h a) -> p h a", a=1).to_broadcast([P, n, width])

    def ssd_pool(pool):
        pool.wait_ge(d_sem.step, 12)
        for b in range(16):
            k, q, d = b // 4, b // 2 % 2, b % 2
            g, c = k // 2, k % 2
            if b >= 2:
                pool.wait_ge(s_sem.diff, b - 1)
            o = 32 * c + 16 * d + 8 * g + 4 * q
            mask = (gt, lt)[d].rearrange("p (a b) -> p a b", a=1).to_broadcast([P, 4, P])
            pool.tensor_tensor(S_LA[:, b % 2, :].rearrange("p (h t) -> p h t", h=4), mask,
                               heads_bc(dts[:, V_DA, o:o + 4], 4, P), ALU.mult).then_inc(s_sem.la, 1)

    def ssd_pe(pe):
        def diff(b):
            pe.wait_ge(s_sem.la, b + 1)
            if b >= 2:
                pe.wait_ge(s_sem.exp, b - 1)
            for h in range(4):
                mm = pe.matmul(ps[:, 4 + b % 2, h * P:(h + 1) * P], S_LA[:, b % 2, h * P:(h + 1) * P],
                               (le, ge)[b % 2], start=True, stop=True)
            mm.then_inc(s_sem.diff, 1)

        def products(k):
            g, c = k // 2, k % 2
            t = slice(c * P, (c + 1) * P)
            if k >= 1:
                pe.wait_ge(s_sem.cb_out, 2 * k)
            pe.matmul(ps[:, 6, 0:P], S_F[:, g, t], S_F[:, 2 + g, t], start=True,
                      stop=True).then_inc(s_sem.cb, 1)

        def diagonal(j):
            k, q = j // 2, j % 2
            g, c = k // 2, k % 2
            pe.wait_ge(s_sem.m, 2 * j + 2)
            pe.wait_ge(s_sem.xd, 2 * k + 2)
            if g and q == 0:
                pe.wait_ge(s_sem.comb, 2)
            for h in range(4):
                o = (4 * q + h) * DH
                for d in range(2):
                    mm = pe.matmul(ps[:, c, o:o + DH], S_E[:, (2 * j + d) % 4, h * P:(h + 1) * P],
                                   S_XD[:, d, o:o + DH], start=(d == 0), stop=(d == 1))
            mm.then_inc(s_sem.y, 1)

        def state(k):
            g, c = k // 2, k % 2
            pe.wait_ge(s_sem.xdd, k + 1)
            if k >= 1:
                pe.wait_ge(s_sem.state_out, k)
            pe.matmul(ps[:, 7, :], S_B[:, c, g * P:(g + 1) * P], S_XDD, start=True,
                      stop=True).then_inc(s_sem.state, 1)

        def off(k):
            g, c = k // 2, k % 2
            pe.wait_ge(s_sem.state_out, k + 1)
            if g:
                pe.wait_ge(s_sem.comb, 2)
            pe.matmul(ps[:, 2 + (1 - c), :], S_F[:, 2 + g, (1 - c) * P:(2 - c) * P], S_ST[:, c, :],
                      start=True, stop=True).then_inc(s_sem.off, 1)

        pe.wait_ge(d_sem.decay, 1)
        for k in range(4):
            products(k)
            diff(4 * k)
            diff(4 * k + 1)
            state(k)
            diff(4 * k + 2)
            diff(4 * k + 3)
            diagonal(2 * k)
            off(k)
            diagonal(2 * k + 1)

    def ssd_act(act):
        for k in range(4):
            for b in range(4 * k, 4 * k + 4):
                act.wait_ge(s_sem.diff, b + 1)
                if b >= 4:
                    act.wait_ge(s_sem.y, b // 2 - 1)
                act.activation(S_E[:, b % 4, :], ps[:, 4 + b % 2, :], ACT.Exp).then_inc(s_sem.exp, 1)
                if b % 4 == 1:
                    act.wait_ge(s_sem.state, k + 1)
                    if k >= 2:
                        act.wait_ge(s_sem.off, k - 1)
                    act.activation(S_ST[:, k % 2, :], ps[:, 7, :], ACT.Copy).then_inc(s_sem.state_out, 1)

    def ssd_dve(dve):
        eight = lambda v: v.rearrange("p (h e) -> p h e", h=8)
        dve.wait_ge(d_sem.decay, 1)
        for k in range(4):
            g, c = k // 2, k % 2
            if k:
                dve.wait_ge(s_sem.y, 2 * k)
            for d in range(2):
                o = 32 * c + 16 * d + 8 * g
                dve.tensor_tensor(eight(S_XD[:, d, :]), eight(S_X[:, c, g * 512:(g + 1) * 512]),
                                  heads_bc(dts[:, V_DT, o:o + 8], 8, DH), ALU.mult).then_inc(s_sem.xd, 1)
            dve.wait_ge(s_sem.xd, 2 * k + 2)
            if k:
                dve.wait_ge(s_sem.state, k)
            dve.tensor_tensor(eight(S_XDD), eight(S_XD[:, c, :]), heads_bc(ex[:, c, 8 * g:8 * g + 8], 8, DH),
                              ALU.mult).then_inc(s_sem.xdd, 1)
            dve.wait_ge(s_sem.cb, k + 1)
            for d in range(2):
                dve.tensor_tensor(S_CB[:, k % 2, d, :], ps[:, 6, 0:P], (le, ge)[d], ALU.mult).then_inc(s_sem.cb_out, 1)
            dve.wait_ge(s_sem.cb_out, 2 * k + 2)
            for b in range(4 * k, 4 * k + 4):
                dve.wait_ge(s_sem.exp, b + 1)
                e = S_E[:, b % 4, :].rearrange("p (h t) -> p h t", h=4)
                dve.tensor_tensor(e, e, S_CB[:, k % 2, b % 2:b % 2 + 1, :].to_broadcast([P, 4, P]),
                                  ALU.mult).then_inc(s_sem.m, 1)
            if c == 0:
                continue
            dve.wait_ge(s_sem.off, k + 1)
            for cc in range(2):
                n = 2 * g + cc
                y = ybuf[:, cc, g * 512:(g + 1) * 512]
                dve.wait_ge(s_sem.y, 2 * n + 2)
                if n:
                    dve.wait_ge(s_sem.comb, n)
                dve.tensor_tensor(eight(S_T), eight(ps[:, 2 + cc, :]), heads_bc(ex[:, 2 + cc, 8 * g:8 * g + 8], 8, DH),
                                  ALU.mult).then_inc(s_sem.t, 1)
                dve.tensor_tensor(eight(y), eight(S_X[:, cc, g * 512:(g + 1) * 512]),
                                  heads_bc(misc[:, M_SKIP + 8 * g:M_SKIP + 8 * g + 8], 8, DH), ALU.mult).then_inc(s_sem.t, 1)
                dve.wait_ge(s_sem.t, 3 * n + 1)
                dve.tensor_tensor(S_T, S_T, ps[:, cc, :], ALU.add).then_inc(s_sem.t, 1)
                dve.wait_ge(s_sem.t, 3 * n + 3)
                dve.tensor_tensor(y, y, S_T, ALU.add).then_inc(s_sem.comb, 1)

    z_sem = signals("z", "silu gated")

    def z_pe(pe):
        pe.wait_ge(s_sem.exp, 16)
        pe.wait_ge(s_sem.state_out, 4)
        pe.wait_ge(s_sem.cb_out, 8)
        for c in range(2):
            for k in range(4):
                tokens(pe, N_Z + 4 * c + k, [ps[:, 4 + 2 * c, :], ps[:, 5 + 2 * c, :]], 2 * k, 2, 512)

    def z_act(act):
        act.wait_ge(s_sem.comb, 4)
        for c in range(2):
            hi_to(act, N_Z + 4 * c + 8)
            for tt in range(TT):
                act.wait_ge(unit_used, N_Z + 4 * c + 4)
                act.activation(S_Z[:, tt, c * 512:(c + 1) * 512], ps[:, 4 + 2 * c + tt, :],
                               ACT.Silu).then_inc(z_sem.silu, 1)
        hi_to(act, N_Z + 7 + RING)

    def z_dve(dve):
        lo_to(dve, N_Z + 7 + RING)
        dve.wait_ge(s_sem.comb, 4)
        dve.wait_ge(z_sem.silu, 4)
        for tt in range(TT):
            dve.tensor_tensor(ybuf[:, tt, :], ybuf[:, tt, :], S_Z[:, tt, :], ALU.mult).then_inc(z_sem.gated, 1)

    M_PR, M_RL = cut(3072, 3, SEQ), cut(3840, 3, SEQ)
    m_sem = signals("mlp", "relu square hi lo")

    def m_up(t):
        return N_MLP + 2 * t - 1 if t else N_MLP

    def m_down(t):
        return N_MLP + 2 * MT - 1 if t == MT - 1 else N_MLP + 2 + 2 * t

    def mlp_in_pe(pe, t, i=0):
        if t >= 3:
            pe.wait_ge(m_sem.relu, t - 2 + 3 * i)
        features(pe, m_up(t), ps[:, 4 + t % 3, 0:SEQ], i)

    def mlp_pe(pe, pre):
        features(pe, m_up(0), ps[:, 0, 0:SEQ], pre=pre)
        for t in (1, 2, 3, 4):
            mlp_in_pe(pe, t)
            pe.wait_ge(m_sem.lo, t)
            accumulate(pe, m_down(t - 1), KT + (t - 1) % 3, t == 1, False)
        with pe.Fori(0, (MT - 5) // 3) as i:
            for t in (5, 6, 7):
                mlp_in_pe(pe, t, i)
                pe.wait_ge(m_sem.lo, t + 3 * i)
                accumulate(pe, m_down(t - 1), KT + (t - 1) % 3, False, False, i)
        pe.wait_ge(m_sem.lo, MT)
        accumulate(pe, m_down(MT - 1), KT + (MT - 1) % 3, False, True)

    def mlp_act(act):
        def step(t, i, split):
            act.wait_ge(unit_used, m_up(t) + 1 + RING * i)
            if t >= 3:
                act.wait_ge(m_sem.square, t - 2 + 3 * i)
            act.activation(M_RL[:, t % 3, :], ps[:, 4 + t % 3 if t else 0, 0:SEQ], ACT.Relu).then_inc(m_sem.relu, 1)
            split(0)
            act.wait_ge(m_sem.square, t + 1 + 3 * i)
            if t >= 3:
                act.wait_ge(unit_used, m_down(t - 3) + 1 + RING * i)
            act.activation(a_hi[:, KT + t % 3, :], M_PR[:, t % 3, :], ACT.Copy).then_inc(m_sem.hi, 1)
            split(1)
        mlp_steps(act, step, hi_of, hi_to, act_at)

    def mlp_dve(dve):
        def step(t, i, split):
            dve.wait_ge(m_sem.relu, t + 1 + 3 * i)
            dve.tensor_tensor(M_PR[:, t % 3, :], M_RL[:, t % 3, :], M_RL[:, t % 3, :],
                              ALU.mult).then_inc(m_sem.square, 1)
            split(0)
            dve.wait_ge(m_sem.hi, t + 1 + 3 * i)
            dve.tensor_tensor(a_lo[:, KT + t % 3, :], M_PR[:, t % 3, :], a_hi[:, KT + t % 3, :].bitcast(F32),
                              ALU.subtract).then_inc(m_sem.lo, 1)
            split(1)
        mlp_steps(dve, step, lo_of, lo_to, dve_at)

    def mlp_steps(eng, step, half_of, half_to, at):
        half_to(eng, N_MLP + 5)
        step(0, 0, lambda j: half_to(eng, N_MLP + 6) if j == 0 else None)
        for t in range(1, 5):
            step(t, 0, lambda j, t=t: half_to(eng, m_up(t) + 6 + j))
        with eng.Fori(0, 8) as i:
            for t in (5, 6, 7):
                step(t, i, lambda j, t=t: half_of(eng, m_up(t) + 6 + j, i))
        at[0] = UNITS - 1
        for t in range(29, MT):
            step(t, 0, lambda j, t=t: half_to(eng, UNITS - 1))

    first, mix = Norm(0, *pre_sems), Norm(5, *pre_sems)
    updates = [update(n, Norm(k, *pre_sems)) for n, k in enumerate((1, 2, 3, 4, 6, 7))]
    ffn = [ffn_sems("ffn0"), ffn_sems("ffn1")]
    at1, at2 = attn_sems("attn1"), attn_sems("attn2")
    x_rows = x_in.rearrange("(t p) d -> p t d", p=P)

    with nc.Block() as block:

        @block.sync
        def _(sp):
            sp.dma_start(x[:], x_rows).then_inc(x_loaded, 16)
            for s in range(RING):
                sp.dma_start(raw[:, s, :], w[s]).then_inc(raw_loaded[s], 16)
                if s == 2:
                    sp.dma_start(misc[:], misc_in.to_broadcast([P, MISC])).then_inc(const_loaded, 16)
            sp.dma_start(tab[:, P:], tables_in[:, P:]).then_inc(const_loaded, 16)
            sp.dma_start(wdt[:], wdt_in).then_inc(const_loaded, 16)
            with sp.Fori(0, UNITS // RING - 1) as i:
                for s in range(RING):
                    sp.wait_ge(lo_done, s + 1 + RING * i)
                    sp.dma_start(raw[:, s, :], w[bass.ds(i * RING + RING + s, 1)].rearrange("a p n -> p (a n)")
                                 ).then_inc(raw_loaded[s], 16)
            sp.wait_ge(add_sems.added, 6 * TT)
            sp.dma_start(out.rearrange("(t p) d -> p t d", p=P), x[:]).then_inc(out_done, 16)
            sp.wait_ge(out_done, 16)

        @block.gpsimd
        def _(pool):
            def load_row(r):
                pool.dma_start(row[:, r % 2, :], rows_in[r:r + 1, :].to_broadcast([P, D])).then_inc(row_loaded[r % 2], 16)

            def updated(u):
                pool.wait_ge(add_sems.added, TT * (u + 1))

            pool.memset(pad[:], 0.0).then_inc(pad_ready, 1)
            load_row(0)
            load_row(1)
            pool.wait_ge(const_loaded, 48)
            pool.dma_start(G_WS, ws_in).then_inc(ws_loaded, 16)
            pool.wait_ge(ws_loaded, 16)
            pool.tensor_tensor(G_WS, G_WS, le.rearrange("p (a b) -> p a b", a=1).to_broadcast([P, GROUPS, P]),
                               ALU.mult).then_inc(g_sem.masked, 1)
            pool.wait_ge(updates[0].biased, TT)
            load_row(2)
            updated(0)
            load_row(3)
            updated(1)
            load_row(4)
            sgu_pool(pool)
            updated(2)
            load_row(5)
            updated(3)
            load_row(6)
            ssd_pool(pool)
            updated(4)

        @block.scalar
        def _(act):
            act.dma_start(ident, tables_in[:, T_ID:T_ID + P]).then_inc(ident_loaded, 16)
            act.dma_start(cols[:], cols_in).then_inc(cols_loaded, 16)
            norm_act(act, first, lambda tt: x[:, tt, :], lambda tt: (x_loaded, 16), 8)
            hi_to(act, 1)
            act.wait_ge(cols_loaded, 16)
            halves_act(act, first, 0)
            hi_to(act, 5)
            act.wait_ge(const_loaded, 48)
            act.activation(wdt_hi[:], wdt[:], ACT.Copy).then_inc(d_sem.w_hi, 1)
            hi_to(act, N_WO1 + RING - 1)
            attn_act(act, at1, True)
            hi_to(act, N_FFN0 - 1)
            update_act(act, updates[0], N_FFN0 - 1, 1, True)
            act.wait_ge(pad_ready, 1)
            ffn_act(act, ffn[0], N_FFN0)
            update_act(act, updates[1], N_SGV - 1, 2, False)
            sgu_act(act)
            update_act(act, updates[2], N_FFN1 - 1, 3, False)
            ffn_act(act, ffn[1], N_FFN1)
            update_act(act, updates[3], N_XBC - 1, 4, False)
            xbc_act(act)
            hi_to(act, N_QKV2 + 5)
            dt_act(act)
            hi_to(act, N_Z + 5)
            decay_act(act)
            ssd_act(act)
            z_act(act)
            norm_act(act, mix, lambda tt: ybuf[:, tt, :], lambda tt: (z_sem.gated, tt + 1), 8)
            halves_act(act, mix, 6)
            attn_act(act, at2, False)
            hi_to(act, N_MLP - 1)
            update_act(act, updates[4], N_MLP - 1, 5, False)
            mlp_act(act)
            update_act(act, updates[5], UNITS - 1, None, False)

        @block.vector
        def _(dve):
            norm_dve(dve, first, 8)
            scale_dve(dve, first, 8, x)
            lo_to(dve, 1)
            dve.wait_ge(cols_loaded, 16)
            halves_dve(dve, first, 0)
            dve.wait_ge(const_loaded, 48)
            qkv_dve(dve, N_QKV1, at1.qk, at1.v, True)
            dve.wait_ge(d_sem.w_hi, 1)
            dve.tensor_tensor(wdt_lo[:], wdt[:], wdt_hi[:].bitcast(F32), ALU.subtract).then_inc(d_sem.w_lo, 1)
            attn_dve(dve, at1, True, M_SINK1)
            lo_to(dve, N_FFN0 - 1)
            update_dve(dve, updates[0], N_FFN0 - 1, 1, 1, 0)
            ffn_dve(dve, ffn[0], N_FFN0, 0)
            update_dve(dve, updates[1], N_SGV - 1, 2, 2, None)
            sgu_dve(dve)
            update_dve(dve, updates[2], N_FFN1 - 1, 3, 3, None)
            ffn_dve(dve, ffn[1], N_FFN1, 1)
            update_dve(dve, updates[3], N_XBC - 1, 4, 4, None)
            xbc_dve(dve)
            dt_dve(dve)
            qkv_dve(dve, N_QKV2, at2.qk, at2.v, False)
            ssd_dve(dve)
            z_dve(dve)
            norm_dve(dve, mix, 8)
            scale_dve(dve, mix, 8, ybuf)
            halves_dve(dve, mix, 6)
            attn_dve(dve, at2, False, M_SINK2)
            lo_to(dve, N_MLP - 1)
            update_dve(dve, updates[4], N_MLP - 1, 5, 5, None)
            mlp_dve(dve)
            update_dve(dve, updates[5], UNITS - 1, None, 6, None)

        @block.tensor
        def _(pe):
            pe.wait_ge(ident_loaded, 16)
            turn_pe(pe, first)
            qkv_pe(pe, N_QKV1, at1.qk, first)
            attn_pe(pe, at1, True)
            pe.wait_ge(at1.lo, KV_HEADS)
            for k in range(KT):
                accumulate(pe, N_WO1 + k, KT + k, k == 0, k == KT - 1)
            turn_pe(pe, updates[0].pre)
            ffn_pe(pe, ffn[0], N_FFN0, updates[0].pre)
            turn_pe(pe, updates[1].pre)
            sgu_pe(pe, updates[1].pre)
            turn_pe(pe, updates[2].pre)
            ffn_pe(pe, ffn[1], N_FFN1, updates[2].pre)
            turn_pe(pe, updates[3].pre)
            xbc_pe(pe, updates[3].pre)
            dt_pe(pe)
            pe.wait_ge(x_sem.moved, XT - 2)
            qkv_pe(pe, N_QKV2, at2.qk)
            dt_sums_pe(pe)
            pe.wait_ge(at2.qk, QKT)
            pe.wait_ge(at2.v, TT)
            ssd_pe(pe)
            z_pe(pe)
            turn_pe(pe, mix)
            ready(pe, mix)
            attn_pe(pe, at2, False)
            pe.wait_ge(at2.lo, KV_HEADS)
            for k in range(2 * KT):
                accumulate(pe, N_WO2 + k, k, k == 0, k == 2 * KT - 1)
            turn_pe(pe, updates[4].pre)
            mlp_pe(pe, updates[4].pre)


def head_order():
    order = []
    for t in range(QT):
        for half in range(2):
            h = REP * (2 * (t // REP) + half) + t % REP
            order += range(h * DH, (h + 1) * DH)
    return np.array(order)


def as_features(m):
    k, n = m.shape
    return m.reshape(KT, P, n // P, P).transpose(2, 1, 0, 3).reshape(n // P, P, KT * P)


def as_tokens(m, width):
    k, n = m.shape
    nk = UNIT // width
    v = m.reshape(KT // nk, nk, P, n // width, width).transpose(3, 0, 2, 1, 4)
    return v.reshape(-1, P, UNIT)


def as_rows(m):
    return m.reshape(-1, P, D)


def interleave(head, groups, tail):
    return np.concatenate([head, np.stack(groups, 1).reshape(-1, P, UNIT), tail])


def ffn_units(w_in, w_out):
    g, u, o = as_features(w_in[:, :FT * P]), as_features(w_in[:, FT * P:]), as_rows(w_out)
    return interleave(np.stack([g[0], u[0]]), [g[1:], u[1:], o[:-1]], o[-1:])


def qkv_units(q, k, v):
    return np.concatenate([as_features(q[:, head_order()]), as_features(k), as_tokens(v, 256)])


def tiles(v):
    return v.reshape(-1, P).T


def tables():
    p, f = np.arange(P)[:, None], np.arange(P)[None, :]
    masks = [p == f, p <= f, p > f, p >= f, p < f, p >= 0 * f]
    own = np.where(p >= f, p - f, FAR)
    before = np.where(f > p, p + P - f, FAR)
    near = []
    for b in range(TT):
        dist = np.abs(p + b * P - np.arange(SEQ)[None, :])
        near.append(np.where(dist <= P, dist, FAR))
    return np.concatenate([*masks, own, before, own, *near], 1).astype(np.float32)


def kernel(**inputs):
    from concourse import bacc
    from concourse.bass_utils import run_bass_kernel_spmd

    v = {k: np.asarray(a) for k, a in inputs.items()}
    arrays = layouts(v)
    nc = bacc.Bacc("TRN2", target_bir_lowering=False, num_devices=1)
    aps = {n: nc.dram_tensor("in_" + n, a.shape, F32, kind="ExternalInput").ap() for n, a in arrays.items()}
    out = nc.dram_tensor("out", (SEQ, D), F32, kind="ExternalOutput").ap()
    build(nc, *(aps[n] for n in ("w", "x", "cols", "misc", "tables", "rows", "ws", "wdt")), out)
    r = run_bass_kernel_spmd(nc, [{"in_" + n: a for n, a in arrays.items()}], core_ids=[0])
    return r.results[0]["out"].reshape(1, SEQ, D)


def layouts(v):
    order = head_order()
    qkv, win2 = v["attn_w_qkv"][0], v["w_in_2"][0]
    z, xbc, dt, q2, k2, v2 = np.split(win2, np.cumsum([D, XT * P, 32, QT * P, 256]), 1)
    wout2 = v["w_out_2"][0]
    up, down = as_features(v["w_up_2"][0]), as_rows(v["w_down_2"][0])
    w = np.concatenate([
        qkv_units(qkv[:, :D], qkv[:, D:D + 256], qkv[:, D + 256:]),
        as_rows(v["attn_w_o"][0][order]),
        ffn_units(v["ffn_w_in"][0], v["ffn_w_out"][0]),
        as_tokens(v["sgu_w_in"][0][:, SG:], 512),
        as_features(v["sgu_w_in"][0][:, :SG]),
        as_rows(v["sgu_w_out"][0]),
        ffn_units(v["ffn_w_in"][1], v["ffn_w_out"][1]),
        as_features(xbc),
        qkv_units(q2, k2, v2),
        as_tokens(z, 512),
        as_rows(np.concatenate([wout2[:D], wout2[D:][order]])),
        interleave(up[:1], [up[1:], down[:-1]], down[-1:]),
    ])
    bq = v["attn_b_qkv"][0]
    gains = [v["norm_mix_pre"][0], v["norm_ffn_pre"][0], v["norm_mix_pre"][1], v["norm_ffn_pre"][1],
             v["norm_mix_pre_2"][0], v["norm_mlp_pre_2"][0], v["ssm_norm_2"][0]]
    conv = np.concatenate([v["ffn_conv_w"], v["ffn_conv_b"][:, None]], 1)
    conv = conv.reshape(2, 4, FT, P).transpose(3, 0, 2, 1).reshape(P, -1)
    xc = np.concatenate([v["conv_w_2"][0], v["conv_b_2"]], 0).reshape(6, XT, P).transpose(2, 1, 0).reshape(P, -1)
    ln = np.stack([v["sgu_ln_g"][0], v["sgu_ln_b"][0]]).reshape(2, SGT, P).transpose(2, 1, 0).reshape(P, -1)
    cols = np.concatenate([*(tiles(g) for g in gains), tiles(bq[:D][order]), tiles(bq[D:D + 256]), conv, xc, ln], 1)
    misc = np.concatenate([v["attn_sinks"][0], v["attn_sink_2"][0], bq[D + 256:], v["dt_bias_2"].ravel(),
                           v["a_log_2"].ravel(), v["d_skip_2"].ravel(), v["sgu_b_s"].ravel()])[None]
    rows = np.stack([v["attn_b_o"][0], v["norm_mix_post"][0], v["norm_ffn_post"][0], v["norm_mix_post"][1],
                     v["norm_ffn_post"][1], v["norm_mix_post_2"][0], v["norm_mlp_post_2"][0]])
    ws = v["sgu_w_s"][0].transpose(2, 0, 1)
    wdt = dt.reshape(KT, P, 32).transpose(1, 0, 2)
    arrays = dict(w=w, x=v["x"][0], cols=cols, misc=misc, tables=tables(), rows=rows, ws=ws, wdt=wdt)
    return {k: np.ascontiguousarray(a) for k, a in arrays.items()}
```

```python
import math
from collections import namedtuple

import concourse.bass as bass
import numpy as np
from concourse import mybir

F32 = mybir.dt.float32
F32R = mybir.dt.float32r
ACT = mybir.ActivationFunctionType
ALU = mybir.AluOpType
AX = mybir.AxisListType

P = 128
SEQ = 256
TT = SEQ // P
D = 1024
KT = D // P
EPS = 1e-6

HEADS, KV_HEADS, DH = 16, 4, 64
REP = HEADS // KV_HEADS
QT = HEADS * DH // P
KVT = KV_HEADS * DH // P
QKT = QT + KVT
QK_ORDER = [t for g in range(KVT) for t in (QT + g, *range(REP * g, REP * g + REP))]
SLOPE = [2.0 ** (-8.0 * (h + 1) / HEADS) for h in range(HEADS)]

FT = 2816 // P
SG = 3072
SGT = SG // P
SGC = SG // 512
GROUPS = 8
XT = 1536 // P
MT = 4096 // P

RING = 6
UNIT = 1024

N_QKV1 = 0
N_WO1 = N_QKV1 + QT + KVT + 2
N_FFN0 = N_WO1 + KT
N_SGV = N_FFN0 + 3 * FT
N_SGU = N_SGV + 4 * SGC
N_SGO = N_SGU + SGT
N_FFN1 = N_SGO + SGT
N_MIX = N_FFN1 + 3 * FT
N_Z = N_MIX + XT + QT + KVT + 2
N_WO2 = N_Z + KT
N_MLP = N_WO2 + 2 * KT
UNITS = N_MLP + 2 * MT
assert UNITS % RING == 0

C_GAIN = 0
C_BQK = C_GAIN + 7 * KT
C_CONV = C_BQK + QT + KVT
C_XBC = C_CONV + 2 * FT * 4
C_LN = C_XBC + XT * 6
COLS = C_LN + SGT * 2

M_SINK1, M_SINK2, M_BV, M_DTB, M_ALOG, M_SKIP, M_BS, MISC = np.cumsum(
    [0, HEADS, HEADS, KV_HEADS * DH, 2 * HEADS, 2 * HEADS, HEADS, GROUPS * P]).tolist()

T_ID, T_LE, T_GT, T_GE, T_LT, T_ONE, T_D1, T_D2, TABLES = np.cumsum(
    [0, P, P, P, P, P, P, 3 * P, 4 * P]).tolist()
FAR = 1e30


def build(nc, w, x_in, cols_in, misc_in, tables_in, rows_in, ws_in, wdt_in, out):
    def sb(name, shape, dt=F32):
        return nc.alloc_sbuf_tensor(name, shape, dt)

    def sem(name):
        return nc.alloc_semaphore(name)

    def signals(prefix, names):
        return namedtuple(prefix, names)(*(sem(f"{prefix}_{name}") for name in names.split()))

    raw = sb("raw", [P, RING, UNIT])
    w_hi = sb("w_hi", [P, RING, UNIT], F32R)
    w_lo = sb("w_lo", [P, RING, UNIT], F32R)
    x = sb("x", [P, TT, D])
    a_hi = sb("a_hi", [P, 2 * KT, SEQ], F32R)
    a_lo = sb("a_lo", [P, 2 * KT, SEQ], F32R)
    cols = sb("cols", [P, COLS])
    misc = sb("misc", [P, MISC])
    tab = sb("tab", [P, TABLES])
    row = sb("row", [P, 2, D])
    wdt = sb("wdt", [P, KT, 32])
    wdt_hi = sb("wdt_hi", [P, KT, 32], F32R)
    wdt_lo = sb("wdt_lo", [P, KT, 32], F32R)
    st = sb("st", [P, 96])
    pad = sb("pad", [P, 2, SEQ + 4])
    arena = sb("arena", [P, 16640])
    ps = nc.alloc_psum_tensor("ps", [P, 8, 512], F32)

    def cut(at, *shape):
        n = math.prod(shape)
        assert at + n <= 16640
        v = arena[:, at:at + n]
        if len(shape) == 1:
            return v
        names = "abcd"[:len(shape)]
        return v.rearrange(f"p ({' '.join(names)}) -> p {' '.join(names)}",
                           **{k: s for k, s in zip(names[1:], shape[1:])})

    ident, le, gt, ge, lt, one = (tab[:, o:o + P] for o in (T_ID, T_LE, T_GT, T_GE, T_LT, T_ONE))
    ybuf = cut(0, TT, D)
    junk = cut(2048, D)

    raw_loaded = [sem(f"raw_loaded{s}") for s in range(RING)]
    hi_done = sem("hi_done")
    lo_done = sem("lo_done")
    unit_used = sem("unit_used")
    x_loaded, ident_loaded, cols_loaded = sem("x_loaded"), sem("ident_loaded"), sem("cols_loaded")
    const_loaded, ws_loaded = sem("const_loaded"), sem("ws_loaded")
    row_loaded = [sem("row_loaded0"), sem("row_loaded1")]
    out_done, pad_ready = sem("out_done"), sem("pad_ready")

    def hi_of(act, n, i=0):
        s = n % RING
        act.wait_ge(raw_loaded[s], 16 * (n // RING + 1) + 16 * i)
        if n >= RING:
            act.wait_ge(unit_used, n - RING + 1 + RING * i)
        act.activation(w_hi[:, s, :], raw[:, s, :], ACT.Copy).then_inc(hi_done, 1)

    def lo_of(dve, n, i=0):
        s = n % RING
        dve.wait_ge(hi_done, n + 1 + RING * i)
        dve.tensor_tensor(w_lo[:, s, :], raw[:, s, :], w_hi[:, s, :].bitcast(F32),
                          ALU.subtract).then_inc(lo_done, 1)

    act_at, dve_at = [0], [0]

    def hi_to(act, n):
        while act_at[0] <= min(n, UNITS - 1):
            hi_of(act, act_at[0])
            act_at[0] += 1

    def lo_to(dve, n):
        while dve_at[0] <= min(n, UNITS - 1):
            lo_of(dve, dve_at[0])
            dve_at[0] += 1

    def three(pe, o, l_hi, l_lo, r_hi, r_lo, first, last):
        pe.matmul(o, l_hi, r_hi, start=first, stop=False)
        pe.matmul(o, l_hi, r_lo, start=False, stop=False)
        return pe.matmul(o, l_lo, r_hi, start=False, stop=last)

    def features(pe, n, o, i=0, pre=None):
        s = n % RING
        pe.wait_ge(lo_done, n + 1 + RING * i)
        for k in range(KT):
            if pre is not None:
                pe.wait_ge(pre.lo, KT * pre.n + k + 1)
            c = slice(k * P, (k + 1) * P)
            mm = three(pe, o, w_hi[:, s, c], w_lo[:, s, c], a_hi[:, k, :], a_lo[:, k, :],
                       k == 0, k == KT - 1)
        mm.then_inc(unit_used, 1)

    def tokens(pe, n, o, k0, nk, width, i=0, pre=None):
        s = n % RING
        pe.wait_ge(lo_done, n + 1 + RING * i)
        for k in range(nk):
            if pre is not None:
                pe.wait_ge(pre.lo, KT * pre.n + k0 + k + 1)
            c = slice(k * width, (k + 1) * width)
            for tt in range(TT):
                t = slice(tt * P, (tt + 1) * P)
                mm = three(pe, o[tt], a_hi[:, k0 + k, t], a_lo[:, k0 + k, t],
                           w_hi[:, s, c], w_lo[:, s, c], k0 + k == 0, k0 + k == KT - 1)
        mm.then_inc(unit_used, 1)

    def accumulate(pe, n, slot, first, last, i=0):
        s = n % RING
        pe.wait_ge(lo_done, n + 1 + RING * i)
        for tt in range(TT):
            t = slice(tt * P, (tt + 1) * P)
            for a, b, f, z in ((a_hi, w_hi, first, False), (a_hi, w_lo, False, False),
                               (a_lo, w_hi, False, last)):
                for c in range(2):
                    mm = pe.matmul(ps[:, 2 * tt + c, :], a[:, slot, t],
                                   b[:, s, c * 512:(c + 1) * 512], start=f, stop=z)
        mm.then_inc(unit_used, 1)

    pre_sems = signals("pre", "sum mean root inv scaled turned hi lo")
    post_sems = signals("post", "sum mean root inv scaled turned hi lo")
    add_sems = signals("update", "biased term added")

    Norm = namedtuple("Norm", "n sum mean root inv scaled turned hi lo")
    Update = namedtuple("Update", "n post pre biased term added")

    def turn_pe(pe, q, base=4):
        for tt in range(TT):
            pe.wait_ge(q.scaled, TT * q.n + tt + 1)
            for k in range(KT):
                o = turned(k, base)[:, tt * P:(tt + 1) * P]
                mm = pe.transpose(o, ybuf[:, tt, k * P:(k + 1) * P], ident)
            mm.then_inc(q.turned, 1)

    def norm_squares(act, q, view, done, c0):
        for tt in range(TT):
            act.wait_ge(*done(tt))
            if tt:
                act.wait_ge(q.sum, TT * q.n + tt)
            act.activation(junk[:, :], view(tt), ACT.Square,
                           accum_out=st[:, c0 + tt:c0 + tt + 1]).then_inc(q.sum, 1)

    def norm_root(act, q, c0):
        act.wait_ge(q.mean, q.n + 1)
        act.activation(st[:, c0 + 4:c0 + 6], st[:, c0 + 2:c0 + 4], ACT.Sqrt).then_inc(q.root, 1)

    def norm_act(act, q, view, done, c0):
        norm_squares(act, q, view, done, c0)
        norm_root(act, q, c0)

    def norm_mean(dve, q, c0):
        dve.wait_ge(q.sum, TT * (q.n + 1))
        dve.tensor_scalar(st[:, c0 + 2:c0 + 4], st[:, c0:c0 + 2], 1.0 / D, EPS,
                          ALU.mult, ALU.add).then_inc(q.mean, 1)

    def norm_inverse(dve, q, c0):
        dve.wait_ge(q.root, q.n + 1)
        dve.reciprocal(st[:, c0 + 6:c0 + 8], st[:, c0 + 4:c0 + 6]).then_inc(q.inv, 1)
        dve.wait_ge(q.inv, q.n + 1)

    def norm_dve(dve, q, c0):
        norm_mean(dve, q, c0)
        norm_inverse(dve, q, c0)

    def scale_dve(dve, q, c0, src):
        for tt in range(TT):
            dve.tensor_scalar(ybuf[:, tt, :], src[:, tt, :], st[:, c0 + 6 + tt:c0 + 7 + tt], None,
                              ALU.mult).then_inc(q.scaled, 1)

    def turned(k, base=4):
        return ps[:, base + k % 4, (k // 4) * SEQ:(k // 4 + 1) * SEQ]

    def gain(g, k):
        return cols[:, C_GAIN + g * KT + k:C_GAIN + g * KT + k + 1]

    def halves_act(act, q, g, base=4, tiles=range(KT)):
        act.wait_ge(q.turned, TT * (q.n + 1))
        for k in tiles:
            if k >= 4:
                act.wait_ge(q.lo, KT * q.n + k - 3)
            act.activation(a_hi[:, k, :], turned(k, base), ACT.Copy, scale=gain(g, k)).then_inc(q.hi, 1)

    def halves_dve(dve, q, g, base=4):
        dve.wait_ge(q.turned, TT * (q.n + 1))
        for k in range(KT):
            dve.wait_ge(q.hi, KT * q.n + k + 1)
            dve.scalar_tensor_tensor(a_lo[:, k, :], turned(k, base), gain(g, k),
                                     a_hi[:, k, :].bitcast(F32), ALU.mult,
                                     ALU.subtract).then_inc(q.lo, 1)

    def update(n, pre):
        return Update(n, Norm(n, *post_sems), pre, *add_sems)

    acc = [ps[:, 2 * tt:2 * tt + 2, :].rearrange("p a b -> p (a b)") for tt in range(TT)]

    def update_act(act, u, n_last, g, bias):
        hi_to(act, n_last + RING - 1)
        if bias:
            norm_act(act, u.post, lambda tt: ybuf[:, tt, :], lambda tt: (u.biased, tt + 1), 0)
        else:
            norm_act(act, u.post, lambda tt: acc[tt],
                     lambda tt: (u.term, TT * u.n + 1) if tt else (unit_used, n_last + 1), 0)
        if g is None:
            return
        norm_act(act, u.pre, lambda tt: x[:, tt, :], lambda tt: (u.added, TT * u.n + tt + 1), 8)
        halves_act(act, u.pre, g)

    def update_dve(dve, u, n_last, g, r, bias):
        lo_to(dve, n_last + RING - 1)
        dve.wait_ge(row_loaded[r % 2], 16 * (r // 2 + 1))
        dve.wait_ge(unit_used, n_last + 1)
        if bias is not None:
            dve.wait_ge(row_loaded[bias % 2], 16 * (bias // 2 + 1))
            for tt in range(TT):
                dve.tensor_tensor(ybuf[:, tt, :], acc[tt], row[:, bias % 2, :],
                                  ALU.add).then_inc(u.biased, 1)
            for tt in range(TT):
                dve.wait_ge(u.post.sum, TT * u.n + tt + 1)
                dve.tensor_tensor(ybuf[:, tt, :], ybuf[:, tt, :], row[:, r % 2, :],
                                  ALU.mult).then_inc(u.term, 1)
        else:
            for n, tt in enumerate((1, 0)):
                if n:
                    dve.wait_ge(u.post.sum, TT * u.n + 1)
                dve.tensor_tensor(ybuf[:, tt, :], acc[tt], row[:, r % 2, :], ALU.mult).then_inc(u.term, 1)
        norm_dve(dve, u.post, 0)
        dve.wait_ge(u.term, TT * (u.n + 1))
        for tt in range(TT):
            dve.scalar_tensor_tensor(x[:, tt, :], ybuf[:, tt, :], st[:, 6 + tt:7 + tt], x[:, tt, :],
                                     ALU.mult, ALU.add).then_inc(u.added, 1)
        dve.wait_ge(u.added, TT * (u.n + 1))
        if g is None:
            return
        norm_dve(dve, u.pre, 8)
        scale_dve(dve, u.pre, 8, x)
        halves_dve(dve, u.pre, g)

    F_CV, F_GL, F_PR = cut(3072, 2, SEQ), cut(3584, 2, SEQ), cut(4096, 2, SEQ)

    def ffn_sems(name):
        return signals(name, "copied conv gelu product hi lo")

    def f_g(n0, t):
        return n0 + 3 * t - 1 if t else n0

    def f_out(n0, t):
        return n0 + 3 * FT - 1 if t == FT - 1 else n0 + 4 + 3 * t

    def ffn_in_pe(pe, f, n0, t, i=0, first=False):
        b = t % 2
        if not first:
            pe.wait_ge(f.product, t - 1 + 2 * i)
        features(pe, f_g(n0, t), ps[:, 4 + b, 0:SEQ], i)
        features(pe, f_g(n0, t) + 1, ps[:, 6 + b, 0:SEQ], i)

    def f_banks(t, i):
        return (0, 1) if t == 0 and isinstance(i, int) else (4 + t % 2, 6 + t % 2)

    def ready(pe, q):
        pe.wait_ge(q.lo, KT * (q.n + 1))

    def ffn_pe(pe, f, n0, pre):
        for n in range(2):
            features(pe, n0 + n, ps[:, n, 0:SEQ], pre=pre)
        ffn_in_pe(pe, f, n0, 1, first=True)
        pe.wait_ge(f.lo, 1)
        accumulate(pe, f_out(n0, 0), KT, True, False)
        with pe.Fori(0, (FT - 2) // 2) as i:
            for t in (2, 3):
                ffn_in_pe(pe, f, n0, t, i)
                pe.wait_ge(f.lo, t + 2 * i)
                accumulate(pe, f_out(n0, t - 1), KT + (t - 1) % 2, False, False, i)
        pe.wait_ge(f.lo, FT)
        accumulate(pe, f_out(n0, FT - 1), KT + (FT - 1) % 2, False, True)

    def ffn_act_step(act, f, n0, t, i, split):
        b = t % 2
        act.wait_ge(unit_used, f_g(n0, t) + 1 + RING * i)
        if t >= 2:
            act.wait_ge(f.conv, 3 * t - 3 + 6 * i)
        act.activation(pad[:, b, 2:2 + SEQ], ps[:, f_banks(t, i)[0], 0:SEQ], ACT.Copy).then_inc(f.copied, 1)
        split(0)
        act.wait_ge(f.conv, 3 * t + 3 + 6 * i)
        if t >= 2:
            act.wait_ge(f.product, t - 1 + 2 * i)
        act.activation(F_GL[:, b, :], F_CV[:, b, :], ACT.Gelu_apprx_tanh).then_inc(f.gelu, 1)
        split(1)
        act.wait_ge(f.product, t + 1 + 2 * i)
        if t >= 2:
            act.wait_ge(unit_used, f_out(n0, t - 2) + 1 + RING * i)
        act.activation(a_hi[:, KT + b, :], F_PR[:, b, :], ACT.Copy).then_inc(f.hi, 1)
        split(2)

    def ffn_dve_step(dve, f, n0, layer, t, i, split):
        b = t % 2
        c = C_CONV + (layer * FT + t) * 4

        def col(k):
            return cols[:, bass.ds(c + k + 8 * i, 1)] if not isinstance(i, int) else cols[:, c + k:c + k + 1]

        dve.wait_ge(f.copied, t + 1 + 2 * i)
        if t >= 2:
            dve.wait_ge(f.gelu, t - 1 + 2 * i)
        dve.tensor_scalar(F_CV[:, b, :], pad[:, b, 0:SEQ], col(0), col(3), ALU.mult,
                          ALU.add).then_inc(f.conv, 1)
        for k in (1, 2):
            dve.wait_ge(f.conv, 3 * t + k + 6 * i)
            dve.scalar_tensor_tensor(F_CV[:, b, :], pad[:, b, k:k + SEQ], col(k), F_CV[:, b, :],
                                     ALU.mult, ALU.add).then_inc(f.conv, 1)
        split(0)
        split(1)
        dve.wait_ge(f.gelu, t + 1 + 2 * i)
        dve.wait_ge(unit_used, f_g(n0, t) + 2 + RING * i)
        dve.tensor_tensor(F_PR[:, b, :], F_GL[:, b, :], ps[:, f_banks(t, i)[1], 0:SEQ],
                          ALU.mult).then_inc(f.product, 1)
        split(2)
        dve.wait_ge(f.hi, t + 1 + 2 * i)
        dve.tensor_tensor(a_lo[:, KT + b, :], F_PR[:, b, :], a_hi[:, KT + b, :].bitcast(F32),
                          ALU.subtract).then_inc(f.lo, 1)

    def ffn_run(eng, step, half_of, half_to, at, n0):
        half_to(eng, n0 + 5)
        step(0, 0, lambda j: half_to(eng, n0 + 6 + min(j, 1)))
        step(1, 0, lambda j: half_to(eng, n0 + 8 + j))
        with eng.Fori(0, (FT - 2) // 2) as i:
            for t in (2, 3):
                step(t, i, lambda j, t=t: half_of(eng, f_g(n0, t) + 6 + j, i))
        at[0] = n0 + 8 + 3 * (FT - 1)

    def ffn_act(act, f, n0):
        ffn_run(act, lambda t, i, s: ffn_act_step(act, f, n0, t, i, s), hi_of, hi_to, act_at, n0)

    def ffn_dve(dve, f, n0, layer):
        ffn_run(dve, lambda t, i, s: ffn_dve_step(dve, f, n0, layer, t, i, s), lo_of, lo_to, dve_at, n0)

    A_Q, A_K, A_V = cut(3072, QT, SEQ), cut(5120, KVT, SEQ), cut(5632, TT, KV_HEADS * DH)

    def qk_bank(j):
        return 4 + j % 4 if j else 0

    def qk1_pe(pe, j, pre=None):
        if j >= 4:
            pe.wait_ge(at1.qk, j - 3)
        features(pe, N_QKV1 + j, ps[:, qk_bank(j), 0:SEQ], pre=pre)

    def v1_pe(pe):
        pe.wait_ge(at1.qk, QKT - 2)
        for h in range(2):
            tokens(pe, N_QKV1 + QKT + h, [ps[:, 6, 0:256], ps[:, 7, 0:256]], 4 * h, 4, 256)

    def qk1_dve(dve, j):
        dve.wait_ge(unit_used, N_QKV1 + j + 1)
        is_k, g = j % (1 + REP) == 0, j // (1 + REP)
        dst = A_K[:, g, :] if is_k else A_Q[:, j - 1 - g, :]
        dve.tensor_scalar(dst, ps[:, qk_bank(j), 0:SEQ], cols[:, C_BQK + j:C_BQK + j + 1],
                          1.0 if is_k else DH ** -0.5, ALU.add, ALU.mult).then_inc(at1.qk, 1)

    def v1_dve(dve):
        dve.wait_ge(unit_used, N_QKV1 + QKT + 2)
        for tt in range(TT):
            dve.tensor_tensor(A_V[:, tt, :], ps[:, 6 + tt, 0:256], misc[:, M_BV:M_BV + 256],
                              ALU.add).then_inc(at1.v, 1)

    A_S, A_PT = cut(6144, 3, REP, 512), cut(14336, 2, 512)

    def attn_plan(first):
        seen = [[0], [0, 1]] if first else [[0, 1], [0, 1]]
        at, off = [], 0
        for keys in seen:
            at.append(off)
            off += P * len(keys)
        return seen, at, off

    def attn_sems(name):
        return signals(name, "qk v scores biased stat exp den norm0 norm1 turned copied out hi lo")

    AttnPe = namedtuple("AttnPe", "scores turn values")
    AttnAct = namedtuple("AttnAct", "exponentials copy high")
    AttnDve = namedtuple("AttnDve", "maxima divide low")

    def attn_pe(pe, q, first):
        seen, at, width = attn_plan(first)

        def scores(g, r):
            half = slice(64 * (g % 2), 64 * (g % 2) + 64)
            if g >= 1:
                pe.wait_ge(q.biased, REP * (g - 1) + r + 1)
            for b in range(TT):
                keys = seen[b]
                mm = pe.matmul(ps[:, r, at[b]:at[b] + P * len(keys)],
                               A_Q[half, REP * (g // 2) + r, b * P:(b + 1) * P],
                               A_K[half, g // 2, keys[0] * P:(keys[-1] + 1) * P],
                               start=True, stop=True)
            mm.then_inc(q.scores, 1)

        def turn(h):
            g, r = h // REP, h % REP
            pe.wait_ge(q.norm0, g + 1)
            pe.wait_ge(q.norm1, g + 1)
            if h >= 2:
                pe.wait_ge(q.copied, h - 1)
            for j in range(width // P):
                mm = pe.transpose(ps[:, 4 + h % 2, j * P:(j + 1) * P],
                                  A_S[:, g % 3, r, j * P:(j + 1) * P], ident)
            mm.then_inc(q.turned, 1)

        def values(h):
            g, r = h // REP, h % REP
            half = slice(64 * (r % 2), 64 * (r % 2) + 64)
            pe.wait_ge(q.copied, h + 1)
            if g >= 2 and r == 0:
                pe.wait_ge(q.lo, g - 1)
            for b in range(TT):
                o = (r // 2) * SEQ + b * P
                for j, kb in enumerate(seen[b]):
                    c = at[b] + j * P
                    mm = pe.matmul(ps[half, 6 + g % 2, o:o + P], A_V[:, kb, g * DH:(g + 1) * DH],
                                   A_PT[:, h % 2, c:c + P], start=(j == 0), stop=(j == len(seen[b]) - 1))
            if r == REP - 1:
                mm.then_inc(q.out, 1)

        return AttnPe(scores, turn, values)

    stq = sb("stq", [P, 2, 7, 2 * REP])

    def attn_act(act, q, first):
        seen, at, width = attn_plan(first)

        def exponentials(g, heads=range(REP)):
            if heads[0] == 0:
                act.wait_ge(q.stat, 5 * g + 5)
                if g >= 2:
                    act.wait_ge(q.den, 2 * g - 3)
                act.activation(stq[:, g % 2, 3, :], stq[:, g % 2, 2, :], ACT.Exp).then_inc(q.exp, 1)
            for r in heads:
                for b in range(TT):
                    s = A_S[:, g % 3, r, at[b]:at[b] + P * len(seen[b])]
                    k = b * REP + r
                    act.activation(s, s, ACT.Exp, bias=stq[:, g % 2, 1, k:k + 1],
                                   accum_out=stq[:, g % 2, 4, k:k + 1]).then_inc(q.exp, 1)

        def copy(h):
            act.wait_ge(q.turned, h + 1)
            act.activation(A_PT[:, h % 2, 0:width], ps[:, 4 + h % 2, 0:width],
                           ACT.Copy).then_inc(q.copied, 1)

        def high(g):
            act.wait_ge(q.out, g + 1)
            t = KT + 2 * g
            act.activation(a_hi[:, t:t + 2, :].rearrange("p a b -> p (a b)"), ps[:, 6 + g % 2, :],
                           ACT.Copy).then_inc(q.hi, 1)

        return AttnAct(exponentials, copy, high)

    def attn_normalise(eng, q, first, g, b, done):
        seen, at, width = attn_plan(first)
        s = A_S[:, g % 3, :, at[b]:at[b] + P * len(seen[b])]
        inv = stq[:, g % 2, 6, b * REP:(b + 1) * REP].rearrange("p (r a) -> p r a", a=1)
        eng.wait_ge(q.den, 2 * g + 2)
        eng.tensor_tensor(s, s, inv.to_broadcast([P, REP, P * len(seen[b])]), ALU.mult).then_inc(done, 1)

    def attn_pool(pool, q, first):
        for g in range(KV_HEADS):
            attn_normalise(pool, q, first, g, 1, q.norm1)

    def attn_dve(dve, q, first, m_sink):
        seen, at, width = attn_plan(first)
        dist = tab[:, T_D1:T_D1 + width] if first else tab[:, T_D2:T_D2 + width]

        def maxima(g):
            if g >= 3:
                dve.wait_ge(q.turned, REP * (g - 2))
            if g >= 2:
                dve.wait_ge(q.exp, 9 * (g - 1))
            stat = lambda k: stq[:, g % 2, k, :]
            for r in range(REP):
                h = REP * g + r
                dve.wait_ge(q.scores, h + 1)
                dve.scalar_tensor_tensor(A_S[:, g % 3, r, 0:width], dist, -SLOPE[h],
                                         ps[:, r, 0:width], ALU.mult, ALU.add).then_inc(q.biased, 1)
            dve.wait_ge(q.biased, REP * (g + 1))
            for b in range(TT):
                dve.tensor_reduce(stat(0)[:, b * REP:(b + 1) * REP],
                                  A_S[:, g % 3, :, at[b]:at[b] + P * len(seen[b])],
                                  AX.X, ALU.max).then_inc(q.stat, 1)
            dve.wait_ge(q.stat, 5 * g + 2)
            sink = misc[:, m_sink + REP * g:m_sink + REP * (g + 1)]
            both = sink.rearrange("p (a r) -> p a r", a=1).to_broadcast([P, TT, REP])
            two = lambda k: stat(k).rearrange("p (b r) -> p b r", b=TT)
            dve.tensor_tensor(two(0), two(0), both, ALU.max).then_inc(q.stat, 1)
            dve.wait_ge(q.stat, 5 * g + 3)
            dve.tensor_scalar(stat(1), stat(0), -1.0, None, ALU.mult).then_inc(q.stat, 1)
            dve.tensor_tensor(two(2), both, two(0), ALU.subtract).then_inc(q.stat, 1)

        def divide(g):
            stat = lambda k: stq[:, g % 2, k, :]
            dve.wait_ge(q.exp, 9 * (g + 1))
            dve.tensor_tensor(stat(5), stat(4), stat(3), ALU.add).then_inc(q.den, 1)
            dve.wait_ge(q.den, 2 * g + 1)
            if g >= 2:
                dve.wait_ge(q.norm0, g - 1)
                dve.wait_ge(q.norm1, g - 1)
            dve.reciprocal(stat(6), stat(5)).then_inc(q.den, 1)
            attn_normalise(dve, q, first, g, 0, q.norm0)

        def low(g):
            dve.wait_ge(q.hi, g + 1)
            t = KT + 2 * g
            dve.tensor_tensor(a_lo[:, t:t + 2, :].rearrange("p a b -> p (a b)"), ps[:, 6 + g % 2, :],
                              a_hi[:, t:t + 2, :].rearrange("p a b -> p (a b)").bitcast(F32),
                              ALU.subtract).then_inc(q.lo, 1)

        return AttnDve(maxima, divide, low)

    def wo1(pe, k):
        pe.wait_ge(at1.lo, k // 2 + 1)
        accumulate(pe, N_WO1 + k, KT + k, k == 0, k == KT - 1)

    def attn1_pe(pe):
        at = attn_pe(pe, at1, True)
        for j in range(QKT):
            if j == 5:
                pe.wait_ge(at1.qk, 5)
                for r in range(REP):
                    at.scores(0, r)
            if j == 7:
                for r in range(REP):
                    at.scores(1, r)
            qk1_pe(pe, j, None if j else first)
        v1_pe(pe)
        pe.wait_ge(at1.qk, QKT)
        for r in range(REP):
            at.scores(2, r)
        pe.wait_ge(at1.v, TT)
        at.turn(0)
        for h in range(HEADS):
            if h == HEADS - REP - 1:
                pe.wait_ge(at1.biased, HEADS)
            if h >= HEADS - REP - 1 and h < HEADS - 1:
                wo1(pe, h - (HEADS - REP - 1))
            if h + 1 < HEADS:
                at.turn(h + 1)
            at.values(h)
            if h < REP:
                at.scores(3, h)
        for k in range(REP, KT):
            wo1(pe, k)

    def attn1_act(act):
        at = attn_act(act, at1, True)
        hi_to(act, N_QKV1 + 10)
        at.exponentials(0)
        hi_to(act, N_QKV1 + 13)
        at.exponentials(1)
        hi_to(act, N_WO1 + RING - 1)
        for g in range(KV_HEADS):
            for r in range(REP):
                at.copy(REP * g + r)
                if r and g + 2 < KV_HEADS:
                    at.exponentials(g + 2, ([0], [1], [2, 3])[r - 1])
            at.high(g)

    def attn1_dve(dve):
        at = attn_dve(dve, at1, True, M_SINK1)
        for j in range(5):
            lo_to(dve, N_QKV1 + j + 5)
            qk1_dve(dve, j)
        lo_to(dve, N_QKV1 + 10)
        at.maxima(0)
        qk1_dve(dve, 5)
        qk1_dve(dve, 6)
        at.maxima(1)
        qk1_dve(dve, 7)
        lo_to(dve, N_QKV1 + 12)
        at.divide(0)
        qk1_dve(dve, 8)
        qk1_dve(dve, 9)
        lo_to(dve, N_QKV1 + 13)
        at.maxima(2)
        v1_dve(dve)
        at.divide(1)
        lo_to(dve, N_WO1 + RING - 1)
        at.maxima(3)
        at.low(0)
        at.divide(2)
        at.low(1)
        at.divide(3)
        at.low(2)
        at.low(3)

    G_V, G_U = cut(0, TT, SG), cut(TT * SG, SGT, SEQ)
    G_WS, G_R = cut(12288, GROUPS, P), cut(13312, GROUPS, P)
    G_VN, G_AFF, G_PR = cut(14336, 3, TT, P), cut(15104, 3, P), cut(15488, 3, SEQ)
    lns = sb("lns", [P, 40])
    L_SUM, L_SQ, L_TOT, L_NEG, L_VSUM, L_VAR, L_ROOT, L_INV, L_SHIFT = 0, 12, 24, 26, 28, 30, 32, 34, 36
    g_sem = signals("sgu", "v u masked rows rows_out stat square root vn mixed affine gated product hi lo")
    VB = (2, 4, 6)

    def sgu_v_pe(pe, c, first=False, pre=None):
        if not first:
            pe.wait_ge(g_sem.v, 2 * (c - 2))
        b = VB[c % 3]
        for k in range(4):
            tokens(pe, N_SGV + 4 * c + k, [ps[:, b, :], ps[:, b + 1, :]], 2 * k, 2, 512, pre=pre)

    def sgu_spatial(pe, j, i=0):
        pe.wait_ge(g_sem.vn, 2 * j + 2 + 12 * i)
        if j >= 3:
            pe.wait_ge(g_sem.gated, j - 2 + 6 * i)
        for c in range(TT):
            g = j // 3
            rhs = G_WS[:, g, :] if isinstance(i, int) else \
                G_WS[:, bass.ds(g + 2 * i, 1), :].rearrange("p a t -> p (a t)")
            mm = pe.matmul(ps[:, 4 + j % 3, c * P:(c + 1) * P], G_VN[:, j % 3, c, :], rhs,
                           start=True, stop=True)
        mm.then_inc(g_sem.mixed, 1)

    def sgu_pe(pe, pre):
        pe.wait_ge(g_sem.masked, 1)
        for h in range(2):
            mm = pe.matmul(ps[:, h, :], one, G_WS[:, 4 * h:4 * h + 4, :], start=True, stop=True)
        mm.then_inc(g_sem.rows, 1)
        for c in range(3):
            sgu_v_pe(pe, c, first=True, pre=None if c else pre)
        for c in range(3, 6):
            sgu_v_pe(pe, c)
        pe.wait_ge(g_sem.v, 2 * SGC)
        for p in range(3):
            for k in range(2):
                features(pe, N_SGU + 2 * p + k, ps[:, 4 + p, k * SEQ:(k + 1) * SEQ])
        with pe.Fori(0, SGT // 6 - 1) as i:
            for p in range(3, 6):
                pe.wait_ge(g_sem.u, p - 2 + 3 * i)
                for k in range(2):
                    features(pe, N_SGU + 2 * p + k, ps[:, 4 + p % 3, k * SEQ:(k + 1) * SEQ], i)
        pe.wait_ge(g_sem.u, SGT // 2)

        def out_tile(j, i=0):
            pe.wait_ge(g_sem.lo, j + 1 + 6 * i)
            accumulate(pe, N_SGO + j, KT + j % 3, j == 0, j == SGT - 1, i)

        for j in range(3):
            sgu_spatial(pe, j)
        out_tile(0)
        with pe.Fori(0, 3) as i:
            for j in range(1, 7):
                sgu_spatial(pe, j + 2, i)
                out_tile(j, i)
        for j in range(19, SGT):
            if j + 2 < SGT:
                sgu_spatial(pe, j + 2)
            out_tile(j)

    def sgu_act(act):
        act.wait_ge(g_sem.rows, 1)
        act.activation(G_R.rearrange("p a b -> p (a b)"), ps[:, 0:2, :].rearrange("p a b -> p (a b)"),
                       ACT.Copy).then_inc(g_sem.rows_out, 1)
        hi_to(act, N_SGV + 5)
        for c in range(SGC):
            hi_to(act, N_SGV + 4 * c + 8)
            for tt in range(TT):
                act.wait_ge(unit_used, N_SGV + 4 * c + 4)
                act.activation(G_V[:, tt, c * 512:(c + 1) * 512], ps[:, VB[c % 3] + tt, :],
                               ACT.Gelu_apprx_tanh,
                               accum_out=lns[:, L_SUM + 6 * tt + c:L_SUM + 6 * tt + c + 1]).then_inc(g_sem.v, 1)
            hi_to(act, N_SGV + 4 * c + 9)

        def moments():
            act.wait_ge(g_sem.stat, 2)
            for tt in range(TT):
                for c in range(SGC):
                    if tt or c:
                        act.wait_ge(g_sem.square, SGC * tt + c)
                    act.activation(G_PR[:, 0:2, :].rearrange("p a b -> p (a b)"), G_V[:, tt, c * 512:(c + 1) * 512],
                                   ACT.Square, bias=lns[:, L_NEG + tt:L_NEG + tt + 1],
                                   accum_out=lns[:, L_SQ + 6 * tt + c:L_SQ + 6 * tt + c + 1]).then_inc(g_sem.square, 1)
            act.wait_ge(g_sem.stat, 4)
            act.activation(lns[:, L_ROOT:L_ROOT + 2], lns[:, L_VAR:L_VAR + 2], ACT.Sqrt).then_inc(g_sem.root, 1)

        def pair(p, i, split):
            split(0)
            act.wait_ge(unit_used, N_SGU + 2 * p + 2 + 6 * i)
            dst = G_U[:, 2 * p:2 * p + 2, :] if isinstance(i, int) else G_U[:, bass.ds(2 * p + 6 * i, 2), :]
            act.activation(dst.rearrange("p a b -> p (a b)"), ps[:, 4 + p % 3, :],
                           ACT.Gelu_apprx_tanh).then_inc(g_sem.u, 1)
            split(1)

        for p in range(3):
            pair(p, 0, lambda j, p=p: hi_to(act, N_SGU + 2 * p + 6 + j))
        moments()
        with act.Fori(0, SGT // 6 - 1) as i:
            for p in range(3, 6):
                pair(p, i, lambda j, p=p: hi_of(act, N_SGU + 2 * p + 6 + j, i))
        act_at[0] = N_SGO + 6

        def vn(j, i=0):
            if j >= 3:
                act.wait_ge(g_sem.mixed, j - 2 + 6 * i)
            for tt in range(TT):
                src = G_V[:, tt, j * P:(j + 1) * P] if isinstance(i, int) else \
                    G_V[:, tt, bass.ds(j * P + 6 * P * i, P)]
                act.activation(G_VN[:, j % 3, tt, :], src, ACT.Identity,
                               bias=lns[:, L_SHIFT + tt:L_SHIFT + tt + 1],
                               scale=lns[:, L_INV + tt:L_INV + tt + 1]).then_inc(g_sem.vn, 1)

        def high(j, i=0):
            act.wait_ge(g_sem.product, j + 1 + 6 * i)
            if j >= 3:
                act.wait_ge(unit_used, N_SGO + j - 2 + 6 * i)
            act.activation(a_hi[:, KT + j % 3, :], G_PR[:, j % 3, :], ACT.Copy).then_inc(g_sem.hi, 1)

        act.wait_ge(g_sem.stat, 6)
        for j in range(4):
            if j == 3:
                high(0)
            vn(j)
        high(1)
        with act.Fori(0, 3) as i:
            for j in range(1, 7):
                vn(j + 3, i)
                high(j + 1, i)
                hi_of(act, N_SGO + j + 5, i)
        act_at[0] = N_SGO + 24
        for j in range(19, SGT):
            if j + 3 < SGT:
                vn(j + 3)
            if j + 1 < SGT:
                high(j + 1)
            hi_to(act, N_SGO + j + 5)

    def sgu_dve(dve):
        lo_to(dve, N_SGV + 4 * SGC - 1 + 6)
        dve.wait_ge(g_sem.v, 2 * SGC)
        dve.tensor_reduce(lns[:, L_TOT:L_TOT + 2], lns[:, L_SUM:L_SUM + 12].rearrange("p (a b) -> p a b", a=2),
                          AX.X, ALU.add).then_inc(g_sem.stat, 1)
        dve.wait_ge(g_sem.stat, 1)
        dve.tensor_scalar(lns[:, L_NEG:L_NEG + 2], lns[:, L_TOT:L_TOT + 2], -1.0 / SG, None,
                          ALU.mult).then_inc(g_sem.stat, 1)
        lo_to(dve, N_SGU + 11)
        dve.wait_ge(g_sem.square, 12)
        dve.tensor_reduce(lns[:, L_VSUM:L_VSUM + 2], lns[:, L_SQ:L_SQ + 12].rearrange("p (a b) -> p a b", a=2),
                          AX.X, ALU.add).then_inc(g_sem.stat, 1)
        dve.wait_ge(g_sem.stat, 3)
        dve.tensor_scalar(lns[:, L_VAR:L_VAR + 2], lns[:, L_VSUM:L_VSUM + 2], 1.0 / SG, EPS,
                          ALU.mult, ALU.add).then_inc(g_sem.stat, 1)
        dve.wait_ge(g_sem.root, 1)
        dve.reciprocal(lns[:, L_INV:L_INV + 2], lns[:, L_ROOT:L_ROOT + 2]).then_inc(g_sem.stat, 1)
        dve.wait_ge(g_sem.stat, 5)
        dve.tensor_tensor(lns[:, L_SHIFT:L_SHIFT + 2], lns[:, L_INV:L_INV + 2], lns[:, L_NEG:L_NEG + 2],
                          ALU.mult).then_inc(g_sem.stat, 1)
        with dve.Fori(0, SGT // 6 - 1) as i:
            for n in range(12, 18):
                lo_of(dve, N_SGU + n, i)
        dve_at[0] = N_SGO + 6

        def gate(j, i=0):
            b = j % 3
            c = C_LN + 2 * j
            g = cols[:, c:c + 1] if isinstance(i, int) else cols[:, bass.ds(c + 12 * i, 1)]
            u = G_U[:, j, :] if isinstance(i, int) else \
                G_U[:, bass.ds(j + 6 * i, 1), :].rearrange("p a t -> p (a t)")
            dve.wait_ge(g_sem.mixed, j + 1 + 6 * i)
            dve.wait_ge(g_sem.affine, 2 * j + 2 + 12 * i)
            if j >= 3:
                dve.wait_ge(g_sem.lo, j - 2 + 6 * i)
            dve.scalar_tensor_tensor(G_PR[:, b, :].rearrange("p (c t) -> p c t", c=TT),
                                     ps[:, 4 + b, 0:SEQ].rearrange("p (c t) -> p c t", c=TT), g,
                                     G_AFF[:, b:b + 1, :].to_broadcast([P, TT, P]), ALU.mult,
                                     ALU.add).then_inc(g_sem.gated, 1)
            dve.wait_ge(g_sem.gated, j + 1 + 6 * i)
            dve.tensor_tensor(G_PR[:, b, :], G_PR[:, b, :], u, ALU.mult).then_inc(g_sem.product, 1)

        def low(j, i=0):
            dve.wait_ge(g_sem.hi, j + 1 + 6 * i)
            dve.tensor_tensor(a_lo[:, KT + j % 3, :], G_PR[:, j % 3, :],
                              a_hi[:, KT + j % 3, :].bitcast(F32), ALU.subtract).then_inc(g_sem.lo, 1)

        gate(0)
        gate(1)
        low(0)
        gate(2)
        low(1)
        with dve.Fori(0, 3) as i:
            for j in range(1, 7):
                gate(j + 2, i)
                lo_of(dve, N_SGO + j + 5, i)
                low(j + 1, i)
        dve_at[0] = N_SGO + 24
        for j in range(19, SGT):
            if j + 2 < SGT:
                gate(j + 2)
            lo_to(dve, N_SGO + j + 5)
            if j + 1 < SGT:
                low(j + 1)

    def sgu_pool(pool):
        def affine(j):
            b, c, g = j % 3, C_LN + 2 * j + 1, j // 3
            if j >= 3:
                pool.wait_ge(g_sem.gated, j - 2)
            pool.tensor_tensor(G_AFF[:, b, :], G_R[:, g, :], cols[:, c:c + 1].to_broadcast([P, P]),
                               ALU.mult).then_inc(g_sem.affine, 1)
            pool.wait_ge(g_sem.affine, 2 * j + 1)
            pool.tensor_tensor(G_AFF[:, b, :], G_AFF[:, b, :], misc[:, M_BS + g * P:M_BS + (g + 1) * P],
                               ALU.add).then_inc(g_sem.affine, 1)

        pool.wait_ge(g_sem.rows_out, 1)
        for j in range(SGT):
            affine(j)

    DT_STEP, DT_SUMS = 2, 4
    S_X, S_B, S_F = cut(6144, TT, D), cut(8192, TT, 256), cut(8704, 4, SEQ)
    S_XD, S_XDD, S_ST = cut(9728, 2, 512), cut(10752, 512), cut(11264, 2, 512)
    S_E, S_LA, S_CB, S_T = cut(12288, 4, 512), cut(14336, 2, 512), cut(15360, 2, 2, P), cut(15872, 512)
    S_CV, S_SL = cut(12288, 2, SEQ), cut(12800, 2, SEQ)
    S_Z = cut(12288, TT, D)
    x_sem = signals("xbc", "copied conv silu turned moved")

    def xbc_dst(j):
        return S_SL[:, j % 2, :] if j < 8 else S_F[:, j - 8, :]

    def x_unit(j):
        return N_MIX + 2 * j

    def x_bank(j):
        return 4 + j % 2 if j else 0

    def mixer_in_pe(pe, pre, q):
        def turn(j):
            pe.wait_ge(x_sem.silu, j + 1)
            if j >= 2:
                pe.wait_ge(x_sem.moved, j - 1)
            for tt in range(TT):
                mm = pe.transpose(ps[:, 6 + j % 2, tt * P:(tt + 1) * P],
                                  xbc_dst(j)[:, tt * P:(tt + 1) * P], ident)
            mm.then_inc(x_sem.turned, 1)

        for j in range(XT):
            if j >= 2:
                pe.wait_ge(x_sem.copied, j - 1)
            features(pe, x_unit(j), ps[:, x_bank(j), 0:SEQ], pre=None if j else pre)
            if j == 0:
                dt_pe(pe)
            if 1 <= j < XT - 1:
                turn(j - 1)
            if j == DT_SUMS:
                dt_sums_pe(pe)
            if j < QKT:
                if j >= 2:
                    pe.wait_ge(q.qk, j - 1)
                features(pe, x_unit(j) + 1, ps[:, 2 + j % 2, 0:SEQ])
            else:
                if j == QKT:
                    pe.wait_ge(d_sem.decay, 1)
                tokens(pe, x_unit(j) + 1, [ps[:, 0, 0:256], ps[:, 1, 0:256]], 4 * (j - QKT), 4, 256)

    def mixer_in_act(act):
        def move(j):
            act.wait_ge(x_sem.turned, j + 1)
            dst = S_X[:, :, j * P:(j + 1) * P] if j < 8 else S_B[:, :, (j - 8) * P:(j - 7) * P]
            act.activation(dst, ps[:, 6 + j % 2, 0:SEQ].rearrange("p (a b) -> p a b", a=TT),
                           ACT.Copy).then_inc(x_sem.moved, 1)

        for j in range(XT):
            hi_to(act, x_unit(j) + 5)
            act.wait_ge(unit_used, x_unit(j) + 1)
            if j >= 2:
                act.wait_ge(x_sem.conv, 5 * (j - 1))
            act.activation(pad[:, j % 2, 2:2 + SEQ], ps[:, x_bank(j), 0:SEQ], ACT.Copy).then_inc(x_sem.copied, 1)
            if 2 <= j < XT:
                move(j - 2)
            hi_to(act, x_unit(j) + 6)
            if j == DT_STEP:
                dt_act(act)
            if j == DT_SUMS + 1:
                decay_act(act)
            act.wait_ge(x_sem.conv, 5 * j + 5)
            if 2 <= j < 8:
                act.wait_ge(x_sem.turned, j - 1)
            act.activation(xbc_dst(j), S_CV[:, j % 2, :], ACT.Silu).then_inc(x_sem.silu, 1)

    def mixer_in_dve(dve, q):
        for j in range(XT):
            lo_to(dve, x_unit(j) + 5)
            c = C_XBC + 6 * j
            b = j % 2
            dve.wait_ge(x_sem.copied, j + 1)
            if j >= 2:
                dve.wait_ge(x_sem.silu, j - 1)
            dve.tensor_scalar(S_CV[:, b, :], pad[:, b, 0:SEQ], cols[:, c:c + 1], cols[:, c + 5:c + 6],
                              ALU.mult, ALU.add).then_inc(x_sem.conv, 1)
            for k in range(1, 5):
                dve.wait_ge(x_sem.conv, 5 * j + k)
                dve.scalar_tensor_tensor(S_CV[:, b, :], pad[:, b, k:k + SEQ], cols[:, c + k:c + k + 1],
                                         S_CV[:, b, :], ALU.mult, ALU.add).then_inc(x_sem.conv, 1)
            lo_to(dve, x_unit(j) + 6)
            if j == DT_STEP:
                dt_dve(dve)
            if j < QKT:
                dve.wait_ge(unit_used, x_unit(j) + 2)
                dst = A_Q[:, j, :] if j < QT else A_K[:, j - QT, :]
                dve.tensor_scalar(dst, ps[:, 2 + j % 2, 0:SEQ], DH ** -0.5 if j < QT else 1.0, None,
                                  ALU.mult).then_inc(q.qk, 1)
        dve.wait_ge(unit_used, N_Z)
        dve.tensor_copy(A_V[:, :, :], ps[:, 0:2, 0:256]).then_inc(q.v, TT)

    dts = sb("dts", [P, 12, 64])
    ex = sb("ex", [P, 4, HEADS])
    ea = sb("ea", [P, 32])
    d_sem = signals("dt", "w_loaded w_hi w_lo product step exp ln a sums decay")
    V_A, V_NEG, V_E, V_U, V_L, V_D, V_EQ, V_D2, V_RD, V_T, V_DT, V_DA = range(12)

    def dt_pe(pe):
        pe.wait_ge(d_sem.w_lo, 1)
        for tt in range(TT):
            t = slice(tt * P, (tt + 1) * P)
            for k in range(KT):
                mm = three(pe, ps[:, 1, 32 * tt:32 * tt + 32], a_hi[:, k, t], a_lo[:, k, t],
                           wdt_hi[:, k, :], wdt_lo[:, k, :], k == 0, k == KT - 1)
        mm.then_inc(d_sem.product, 1)

    def dt_sums_pe(pe):
        pe.wait_ge(d_sem.step, 12)
        da = dts[:, V_DA, :].rearrange("p (a b) -> p a b", a=TT)
        for n, (m, c, d) in enumerate(((gt, 0, 0), (lt, 1, 1), (ge, 0, 1), (le, 1, 0))):
            mm = pe.matmul(ps[:, 1, 128 + 16 * n:144 + 16 * n], m, da[:, c, 16 * d:16 * d + 16],
                           start=True, stop=True)
        mm.then_inc(d_sem.sums, 1)

    def dt_act(act):
        act.wait_ge(d_sem.step, 2)
        act.activation(dts[:, V_E, :], dts[:, V_NEG, :], ACT.Exp).then_inc(d_sem.exp, 1)
        act.activation(ea[:, :], misc[:, M_ALOG:M_ALOG + 32], ACT.Exp).then_inc(d_sem.exp, 1)
        act.wait_ge(d_sem.step, 3)
        act.activation(dts[:, V_L, :], dts[:, V_U, :], ACT.Ln).then_inc(d_sem.ln, 1)

    def decay_act(act):
        act.wait_ge(d_sem.sums, 1)
        act.activation(ex[:, :, :].rearrange("p a b -> p (a b)"), ps[:, 1, 128:192], ACT.Exp).then_inc(d_sem.decay, 1)

    def dt_dve(dve):
        v = lambda k: dts[:, k, :]
        two = lambda k: v(k).rearrange("p (a b) -> p a b", a=TT)
        row32 = lambda t, o: t[:, o:o + 32].rearrange("p (a b) -> p a b", a=1).to_broadcast([P, TT, 32])
        step = [0]

        def then(ins):
            ins.then_inc(d_sem.step, 1)
            step[0] += 1
            dve.wait_ge(d_sem.step, step[0])

        dve.wait_ge(d_sem.product, 1)
        then(dve.tensor_tensor(two(V_A), ps[:, 1, 0:64].rearrange("p (a b) -> p a b", a=TT), row32(misc, M_DTB), ALU.add))
        then(dve.scalar_tensor_tensor(v(V_NEG), v(V_A), -1.0, v(V_A), ALU.mult, ALU.min))
        dve.wait_ge(d_sem.exp, 2)
        then(dve.tensor_scalar(v(V_U), v(V_E), 1.0, None, ALU.add))
        then(dve.tensor_scalar(v(V_D), v(V_U), 1.0, None, ALU.subtract))
        then(dve.tensor_scalar(v(V_EQ), v(V_U), 1.0, None, ALU.is_equal))
        then(dve.tensor_tensor(v(V_D2), v(V_D), v(V_EQ), ALU.add))
        then(dve.reciprocal(v(V_RD), v(V_D2)))
        then(dve.tensor_tensor(v(V_T), v(V_E), v(V_RD), ALU.mult))
        dve.wait_ge(d_sem.ln, 1)
        then(dve.tensor_tensor(v(V_D), v(V_L), v(V_EQ), ALU.add))
        then(dve.tensor_tensor(v(V_T), v(V_T), v(V_D), ALU.mult))
        then(dve.scalar_tensor_tensor(v(V_DT), v(V_A), 0.0, v(V_T), ALU.max, ALU.add))
        then(dve.scalar_tensor_tensor(two(V_DA), two(V_DT), -1.0, row32(ea, 0), ALU.mult, ALU.mult))

    s_sem = signals("ssd", "la diff exp m cb cb_out xd y xdd state state_out off t comb")

    def heads_bc(v, n, width):
        return v.rearrange("p (h a) -> p h a", a=1).to_broadcast([P, n, width])

    def ssd_pool(pool):
        pool.wait_ge(d_sem.step, 12)
        for b in range(16):
            k, q, d = b // 4, b // 2 % 2, b % 2
            g, c = k // 2, k % 2
            if b >= 2:
                pool.wait_ge(s_sem.diff, b - 1)
            o = 32 * c + 16 * d + 8 * g + 4 * q
            mask = (gt, lt)[d].rearrange("p (a b) -> p a b", a=1).to_broadcast([P, 4, P])
            pool.tensor_tensor(S_LA[:, b % 2, :].rearrange("p (h t) -> p h t", h=4), mask,
                               heads_bc(dts[:, V_DA, o:o + 4], 4, P), ALU.mult).then_inc(s_sem.la, 1)

    def ssd_pe(pe):
        def diff(b):
            pe.wait_ge(s_sem.la, b + 1)
            if b >= 2:
                pe.wait_ge(s_sem.exp, b - 1)
            for h in range(4):
                mm = pe.matmul(ps[:, 4 + b % 2, h * P:(h + 1) * P], S_LA[:, b % 2, h * P:(h + 1) * P],
                               (le, ge)[b % 2], start=True, stop=True)
            mm.then_inc(s_sem.diff, 1)

        def products(k):
            g, c = k // 2, k % 2
            t = slice(c * P, (c + 1) * P)
            if k >= 1:
                pe.wait_ge(s_sem.cb_out, 2 * k)
            pe.matmul(ps[:, 6, 0:P], S_F[:, g, t], S_F[:, 2 + g, t], start=True,
                      stop=True).then_inc(s_sem.cb, 1)

        def diagonal(j):
            k, q = j // 2, j % 2
            g, c = k // 2, k % 2
            pe.wait_ge(s_sem.m, 2 * j + 2)
            pe.wait_ge(s_sem.xd, 2 * k + 2)
            if g and q == 0:
                pe.wait_ge(s_sem.comb, 2)
            for h in range(4):
                o = (4 * q + h) * DH
                for d in range(2):
                    mm = pe.matmul(ps[:, c, o:o + DH], S_E[:, (2 * j + d) % 4, h * P:(h + 1) * P],
                                   S_XD[:, d, o:o + DH], start=(d == 0), stop=(d == 1))
            mm.then_inc(s_sem.y, 1)

        def state(k):
            g, c = k // 2, k % 2
            pe.wait_ge(s_sem.xdd, k + 1)
            if k >= 1:
                pe.wait_ge(s_sem.state_out, k)
            pe.matmul(ps[:, 7, :], S_B[:, c, g * P:(g + 1) * P], S_XDD, start=True,
                      stop=True).then_inc(s_sem.state, 1)

        def off(k):
            g, c = k // 2, k % 2
            pe.wait_ge(s_sem.state_out, k + 1)
            if g:
                pe.wait_ge(s_sem.comb, 2)
            pe.matmul(ps[:, 2 + (1 - c), :], S_F[:, 2 + g, (1 - c) * P:(2 - c) * P], S_ST[:, c, :],
                      start=True, stop=True).then_inc(s_sem.off, 1)

        pe.wait_ge(at2.v, TT)
        for k in range(4):
            products(k)
            diff(4 * k)
            diff(4 * k + 1)
            state(k)
            diff(4 * k + 2)
            diff(4 * k + 3)
            diagonal(2 * k)
            off(k)
            diagonal(2 * k + 1)

    def ssd_act(act):
        act.wait_ge(x_sem.silu, XT)
        for k in range(4):
            for b in range(4 * k, 4 * k + 4):
                act.wait_ge(s_sem.diff, b + 1)
                if b >= 4:
                    act.wait_ge(s_sem.y, b // 2 - 1)
                act.activation(S_E[:, b % 4, :], ps[:, 4 + b % 2, :], ACT.Exp).then_inc(s_sem.exp, 1)
                if b % 4 == 1:
                    act.wait_ge(s_sem.state, k + 1)
                    if k >= 2:
                        act.wait_ge(s_sem.off, k - 1)
                    act.activation(S_ST[:, k % 2, :], ps[:, 7, :], ACT.Copy).then_inc(s_sem.state_out, 1)

    def ssd_dve(dve):
        eight = lambda v: v.rearrange("p (h e) -> p h e", h=8)
        dve.wait_ge(d_sem.decay, 1)
        for k in range(4):
            g, c = k // 2, k % 2
            if k:
                dve.wait_ge(s_sem.y, 2 * k)
            for d in range(2):
                o = 32 * c + 16 * d + 8 * g
                dve.tensor_tensor(eight(S_XD[:, d, :]), eight(S_X[:, c, g * 512:(g + 1) * 512]),
                                  heads_bc(dts[:, V_DT, o:o + 8], 8, DH), ALU.mult).then_inc(s_sem.xd, 1)
            dve.wait_ge(s_sem.xd, 2 * k + 2)
            if k:
                dve.wait_ge(s_sem.state, k)
            dve.tensor_tensor(eight(S_XDD), eight(S_XD[:, c, :]), heads_bc(ex[:, c, 8 * g:8 * g + 8], 8, DH),
                              ALU.mult).then_inc(s_sem.xdd, 1)
            dve.wait_ge(s_sem.cb, k + 1)
            for d in range(2):
                dve.tensor_tensor(S_CB[:, k % 2, d, :], ps[:, 6, 0:P], (le, ge)[d], ALU.mult).then_inc(s_sem.cb_out, 1)
            dve.wait_ge(s_sem.cb_out, 2 * k + 2)
            for b in range(4 * k, 4 * k + 4):
                dve.wait_ge(s_sem.exp, b + 1)
                e = S_E[:, b % 4, :].rearrange("p (h t) -> p h t", h=4)
                dve.tensor_tensor(e, e, S_CB[:, k % 2, b % 2:b % 2 + 1, :].to_broadcast([P, 4, P]),
                                  ALU.mult).then_inc(s_sem.m, 1)
            if c == 0:
                continue
            dve.wait_ge(s_sem.off, k + 1)
            for cc in range(2):
                n = 2 * g + cc
                y = ybuf[:, cc, g * 512:(g + 1) * 512]
                dve.wait_ge(s_sem.y, 2 * n + 2)
                if n:
                    dve.wait_ge(s_sem.comb, n)
                dve.tensor_tensor(eight(S_T), eight(ps[:, 2 + cc, :]), heads_bc(ex[:, 2 + cc, 8 * g:8 * g + 8], 8, DH),
                                  ALU.mult).then_inc(s_sem.t, 1)
                dve.tensor_tensor(eight(y), eight(S_X[:, cc, g * 512:(g + 1) * 512]),
                                  heads_bc(misc[:, M_SKIP + 8 * g:M_SKIP + 8 * g + 8], 8, DH), ALU.mult).then_inc(s_sem.t, 1)
                dve.wait_ge(s_sem.t, 3 * n + 1)
                dve.tensor_tensor(S_T, S_T, ps[:, cc, :], ALU.add).then_inc(s_sem.t, 1)
                dve.wait_ge(s_sem.t, 3 * n + 3)
                dve.tensor_tensor(y, y, S_T, ALU.add).then_inc(s_sem.comb, 1)

    z_sem = signals("z", "silu gated")

    def z_pe(pe, c, k):
        tokens(pe, N_Z + 4 * c + k, [ps[:, 4 + 2 * c, :], ps[:, 5 + 2 * c, :]], 2 * k, 2, 512)

    def z_act(act, c):
        for tt in range(TT):
            act.wait_ge(unit_used, N_Z + 4 * c + 4)
            act.activation(S_Z[:, tt, c * 512:(c + 1) * 512], ps[:, 4 + 2 * c + tt, :],
                           ACT.Silu).then_inc(z_sem.silu, 1)

    def z_dve(dve):
        dve.wait_ge(z_sem.silu, 4)
        for tt in range(TT):
            dve.tensor_tensor(ybuf[:, tt, :], ybuf[:, tt, :], S_Z[:, tt, :], ALU.mult).then_inc(z_sem.gated, 1)

    def wo2(pe, k):
        if k >= KT:
            pe.wait_ge(at2.lo, (k - KT) // 2 + 1)
        accumulate(pe, N_WO2 + k, k, k == 0, k == 2 * KT - 1)

    def attn2_pe(pe):
        at = attn_pe(pe, at2, False)
        pe.wait_ge(s_sem.exp, 16)
        pe.wait_ge(s_sem.state_out, 4)
        pe.wait_ge(s_sem.cb_out, 8)
        pe.wait_ge(at2.qk, QKT)
        for g in range(3):
            for k in range(2):
                z_pe(pe, g // 2, 2 * (g % 2) + k)
            if g == 0:
                pe.wait_ge(s_sem.comb, 4)
            for r in range(REP):
                at.scores(g, r)
        z_pe(pe, 1, 2)
        z_pe(pe, 1, 3)
        pe.wait_ge(z_sem.silu, 4)
        at.turn(0)
        for h in range(HEADS):
            if h == 2 * REP:
                pe.wait_ge(at2.biased, HEADS)
                turn_pe(pe, mix, 0)
            if h == HEADS - REP - 1:
                pe.wait_ge(mix.lo, KT * (mix.n + 1))
            if h >= HEADS - REP - 1 and h < HEADS - 1:
                wo2(pe, h - (HEADS - REP - 1))
            if h + 1 < HEADS:
                at.turn(h + 1)
            at.values(h)
            if h < REP:
                at.scores(3, h)
        for k in range(REP, 2 * KT):
            wo2(pe, k)

    def attn2_act(act):
        at = attn_act(act, at2, False)
        hi_to(act, N_Z + 7)
        at.exponentials(0)
        z_act(act, 0)
        at.exponentials(1)
        z_act(act, 1)
        for h in range(REP):
            at.copy(h)
            if h:
                at.exponentials(2, ([0], [1], [2, 3])[h - 1])
        at.copy(4)
        at.high(0)
        at.copy(5)
        norm_squares(act, mix, lambda tt: ybuf[:, tt, :], lambda tt: (z_sem.gated, tt + 1), 8)
        at.copy(6)
        at.exponentials(3, [0])
        at.copy(7)
        at.exponentials(3, [1, 2, 3])
        at.high(1)
        norm_root(act, mix, 8)
        at.copy(8)
        at.copy(9)
        halves_act(act, mix, 6, 0, range(4))
        at.copy(10)
        halves_act(act, mix, 6, 0, range(4, KT))
        at.copy(11)
        hi_to(act, N_WO2 + 1)
        at.high(2)
        hi_to(act, N_WO2 + 3)
        for h in range(HEADS - REP, HEADS):
            at.copy(h)
            hi_to(act, N_WO2 + h - (HEADS - REP) + 4)
        at.high(3)

    def attn2_dve(dve):
        at = attn_dve(dve, at2, False, M_SINK2)
        at.maxima(0)
        lo_to(dve, N_Z + 7)
        at.maxima(1)
        at.divide(0)
        at.maxima(2)
        at.divide(1)
        z_dve(dve)
        at.divide(2)
        at.maxima(3)
        at.low(0)
        norm_mean(dve, mix, 8)
        at.low(1)
        at.divide(3)
        norm_inverse(dve, mix, 8)
        scale_dve(dve, mix, 8, ybuf)
        halves_dve(dve, mix, 6, 0)
        lo_to(dve, N_WO2 + 1)
        at.low(2)
        lo_to(dve, N_WO2 + 7)
        at.low(3)

    M_PR, M_RL = cut(3072, 3, SEQ), cut(3840, 3, SEQ)
    m_sem = signals("mlp", "relu square hi lo")

    def m_up(t):
        return N_MLP + 2 * t - 1 if t else N_MLP

    def m_down(t):
        return N_MLP + 2 * MT - 1 if t == MT - 1 else N_MLP + 2 + 2 * t

    def mlp_in_pe(pe, t, i=0):
        if t >= 3:
            pe.wait_ge(m_sem.relu, t - 2 + 3 * i)
        features(pe, m_up(t), ps[:, 4 + t % 3, 0:SEQ], i)

    def mlp_pe(pe, pre):
        features(pe, m_up(0), ps[:, 0, 0:SEQ], pre=pre)
        for t in (1, 2, 3, 4):
            mlp_in_pe(pe, t)
            pe.wait_ge(m_sem.lo, t)
            accumulate(pe, m_down(t - 1), KT + (t - 1) % 3, t == 1, False)
        with pe.Fori(0, (MT - 5) // 3) as i:
            for t in (5, 6, 7):
                mlp_in_pe(pe, t, i)
                pe.wait_ge(m_sem.lo, t + 3 * i)
                accumulate(pe, m_down(t - 1), KT + (t - 1) % 3, False, False, i)
        pe.wait_ge(m_sem.lo, MT)
        accumulate(pe, m_down(MT - 1), KT + (MT - 1) % 3, False, True)

    def mlp_act(act):
        def step(t, i, split):
            act.wait_ge(unit_used, m_up(t) + 1 + RING * i)
            if t >= 3:
                act.wait_ge(m_sem.square, t - 2 + 3 * i)
            act.activation(M_RL[:, t % 3, :], ps[:, 4 + t % 3 if t else 0, 0:SEQ], ACT.Relu).then_inc(m_sem.relu, 1)
            split(0)
            act.wait_ge(m_sem.square, t + 1 + 3 * i)
            if t >= 3:
                act.wait_ge(unit_used, m_down(t - 3) + 1 + RING * i)
            act.activation(a_hi[:, KT + t % 3, :], M_PR[:, t % 3, :], ACT.Copy).then_inc(m_sem.hi, 1)
            split(1)
        mlp_steps(act, step, hi_of, hi_to, act_at)

    def mlp_dve(dve):
        def step(t, i, split):
            dve.wait_ge(m_sem.relu, t + 1 + 3 * i)
            dve.tensor_tensor(M_PR[:, t % 3, :], M_RL[:, t % 3, :], M_RL[:, t % 3, :],
                              ALU.mult).then_inc(m_sem.square, 1)
            split(0)
            dve.wait_ge(m_sem.hi, t + 1 + 3 * i)
            dve.tensor_tensor(a_lo[:, KT + t % 3, :], M_PR[:, t % 3, :], a_hi[:, KT + t % 3, :].bitcast(F32),
                              ALU.subtract).then_inc(m_sem.lo, 1)
            split(1)
        mlp_steps(dve, step, lo_of, lo_to, dve_at)

    def mlp_steps(eng, step, half_of, half_to, at):
        half_to(eng, N_MLP + 5)
        step(0, 0, lambda j: half_to(eng, N_MLP + 6) if j == 0 else None)
        for t in range(1, 5):
            step(t, 0, lambda j, t=t: half_to(eng, m_up(t) + 6 + j))
        with eng.Fori(0, 8) as i:
            for t in (5, 6, 7):
                step(t, i, lambda j, t=t: half_of(eng, m_up(t) + 6 + j, i))
        at[0] = UNITS - 1
        for t in range(29, MT):
            step(t, 0, lambda j, t=t: half_to(eng, UNITS - 1))

    first, mix = Norm(0, *pre_sems), Norm(5, *pre_sems)
    updates = [update(n, Norm(k, *pre_sems)) for n, k in enumerate((1, 2, 3, 4, 6, 7))]
    ffn = [ffn_sems("ffn0"), ffn_sems("ffn1")]
    at1, at2 = attn_sems("attn1"), attn_sems("attn2")
    x_rows = x_in.rearrange("(t p) d -> p t d", p=P)

    with nc.Block() as block:

        @block.sync
        def _(sp):
            sp.dma_start(x[:], x_rows).then_inc(x_loaded, 16)
            for s in range(RING):
                sp.dma_start(raw[:, s, :], w[s]).then_inc(raw_loaded[s], 16)
                if s == 2:
                    sp.dma_start(misc[:], misc_in.to_broadcast([P, MISC])).then_inc(const_loaded, 16)
            sp.dma_start(tab[:, P:], tables_in[:, P:]).then_inc(const_loaded, 16)
            sp.dma_start(wdt[:], wdt_in).then_inc(const_loaded, 16)
            with sp.Fori(0, UNITS // RING - 1) as i:
                for s in range(RING):
                    sp.wait_ge(lo_done, s + 1 + RING * i)
                    sp.dma_start(raw[:, s, :], w[bass.ds(i * RING + RING + s, 1)].rearrange("a p n -> p (a n)")
                                 ).then_inc(raw_loaded[s], 16)
            sp.wait_ge(add_sems.added, 6 * TT)
            sp.dma_start(out.rearrange("(t p) d -> p t d", p=P), x[:]).then_inc(out_done, 16)
            sp.wait_ge(out_done, 16)

        @block.gpsimd
        def _(pool):
            def load_row(r):
                pool.dma_start(row[:, r % 2, :], rows_in[r:r + 1, :].to_broadcast([P, D])).then_inc(row_loaded[r % 2], 16)

            def updated(u):
                pool.wait_ge(add_sems.added, TT * (u + 1))

            pool.memset(pad[:], 0.0).then_inc(pad_ready, 1)
            load_row(0)
            load_row(1)
            pool.wait_ge(const_loaded, 48)
            pool.dma_start(G_WS, ws_in).then_inc(ws_loaded, 16)
            attn_pool(pool, at1, True)
            pool.wait_ge(ws_loaded, 16)
            pool.tensor_tensor(G_WS, G_WS, le.rearrange("p (a b) -> p a b", a=1).to_broadcast([P, GROUPS, P]),
                               ALU.mult).then_inc(g_sem.masked, 1)
            pool.wait_ge(updates[0].biased, TT)
            load_row(2)
            updated(0)
            load_row(3)
            updated(1)
            load_row(4)
            sgu_pool(pool)
            updated(2)
            load_row(5)
            updated(3)
            load_row(6)
            ssd_pool(pool)
            attn_pool(pool, at2, False)
            updated(4)

        @block.scalar
        def _(act):
            act.dma_start(ident, tables_in[:, T_ID:T_ID + P]).then_inc(ident_loaded, 16)
            act.dma_start(cols[:], cols_in).then_inc(cols_loaded, 16)
            norm_act(act, first, lambda tt: x[:, tt, :], lambda tt: (x_loaded, 16), 8)
            hi_to(act, 1)
            act.wait_ge(cols_loaded, 16)
            halves_act(act, first, 0)
            hi_to(act, 5)
            act.wait_ge(const_loaded, 48)
            act.activation(wdt_hi[:], wdt[:], ACT.Copy).then_inc(d_sem.w_hi, 1)
            attn1_act(act)
            hi_to(act, N_FFN0 - 1)
            update_act(act, updates[0], N_FFN0 - 1, 1, True)
            act.wait_ge(pad_ready, 1)
            ffn_act(act, ffn[0], N_FFN0)
            update_act(act, updates[1], N_SGV - 1, 2, False)
            sgu_act(act)
            update_act(act, updates[2], N_FFN1 - 1, 3, False)
            ffn_act(act, ffn[1], N_FFN1)
            update_act(act, updates[3], N_MIX - 1, 4, False)
            mixer_in_act(act)
            hi_to(act, N_Z + 5)
            ssd_act(act)
            attn2_act(act)
            hi_to(act, N_MLP - 1)
            update_act(act, updates[4], N_MLP - 1, 5, False)
            mlp_act(act)
            update_act(act, updates[5], UNITS - 1, None, False)

        @block.vector
        def _(dve):
            norm_dve(dve, first, 8)
            scale_dve(dve, first, 8, x)
            lo_to(dve, 1)
            dve.wait_ge(cols_loaded, 16)
            halves_dve(dve, first, 0)
            dve.wait_ge(const_loaded, 48)
            attn1_dve(dve)
            dve.wait_ge(d_sem.w_hi, 1)
            dve.tensor_tensor(wdt_lo[:], wdt[:], wdt_hi[:].bitcast(F32), ALU.subtract).then_inc(d_sem.w_lo, 1)
            lo_to(dve, N_FFN0 - 1)
            update_dve(dve, updates[0], N_FFN0 - 1, 1, 1, 0)
            ffn_dve(dve, ffn[0], N_FFN0, 0)
            update_dve(dve, updates[1], N_SGV - 1, 2, 2, None)
            sgu_dve(dve)
            update_dve(dve, updates[2], N_FFN1 - 1, 3, 3, None)
            ffn_dve(dve, ffn[1], N_FFN1, 1)
            update_dve(dve, updates[3], N_MIX - 1, 4, 4, None)
            mixer_in_dve(dve, at2)
            lo_to(dve, N_Z + 5)
            ssd_dve(dve)
            attn2_dve(dve)
            lo_to(dve, N_MLP - 1)
            update_dve(dve, updates[4], N_MLP - 1, 5, 5, None)
            mlp_dve(dve)
            update_dve(dve, updates[5], UNITS - 1, None, 6, None)

        @block.tensor
        def _(pe):
            pe.wait_ge(ident_loaded, 16)
            turn_pe(pe, first)

            attn1_pe(pe)
            turn_pe(pe, updates[0].pre)
            ffn_pe(pe, ffn[0], N_FFN0, updates[0].pre)
            turn_pe(pe, updates[1].pre)
            sgu_pe(pe, updates[1].pre)
            turn_pe(pe, updates[2].pre)
            ffn_pe(pe, ffn[1], N_FFN1, updates[2].pre)
            turn_pe(pe, updates[3].pre)
            mixer_in_pe(pe, updates[3].pre, at2)
            ssd_pe(pe)
            attn2_pe(pe)
            turn_pe(pe, updates[4].pre)
            mlp_pe(pe, updates[4].pre)


def head_order():
    order = []
    for t in range(QT):
        for half in range(2):
            h = REP * (2 * (t // REP) + half) + t % REP
            order += range(h * DH, (h + 1) * DH)
    return np.array(order)


def as_features(m):
    k, n = m.shape
    return m.reshape(KT, P, n // P, P).transpose(2, 1, 0, 3).reshape(n // P, P, KT * P)


def as_tokens(m, width):
    k, n = m.shape
    nk = UNIT // width
    v = m.reshape(KT // nk, nk, P, n // width, width).transpose(3, 0, 2, 1, 4)
    return v.reshape(-1, P, UNIT)


def as_rows(m):
    return m.reshape(-1, P, D)


def interleave(head, groups, tail):
    return np.concatenate([head, np.stack(groups, 1).reshape(-1, P, UNIT), tail])


def ffn_units(w_in, w_out):
    g, u, o = as_features(w_in[:, :FT * P]), as_features(w_in[:, FT * P:]), as_rows(w_out)
    return interleave(np.stack([g[0], u[0]]), [g[1:], u[1:], o[:-1]], o[-1:])


def qkv_units(q, k, v):
    return np.concatenate([as_features(q[:, head_order()]), as_features(k), as_tokens(v, 256)])


def tiles(v):
    return v.reshape(-1, P).T


def tables():
    p, f = np.arange(P)[:, None], np.arange(P)[None, :]
    masks = [p == f, p <= f, p > f, p >= f, p < f, p >= 0 * f]
    own = np.where(p >= f, p - f, FAR)
    before = np.where(f > p, p + P - f, FAR)
    near = []
    for b in range(TT):
        dist = np.abs(p + b * P - np.arange(SEQ)[None, :])
        near.append(np.where(dist <= P, dist, FAR))
    return np.concatenate([*masks, own, before, own, *near], 1).astype(np.float32)


def kernel(**inputs):
    from concourse import bacc
    from concourse.bass_utils import run_bass_kernel_spmd

    v = {k: np.asarray(a) for k, a in inputs.items()}
    arrays = layouts(v)
    nc = bacc.Bacc("TRN2", target_bir_lowering=False, num_devices=1)
    aps = {n: nc.dram_tensor("in_" + n, a.shape, F32, kind="ExternalInput").ap() for n, a in arrays.items()}
    out = nc.dram_tensor("out", (SEQ, D), F32, kind="ExternalOutput").ap()
    build(nc, *(aps[n] for n in ("w", "x", "cols", "misc", "tables", "rows", "ws", "wdt")), out)
    r = run_bass_kernel_spmd(nc, [{"in_" + n: a for n, a in arrays.items()}], core_ids=[0])
    return r.results[0]["out"].reshape(1, SEQ, D)


def layouts(v):
    order = head_order()
    qkv, win2 = v["attn_w_qkv"][0], v["w_in_2"][0]
    z, xbc, dt, q2, k2, v2 = np.split(win2, np.cumsum([D, XT * P, 32, QT * P, 256]), 1)
    wout2 = v["w_out_2"][0]
    up, down = as_features(v["w_up_2"][0]), as_rows(v["w_down_2"][0])
    w = np.concatenate([
        qkv_units(qkv[:, :D], qkv[:, D:D + 256], qkv[:, D + 256:])[QK_ORDER + [QKT, QKT + 1]],
        as_rows(v["attn_w_o"][0]),
        ffn_units(v["ffn_w_in"][0], v["ffn_w_out"][0]),
        as_tokens(v["sgu_w_in"][0][:, SG:], 512),
        as_features(v["sgu_w_in"][0][:, :SG]),
        as_rows(v["sgu_w_out"][0]),
        ffn_units(v["ffn_w_in"][1], v["ffn_w_out"][1]),
        np.stack([as_features(xbc), qkv_units(q2, k2, v2)], 1).reshape(-1, P, UNIT),
        as_tokens(z, 512),
        as_rows(wout2),
        interleave(up[:1], [up[1:], down[:-1]], down[-1:]),
    ])
    bq = v["attn_b_qkv"][0]
    gains = [v["norm_mix_pre"][0], v["norm_ffn_pre"][0], v["norm_mix_pre"][1], v["norm_ffn_pre"][1],
             v["norm_mix_pre_2"][0], v["norm_mlp_pre_2"][0], v["ssm_norm_2"][0]]
    conv = np.concatenate([v["ffn_conv_w"], v["ffn_conv_b"][:, None]], 1)
    conv = conv.reshape(2, 4, FT, P).transpose(3, 0, 2, 1).reshape(P, -1)
    xc = np.concatenate([v["conv_w_2"][0], v["conv_b_2"]], 0).reshape(6, XT, P).transpose(2, 1, 0).reshape(P, -1)
    ln = np.stack([v["sgu_ln_g"][0], v["sgu_ln_b"][0]]).reshape(2, SGT, P).transpose(2, 1, 0).reshape(P, -1)
    bqk = np.concatenate([tiles(bq[:D][order]), tiles(bq[D:D + 256])], 1)[:, QK_ORDER]
    cols = np.concatenate([*(tiles(g) for g in gains), bqk, conv, xc, ln], 1)
    misc = np.concatenate([v["attn_sinks"][0], v["attn_sink_2"][0], bq[D + 256:], v["dt_bias_2"].ravel(),
                           v["a_log_2"].ravel(), v["d_skip_2"].ravel(), v["sgu_b_s"].ravel()])[None]
    rows = np.stack([v["attn_b_o"][0], v["norm_mix_post"][0], v["norm_ffn_post"][0], v["norm_mix_post"][1],
                     v["norm_ffn_post"][1], v["norm_mix_post_2"][0], v["norm_mlp_post_2"][0]])
    ws = v["sgu_w_s"][0].transpose(2, 0, 1)
    wdt = dt.reshape(KT, P, 32).transpose(1, 0, 2)
    arrays = dict(w=w, x=v["x"][0], cols=cols, misc=misc, tables=tables(), rows=rows, ws=ws, wdt=wdt)
    return {k: np.ascontiguousarray(a) for k, a in arrays.items()}
```

```python
import math
from collections import namedtuple

import concourse.bass as bass
import numpy as np
from concourse import mybir

F32 = mybir.dt.float32
F32R = mybir.dt.float32r
ACT = mybir.ActivationFunctionType
ALU = mybir.AluOpType
AX = mybir.AxisListType

P = 128
SEQ = 256
TT = SEQ // P
D = 1024
KT = D // P
EPS = 1e-6

HEADS, KV_HEADS, DH = 16, 4, 64
REP = HEADS // KV_HEADS
QT = HEADS * DH // P
KVT = KV_HEADS * DH // P
QKT = QT + KVT
QK_ORDER = [t for g in range(KVT) for t in (QT + g, *range(REP * g, REP * g + REP))]
SLOPE = [2.0 ** (-8.0 * (h + 1) / HEADS) for h in range(HEADS)]

FT = 2816 // P
SG = 3072
SGT = SG // P
SGC = SG // 512
GROUPS = 8
XT = 1536 // P
MT = 4096 // P

RING = 6
WARM_SQUARES, WARM_FACTORS, WARM_ADDED, WARM_SQUARES2, WARM_FIRST = 4, 4, 5, 3, 2
UNIT = 1024

N_QKV1 = 0
N_WO1 = N_QKV1 + QT + KVT + 2
N_FFN0 = N_WO1 + KT
N_SGV = N_FFN0 + 3 * FT
N_SGU = N_SGV + 4 * SGC
N_SGO = N_SGU + SGT
N_FFN1 = N_SGO + SGT
N_MIX = N_FFN1 + 3 * FT
N_Z = N_MIX + XT + QT + KVT + 2
N_WO2 = N_Z + KT
N_MLP = N_WO2 + 2 * KT
UNITS = N_MLP + 2 * MT
assert UNITS % RING == 0

C_GAIN = 0
C_BQK = C_GAIN + 7 * KT
C_CONV = C_BQK + QT + KVT
C_XBC = C_CONV + 2 * FT * 4
C_LN = C_XBC + XT * 6
COLS = C_LN + SGT * 2

M_SINK1, M_SINK2, M_BV, M_DTB, M_ALOG, M_SKIP, M_BS, MISC = np.cumsum(
    [0, HEADS, HEADS, KV_HEADS * DH, 2 * HEADS, 2 * HEADS, HEADS, GROUPS * P]).tolist()

T_ID, T_LE, T_GT, T_GE, T_LT, T_ONE, T_D1, T_D2, TABLES = np.cumsum(
    [0, P, P, P, P, P, P, 3 * P, 4 * P]).tolist()
FAR = 1e30


def build(nc, w, x_in, cols_in, misc_in, tables_in, rows_in, ws_in, wdt_in, out):
    def sb(name, shape, dt=F32):
        return nc.alloc_sbuf_tensor(name, shape, dt)

    def sem(name):
        return nc.alloc_semaphore(name)

    def signals(prefix, names):
        return namedtuple(prefix, names)(*(sem(f"{prefix}_{name}") for name in names.split()))

    raw = sb("raw", [P, RING, UNIT])
    w_hi = sb("w_hi", [P, RING, UNIT], F32R)
    w_lo = sb("w_lo", [P, RING, UNIT], F32R)
    x = sb("x", [P, TT, D])
    a_hi = sb("a_hi", [P, 2 * KT, SEQ], F32R)
    a_lo = sb("a_lo", [P, 2 * KT, SEQ], F32R)
    cols = sb("cols", [P, COLS])
    misc = sb("misc", [P, MISC])
    tab = sb("tab", [P, TABLES])
    row = sb("row", [P, 2, D])
    wdt = sb("wdt", [P, KT, 32])
    wdt_hi = sb("wdt_hi", [P, KT, 32], F32R)
    wdt_lo = sb("wdt_lo", [P, KT, 32], F32R)
    st = sb("st", [P, 96])
    pad = sb("pad", [P, 2, SEQ + 4])
    arena = sb("arena", [P, 16640])
    ps = nc.alloc_psum_tensor("ps", [P, 8, 512], F32)

    def cut(at, *shape):
        n = math.prod(shape)
        assert at + n <= 16640
        v = arena[:, at:at + n]
        if len(shape) == 1:
            return v
        names = "abcd"[:len(shape)]
        return v.rearrange(f"p ({' '.join(names)}) -> p {' '.join(names)}",
                           **{k: s for k, s in zip(names[1:], shape[1:])})

    ident, le, gt, ge, lt, one = (tab[:, o:o + P] for o in (T_ID, T_LE, T_GT, T_GE, T_LT, T_ONE))
    ybuf = cut(0, TT, D)
    junk = cut(2048, D)

    raw_loaded = [sem(f"raw_loaded{s}") for s in range(RING)]
    hi_done = sem("hi_done")
    lo_done = sem("lo_done")
    unit_used = sem("unit_used")
    x_loaded = [sem("x_loaded0"), sem("x_loaded1")]
    ident_loaded, cols_loaded = sem("ident_loaded"), sem("cols_loaded")
    early_loaded, late_loaded, ws_loaded = sem("early_loaded"), sem("late_loaded"), sem("ws_loaded")
    row_loaded = [sem("row_loaded0"), sem("row_loaded1")]
    out_done, pad_ready = sem("out_done"), sem("pad_ready")

    def hi_of(act, n, i=0):
        s = n % RING
        act.wait_ge(raw_loaded[s], 16 * (n // RING + 1) + 16 * i)
        if n >= RING:
            act.wait_ge(unit_used, n - RING + 1 + RING * i)
        act.activation(w_hi[:, s, :], raw[:, s, :], ACT.Copy).then_inc(hi_done, 1)

    def lo_of(dve, n, i=0):
        s = n % RING
        dve.wait_ge(hi_done, n + 1 + RING * i)
        dve.tensor_tensor(w_lo[:, s, :], raw[:, s, :], w_hi[:, s, :].bitcast(F32),
                          ALU.subtract).then_inc(lo_done, 1)

    act_at, dve_at = [0], [0]

    def hi_to(act, n):
        while act_at[0] <= min(n, UNITS - 1):
            hi_of(act, act_at[0])
            act_at[0] += 1

    def lo_to(dve, n):
        while dve_at[0] <= min(n, UNITS - 1):
            lo_of(dve, dve_at[0])
            dve_at[0] += 1

    def three(pe, o, l_hi, l_lo, r_hi, r_lo, first, last):
        pe.matmul(o, l_hi, r_hi, start=first, stop=False)
        pe.matmul(o, l_hi, r_lo, start=False, stop=False)
        return pe.matmul(o, l_lo, r_hi, start=False, stop=last)

    def features(pe, n, o, i=0, pre=None):
        s = n % RING
        pe.wait_ge(lo_done, n + 1 + RING * i)
        for k in range(KT):
            if pre is not None:
                pe.wait_ge(pre.lo, KT * pre.n + k + 1)
            c = slice(k * P, (k + 1) * P)
            mm = three(pe, o, w_hi[:, s, c], w_lo[:, s, c], a_hi[:, k, :], a_lo[:, k, :],
                       k == 0, k == KT - 1)
        mm.then_inc(unit_used, 1)

    def tokens(pe, n, o, k0, nk, width, i=0, pre=None):
        s = n % RING
        pe.wait_ge(lo_done, n + 1 + RING * i)
        for k in range(nk):
            if pre is not None:
                pe.wait_ge(pre.lo, KT * pre.n + k0 + k + 1)
            c = slice(k * width, (k + 1) * width)
            for tt in range(TT):
                t = slice(tt * P, (tt + 1) * P)
                mm = three(pe, o[tt], a_hi[:, k0 + k, t], a_lo[:, k0 + k, t],
                           w_hi[:, s, c], w_lo[:, s, c], k0 + k == 0, k0 + k == KT - 1)
        mm.then_inc(unit_used, 1)

    def accumulate(pe, n, slot, first, last, i=0):
        s = n % RING
        pe.wait_ge(lo_done, n + 1 + RING * i)
        for tt in range(TT):
            t = slice(tt * P, (tt + 1) * P)
            for a, b, f, z in ((a_hi, w_hi, first, False), (a_hi, w_lo, False, False),
                               (a_lo, w_hi, False, last)):
                for c in range(2):
                    mm = pe.matmul(ps[:, 2 * tt + c, :], a[:, slot, t],
                                   b[:, s, c * 512:(c + 1) * 512], start=f, stop=z)
        mm.then_inc(unit_used, 1)

    pre_sems = signals("pre", "sum mean root inv scaled turned hi lo")
    post_sems = signals("post", "sum mean root inv scaled turned hi lo")
    add_sems = signals("update", "biased term added")

    Norm = namedtuple("Norm", "n sum mean root inv scaled turned hi lo")
    Update = namedtuple("Update", "n post pre biased term added")

    def turn_pe(pe, q, base=4):
        for k in range(KT):
            if k % 4 == 0:
                pe.wait_ge(q.scaled, 2 * TT * q.n + TT * (k // 4 + 1))
            for tt in range(TT):
                mm = pe.transpose(turned(k, base)[:, tt * P:(tt + 1) * P], ybuf[:, tt, k * P:(k + 1) * P], ident)
            if k % 2:
                mm.then_inc(q.turned, 1)

    def keep_warm(pe, products, *after):
        pe.wait_ge(*after)
        for _ in range(products):
            pe.matmul(ps[:, 7, 0:P], ident, ident, start=True, stop=True)

    def keep_warm_update(pe, u):
        for tt in range(TT):
            keep_warm(pe, WARM_SQUARES, u.post.sum, TT * u.n + tt + 1)
        keep_warm(pe, WARM_FACTORS, u.post.inv, u.n + 1)
        for tt in range(TT):
            keep_warm(pe, WARM_ADDED, u.added, TT * u.n + tt + 1)
        for tt in range(TT):
            keep_warm(pe, WARM_SQUARES2, u.pre.sum, TT * u.pre.n + tt + 1)

    def norm_squares(act, q, view, done, c0):
        for tt in range(TT):
            act.wait_ge(*done(tt))
            if tt:
                act.wait_ge(q.sum, TT * q.n + tt)
            act.activation(junk[:, :], view(tt), ACT.Square,
                           accum_out=st[:, c0 + tt:c0 + tt + 1]).then_inc(q.sum, 1)

    def norm_root(act, q, c0):
        act.wait_ge(q.mean, q.n + 1)
        act.activation(st[:, c0 + 4:c0 + 6], st[:, c0 + 2:c0 + 4], ACT.Sqrt).then_inc(q.root, 1)

    def norm_act(act, q, view, done, c0):
        norm_squares(act, q, view, done, c0)
        norm_root(act, q, c0)

    def norm_mean(dve, q, c0):
        dve.wait_ge(q.sum, TT * (q.n + 1))
        dve.tensor_scalar(st[:, c0 + 2:c0 + 4], st[:, c0:c0 + 2], 1.0 / D, EPS,
                          ALU.mult, ALU.add).then_inc(q.mean, 1)

    def norm_inverse(dve, q, c0):
        dve.wait_ge(q.root, q.n + 1)
        dve.reciprocal(st[:, c0 + 6:c0 + 8], st[:, c0 + 4:c0 + 6]).then_inc(q.inv, 1)
        dve.wait_ge(q.inv, q.n + 1)

    def norm_dve(dve, q, c0):
        norm_mean(dve, q, c0)
        norm_inverse(dve, q, c0)

    def scale_dve(dve, q, c0, src):
        for h in range(2):
            c = slice(h * D // 2, (h + 1) * D // 2)
            for tt in range(TT):
                dve.tensor_scalar(ybuf[:, tt, c], src[:, tt, c], st[:, c0 + 6 + tt:c0 + 7 + tt], None,
                                  ALU.mult).then_inc(q.scaled, 1)

    def turned(k, base=4):
        return ps[:, base + k // 2, (k % 2) * SEQ:(k % 2 + 1) * SEQ]

    def gain(g, k):
        return cols[:, C_GAIN + g * KT + k:C_GAIN + g * KT + k + 1]

    def halves_act(act, q, g, base=4, tiles=range(KT)):
        for k in tiles:
            act.wait_ge(q.turned, KT // 2 * q.n + k // 2 + 1)
            act.activation(a_hi[:, k, :], turned(k, base), ACT.Copy, scale=gain(g, k)).then_inc(q.hi, 1)

    def halves_dve(dve, q, g, base=4):
        for k in range(KT):
            dve.wait_ge(q.hi, KT * q.n + k // 2 * 2 + 2)
            dve.scalar_tensor_tensor(a_lo[:, k, :], turned(k, base), gain(g, k),
                                     a_hi[:, k, :].bitcast(F32), ALU.mult,
                                     ALU.subtract).then_inc(q.lo, 1)

    def update(n, pre):
        return Update(n, Norm(n, *post_sems), pre, *add_sems)

    acc = [ps[:, 2 * tt:2 * tt + 2, :].rearrange("p a b -> p (a b)") for tt in range(TT)]

    def update_act(act, u, n_last, g, bias, following):
        hi_to(act, n_last + RING - 1)
        act.preload_act_table(ACT.Sqrt)
        if bias:
            norm_act(act, u.post, lambda tt: ybuf[:, tt, :], lambda tt: (u.biased, tt + 1), 0)
        else:
            norm_act(act, u.post, lambda tt: acc[tt],
                     lambda tt: (u.term, TT * u.n + 1) if tt else (unit_used, n_last + 1), 0)
        if g is None:
            return
        norm_act(act, u.pre, lambda tt: x[:, tt, :], lambda tt: (u.added, TT * u.n + tt + 1), 8)
        act.preload_act_table(following)
        halves_act(act, u.pre, g)

    def update_dve(dve, u, n_last, g, r, bias):
        lo_to(dve, n_last + RING - 1)
        dve.wait_ge(row_loaded[r % 2], 16 * (r // 2 + 1))
        dve.wait_ge(unit_used, n_last + 1)
        if bias is not None:
            dve.wait_ge(row_loaded[bias % 2], 16 * (bias // 2 + 1))
            for tt in range(TT):
                dve.tensor_tensor(ybuf[:, tt, :], acc[tt], row[:, bias % 2, :],
                                  ALU.add).then_inc(u.biased, 1)
            for tt in range(TT):
                dve.wait_ge(u.post.sum, TT * u.n + tt + 1)
                dve.tensor_tensor(ybuf[:, tt, :], ybuf[:, tt, :], row[:, r % 2, :],
                                  ALU.mult).then_inc(u.term, 1)
        else:
            for n, tt in enumerate((1, 0)):
                if n:
                    dve.wait_ge(u.post.sum, TT * u.n + 1)
                dve.tensor_tensor(ybuf[:, tt, :], acc[tt], row[:, r % 2, :], ALU.mult).then_inc(u.term, 1)
        norm_dve(dve, u.post, 0)
        dve.wait_ge(u.term, TT * (u.n + 1))
        for tt in range(TT):
            dve.scalar_tensor_tensor(x[:, tt, :], ybuf[:, tt, :], st[:, 6 + tt:7 + tt], x[:, tt, :],
                                     ALU.mult, ALU.add).then_inc(u.added, 1)
        dve.wait_ge(u.added, TT * (u.n + 1))
        if g is None:
            return
        norm_dve(dve, u.pre, 8)
        scale_dve(dve, u.pre, 8, x)
        halves_dve(dve, u.pre, g)

    F_CV, F_GL, F_PR = cut(3072, 2, SEQ), cut(3584, 2, SEQ), cut(4096, 2, SEQ)

    def ffn_sems(name):
        return signals(name, "copied conv gelu product hi lo")

    def f_g(n0, t):
        return n0 + 3 * t - 1 if t else n0

    def f_out(n0, t):
        return n0 + 3 * FT - 1 if t == FT - 1 else n0 + 4 + 3 * t

    def ffn_in_pe(pe, f, n0, t, i=0, first=False):
        b = t % 2
        if not first:
            pe.wait_ge(f.product, t - 1 + 2 * i)
        features(pe, f_g(n0, t), ps[:, 4 + b, 0:SEQ], i)
        features(pe, f_g(n0, t) + 1, ps[:, 6 + b, 0:SEQ], i)

    def f_banks(t, i):
        return (0, 1) if t == 0 and isinstance(i, int) else (4 + t % 2, 6 + t % 2)

    def ffn_pe(pe, f, n0, pre):
        for n in range(2):
            features(pe, n0 + n, ps[:, n, 0:SEQ], pre=pre)
        ffn_in_pe(pe, f, n0, 1, first=True)
        pe.wait_ge(f.lo, 1)
        accumulate(pe, f_out(n0, 0), KT, True, False)
        with pe.Fori(0, (FT - 2) // 2) as i:
            for t in (2, 3):
                ffn_in_pe(pe, f, n0, t, i)
                pe.wait_ge(f.lo, t + 2 * i)
                accumulate(pe, f_out(n0, t - 1), KT + (t - 1) % 2, False, False, i)
        pe.wait_ge(f.lo, FT)
        accumulate(pe, f_out(n0, FT - 1), KT + (FT - 1) % 2, False, True)

    def ffn_act_step(act, f, n0, t, i, split):
        b = t % 2
        act.wait_ge(unit_used, f_g(n0, t) + 1 + RING * i)
        if t >= 2:
            act.wait_ge(f.conv, 3 * t - 3 + 6 * i)
        act.activation(pad[:, b, 2:2 + SEQ], ps[:, f_banks(t, i)[0], 0:SEQ], ACT.Copy).then_inc(f.copied, 1)
        split(0)
        act.wait_ge(f.conv, 3 * t + 3 + 6 * i)
        if t >= 2:
            act.wait_ge(f.product, t - 1 + 2 * i)
        act.activation(F_GL[:, b, :], F_CV[:, b, :], ACT.Gelu_apprx_tanh).then_inc(f.gelu, 1)
        split(1)
        act.wait_ge(f.product, t + 1 + 2 * i)
        if t >= 2:
            act.wait_ge(unit_used, f_out(n0, t - 2) + 1 + RING * i)
        act.activation(a_hi[:, KT + b, :], F_PR[:, b, :], ACT.Copy).then_inc(f.hi, 1)
        split(2)

    def ffn_dve_step(dve, f, n0, layer, t, i, split):
        b = t % 2
        c = C_CONV + (layer * FT + t) * 4

        def col(k):
            return cols[:, bass.ds(c + k + 8 * i, 1)] if not isinstance(i, int) else cols[:, c + k:c + k + 1]

        dve.wait_ge(f.copied, t + 1 + 2 * i)
        if t >= 2:
            dve.wait_ge(f.gelu, t - 1 + 2 * i)
        dve.tensor_scalar(F_CV[:, b, :], pad[:, b, 0:SEQ], col(0), col(3), ALU.mult,
                          ALU.add).then_inc(f.conv, 1)
        for k in (1, 2):
            dve.wait_ge(f.conv, 3 * t + k + 6 * i)
            dve.scalar_tensor_tensor(F_CV[:, b, :], pad[:, b, k:k + SEQ], col(k), F_CV[:, b, :],
                                     ALU.mult, ALU.add).then_inc(f.conv, 1)
        split(0)
        split(1)
        dve.wait_ge(f.gelu, t + 1 + 2 * i)
        dve.wait_ge(unit_used, f_g(n0, t) + 2 + RING * i)
        dve.tensor_tensor(F_PR[:, b, :], F_GL[:, b, :], ps[:, f_banks(t, i)[1], 0:SEQ],
                          ALU.mult).then_inc(f.product, 1)
        dve.wait_ge(f.hi, t + 1 + 2 * i)
        dve.tensor_tensor(a_lo[:, KT + b, :], F_PR[:, b, :], a_hi[:, KT + b, :].bitcast(F32),
                          ALU.subtract).then_inc(f.lo, 1)
        split(2)

    def ffn_run(eng, step, half_of, half_to, at, n0):
        half_to(eng, n0 + 5)
        step(0, 0, lambda j: half_to(eng, n0 + 6 + min(j, 1)))
        step(1, 0, lambda j: half_to(eng, n0 + 8 + j))
        with eng.Fori(0, (FT - 2) // 2) as i:
            for t in (2, 3):
                step(t, i, lambda j, t=t: half_of(eng, f_g(n0, t) + 6 + j, i))
        at[0] = n0 + 8 + 3 * (FT - 1)

    def ffn_act(act, f, n0):
        ffn_run(act, lambda t, i, s: ffn_act_step(act, f, n0, t, i, s), hi_of, hi_to, act_at, n0)

    def ffn_dve(dve, f, n0, layer):
        ffn_run(dve, lambda t, i, s: ffn_dve_step(dve, f, n0, layer, t, i, s), lo_of, lo_to, dve_at, n0)

    A_Q, A_K, A_V = cut(3072, QT, SEQ), cut(5120, KVT, SEQ), cut(5632, TT, KV_HEADS * DH)

    def qk_bank(j):
        return 4 + j % 4 if j else 0

    def qk1_pe(pe, j, pre=None):
        if j >= 4:
            pe.wait_ge(at1.qk, j - 3)
        features(pe, N_QKV1 + j, ps[:, qk_bank(j), 0:SEQ], pre=pre)

    def v1_pe(pe):
        pe.wait_ge(at1.qk, QKT - 2)
        for h in range(2):
            tokens(pe, N_QKV1 + QKT + h, [ps[:, 6, 0:256], ps[:, 7, 0:256]], 4 * h, 4, 256)

    def qk1_dve(dve, j):
        dve.wait_ge(unit_used, N_QKV1 + j + 1)
        is_k, g = j % (1 + REP) == 0, j // (1 + REP)
        dst = A_K[:, g, :] if is_k else A_Q[:, j - 1 - g, :]
        dve.tensor_scalar(dst, ps[:, qk_bank(j), 0:SEQ], cols[:, C_BQK + j:C_BQK + j + 1],
                          1.0 if is_k else DH ** -0.5, ALU.add, ALU.mult).then_inc(at1.qk, 1)

    def v1_dve(dve):
        dve.wait_ge(unit_used, N_QKV1 + QKT + 2)
        for tt in range(TT):
            dve.tensor_tensor(A_V[:, tt, :], ps[:, 6 + tt, 0:256], misc[:, M_BV:M_BV + 256],
                              ALU.add).then_inc(at1.v, 1)

    A_S, A_PT = cut(6144, 3, REP, 512), cut(14336, 2, 512)

    def attn_plan(first):
        seen = [[0], [0, 1]] if first else [[0, 1], [0, 1]]
        at, off = [], 0
        for keys in seen:
            at.append(off)
            off += P * len(keys)
        return seen, at, off

    def attn_sems(name):
        return signals(name, "qk v scores biased stat exp den norm0 norm1 turned copied out hi lo")

    AttnPe = namedtuple("AttnPe", "scores turn values")
    AttnAct = namedtuple("AttnAct", "exponentials copy high")
    AttnDve = namedtuple("AttnDve", "maxima divide low")

    def attn_pe(pe, q, first):
        seen, at, width = attn_plan(first)

        def scores(g, r):
            half = slice(64 * (g % 2), 64 * (g % 2) + 64)
            if g >= 1:
                pe.wait_ge(q.biased, REP * (g - 1) + r + 1)
            for b in range(TT):
                keys = seen[b]
                mm = pe.matmul(ps[:, r, at[b]:at[b] + P * len(keys)],
                               A_Q[half, REP * (g // 2) + r, b * P:(b + 1) * P],
                               A_K[half, g // 2, keys[0] * P:(keys[-1] + 1) * P],
                               start=True, stop=True)
            mm.then_inc(q.scores, 1)

        def turn(h):
            g, r = h // REP, h % REP
            pe.wait_ge(q.norm0, g + 1)
            pe.wait_ge(q.norm1, g + 1)
            if h >= 2:
                pe.wait_ge(q.copied, h - 1)
            for j in range(width // P):
                mm = pe.transpose(ps[:, 4 + h % 2, j * P:(j + 1) * P],
                                  A_S[:, g % 3, r, j * P:(j + 1) * P], ident)
            mm.then_inc(q.turned, 1)

        def values(h):
            g, r = h // REP, h % REP
            half = slice(64 * (r % 2), 64 * (r % 2) + 64)
            pe.wait_ge(q.copied, h + 1)
            if g >= 2 and r == 0:
                pe.wait_ge(q.lo, g - 1)
            for b in range(TT):
                o = (r // 2) * SEQ + b * P
                for j, kb in enumerate(seen[b]):
                    c = at[b] + j * P
                    mm = pe.matmul(ps[half, 6 + g % 2, o:o + P], A_V[:, kb, g * DH:(g + 1) * DH],
                                   A_PT[:, h % 2, c:c + P], start=(j == 0), stop=(j == len(seen[b]) - 1))
            if r == REP - 1:
                mm.then_inc(q.out, 1)

        return AttnPe(scores, turn, values)

    stq = sb("stq", [P, 2, 7, 2 * REP])

    def attn_act(act, q, first):
        seen, at, width = attn_plan(first)

        def exponentials(g, heads=range(REP)):
            if heads[0] == 0:
                act.wait_ge(q.stat, 5 * g + 5)
                if g >= 2:
                    act.wait_ge(q.den, 2 * g - 3)
                act.activation(stq[:, g % 2, 3, :], stq[:, g % 2, 2, :], ACT.Exp).then_inc(q.exp, 1)
            for r in heads:
                for b in range(TT):
                    s = A_S[:, g % 3, r, at[b]:at[b] + P * len(seen[b])]
                    k = b * REP + r
                    act.activation(s, s, ACT.Exp, bias=stq[:, g % 2, 1, k:k + 1],
                                   accum_out=stq[:, g % 2, 4, k:k + 1]).then_inc(q.exp, 1)

        def copy(h):
            act.wait_ge(q.turned, h + 1)
            act.activation(A_PT[:, h % 2, 0:width], ps[:, 4 + h % 2, 0:width],
                           ACT.Copy).then_inc(q.copied, 1)

        def high(g):
            act.wait_ge(q.out, g + 1)
            t = KT + 2 * g
            act.activation(a_hi[:, t:t + 2, :].rearrange("p a b -> p (a b)"), ps[:, 6 + g % 2, :],
                           ACT.Copy).then_inc(q.hi, 1)

        return AttnAct(exponentials, copy, high)

    def attn_normalise(eng, q, first, g, b, done):
        seen, at, width = attn_plan(first)
        s = A_S[:, g % 3, :, at[b]:at[b] + P * len(seen[b])]
        inv = stq[:, g % 2, 6, b * REP:(b + 1) * REP].rearrange("p (r a) -> p r a", a=1)
        eng.wait_ge(q.den, 2 * g + 2)
        eng.tensor_tensor(s, s, inv.to_broadcast([P, REP, P * len(seen[b])]), ALU.mult).then_inc(done, 1)

    def attn_pool(pool, q, first, batches=range(KV_HEADS)):
        for g in batches:
            attn_normalise(pool, q, first, g, 1, q.norm1)

    def attn_dve(dve, q, first, m_sink):
        seen, at, width = attn_plan(first)
        dist = tab[:, T_D1:T_D1 + width] if first else tab[:, T_D2:T_D2 + width]

        def maxima(g):
            if g >= 3:
                dve.wait_ge(q.turned, REP * (g - 2))
            if g >= 2:
                dve.wait_ge(q.exp, 9 * (g - 1))
            stat = lambda k: stq[:, g % 2, k, :]
            for r in range(REP):
                h = REP * g + r
                dve.wait_ge(q.scores, h + 1)
                dve.scalar_tensor_tensor(A_S[:, g % 3, r, 0:width], dist, -SLOPE[h],
                                         ps[:, r, 0:width], ALU.mult, ALU.add).then_inc(q.biased, 1)
            dve.wait_ge(q.biased, REP * (g + 1))
            for b in range(TT):
                dve.tensor_reduce(stat(0)[:, b * REP:(b + 1) * REP],
                                  A_S[:, g % 3, :, at[b]:at[b] + P * len(seen[b])],
                                  AX.X, ALU.max).then_inc(q.stat, 1)
            dve.wait_ge(q.stat, 5 * g + 2)
            sink = misc[:, m_sink + REP * g:m_sink + REP * (g + 1)]
            both = sink.rearrange("p (a r) -> p a r", a=1).to_broadcast([P, TT, REP])
            two = lambda k: stat(k).rearrange("p (b r) -> p b r", b=TT)
            dve.tensor_tensor(two(0), two(0), both, ALU.max).then_inc(q.stat, 1)
            dve.wait_ge(q.stat, 5 * g + 3)
            dve.tensor_scalar(stat(1), stat(0), -1.0, None, ALU.mult).then_inc(q.stat, 1)
            dve.tensor_tensor(two(2), both, two(0), ALU.subtract).then_inc(q.stat, 1)

        def divide(g):
            stat = lambda k: stq[:, g % 2, k, :]
            dve.wait_ge(q.exp, 9 * (g + 1))
            dve.tensor_tensor(stat(5), stat(4), stat(3), ALU.add).then_inc(q.den, 1)
            dve.wait_ge(q.den, 2 * g + 1)
            if g >= 2:
                dve.wait_ge(q.norm0, g - 1)
                dve.wait_ge(q.norm1, g - 1)
            dve.reciprocal(stat(6), stat(5)).then_inc(q.den, 1)
            attn_normalise(dve, q, first, g, 0, q.norm0)

        def low(g):
            dve.wait_ge(q.hi, g + 1)
            t = KT + 2 * g
            dve.tensor_tensor(a_lo[:, t:t + 2, :].rearrange("p a b -> p (a b)"), ps[:, 6 + g % 2, :],
                              a_hi[:, t:t + 2, :].rearrange("p a b -> p (a b)").bitcast(F32),
                              ALU.subtract).then_inc(q.lo, 1)

        return AttnDve(maxima, divide, low)

    def wo1(pe, k):
        pe.wait_ge(at1.lo, k // 2 + 1)
        accumulate(pe, N_WO1 + k, KT + k, k == 0, k == KT - 1)

    WO1_FROM = 11

    def attn1_pe(pe):
        at = attn_pe(pe, at1, True)
        for j in range(QKT):
            if j == 5:
                pe.wait_ge(at1.qk, 5)
                for r in range(REP):
                    at.scores(0, r)
            if j == 7:
                for r in range(REP):
                    at.scores(1, r)
            qk1_pe(pe, j, None if j else first)
        v1_pe(pe)
        pe.wait_ge(at1.qk, QKT)
        for r in range(REP):
            at.scores(2, r)
        pe.wait_ge(at1.v, TT)
        at.turn(0)
        for h in range(HEADS):
            if h == WO1_FROM:
                pe.wait_ge(at1.biased, HEADS)
            if WO1_FROM <= h < HEADS - 1:
                wo1(pe, h - WO1_FROM)
            if h + 1 < HEADS:
                at.turn(h + 1)
            if h < 2:
                at.scores(3, 2 * h)
                at.scores(3, 2 * h + 1)
            at.values(h)
        for k in range(HEADS - 1 - WO1_FROM, KT):
            wo1(pe, k)

    def attn1_act(act):
        at = attn_act(act, at1, True)
        hi_to(act, N_QKV1 + 10)
        at.exponentials(0)
        hi_to(act, N_QKV1 + 13)
        at.exponentials(1)
        hi_to(act, N_WO1 + RING - 1)
        for g in range(KV_HEADS):
            for r in range(REP):
                at.copy(REP * g + r)
                if r and g + 2 < KV_HEADS:
                    at.exponentials(g + 2, ([0], [1], [2, 3])[r - 1])
            at.high(g)

    def attn1_dve(dve):
        at = attn_dve(dve, at1, True, M_SINK1)
        for j in range(5):
            lo_to(dve, N_QKV1 + j + 5)
            qk1_dve(dve, j)
        lo_to(dve, N_QKV1 + 10)
        dve.wait_ge(early_loaded, 32)
        at.maxima(0)
        qk1_dve(dve, 5)
        qk1_dve(dve, 6)
        at.maxima(1)
        qk1_dve(dve, 7)
        lo_to(dve, N_QKV1 + 12)
        at.divide(0)
        qk1_dve(dve, 8)
        qk1_dve(dve, 9)
        lo_to(dve, N_QKV1 + 13)
        v1_dve(dve)
        at.maxima(2)
        at.divide(1)
        lo_to(dve, N_WO1)
        at.maxima(3)
        at.divide(2)
        at.low(0)
        lo_to(dve, N_WO1 + RING - 1)
        at.low(1)
        at.divide(3)
        at.low(2)
        at.low(3)

    G_V, G_U = cut(0, TT, SG), cut(TT * SG, SGT, SEQ)
    G_WS, G_R = cut(12288, GROUPS, P), cut(13312, GROUPS, P)
    G_VN, G_AFF, G_PR = cut(14336, 3, TT, P), cut(15104, 3, P), cut(15488, 3, SEQ)
    lns = sb("lns", [P, 40])
    L_SUM, L_SQ, L_TOT, L_NEG, L_VSUM, L_VAR, L_ROOT, L_INV, L_SHIFT = 0, 12, 24, 26, 28, 30, 32, 34, 36
    g_sem = signals("sgu", "v u masked rows rows_out stat square root vn mixed affine gated product hi lo")
    UB = (7, 0, 1)
    VB = (2, 4, 6)

    def sgu_v_pe(pe, c, first=False, pre=None):
        if not first:
            pe.wait_ge(g_sem.v, 2 * (c - 2))
        b = VB[c % 3]
        for k in range(4):
            tokens(pe, N_SGV + 4 * c + k, [ps[:, b, :], ps[:, b + 1, :]], 2 * k, 2, 512, pre=pre)

    def sgu_spatial(pe, j, i=0):
        pe.wait_ge(g_sem.vn, 2 * j + 2 + 12 * i)
        if j >= 3:
            pe.wait_ge(g_sem.gated, j - 2 + 6 * i)
        for c in range(TT):
            g = j // 3
            rhs = G_WS[:, g, :] if isinstance(i, int) else \
                G_WS[:, bass.ds(g + 2 * i, 1), :].rearrange("p a t -> p (a t)")
            mm = pe.matmul(ps[:, 4 + j % 3, c * P:(c + 1) * P], G_VN[:, j % 3, c, :], rhs,
                           start=True, stop=True)
        mm.then_inc(g_sem.mixed, 1)

    def sgu_pe(pe, pre):
        pe.wait_ge(g_sem.masked, 1)
        for h in range(2):
            mm = pe.matmul(ps[:, h, :], one, G_WS[:, 4 * h:4 * h + 4, :], start=True, stop=True)
        mm.then_inc(g_sem.rows, 1)
        for c in range(3):
            sgu_v_pe(pe, c, first=True, pre=None if c else pre)
        for c in range(3, 6):
            sgu_v_pe(pe, c)
        pe.wait_ge(g_sem.v, 2 * SGC)
        for p in range(3):
            for k in range(2):
                features(pe, N_SGU + 2 * p + k, ps[:, UB[p], k * SEQ:(k + 1) * SEQ])
        def later_pair(p, i=0):
            pe.wait_ge(g_sem.u, p - 2 + 3 * i)
            for k in range(2):
                features(pe, N_SGU + 2 * p + k, ps[:, UB[p % 3], k * SEQ:(k + 1) * SEQ], i)

        with pe.Fori(0, SGT // 6 - 2) as i:
            for p in range(3, 6):
                later_pair(p, i)
        for j in range(3):
            sgu_spatial(pe, j)
        for p in range(SGT // 2 - 3, SGT // 2):
            later_pair(p)
        pe.wait_ge(g_sem.u, SGT // 2)

        def out_tile(j, i=0):
            pe.wait_ge(g_sem.lo, j + 1 + 6 * i)
            accumulate(pe, N_SGO + j, KT + j % 3, j == 0, j == SGT - 1, i)

        out_tile(0)
        with pe.Fori(0, 3) as i:
            for j in range(1, 7):
                sgu_spatial(pe, j + 2, i)
                out_tile(j, i)
        for j in range(19, SGT):
            if j + 2 < SGT:
                sgu_spatial(pe, j + 2)
            out_tile(j)

    def sgu_act(act):
        act.wait_ge(g_sem.rows, 1)
        act.activation(G_R.rearrange("p a b -> p (a b)"), ps[:, 0:2, :].rearrange("p a b -> p (a b)"),
                       ACT.Copy).then_inc(g_sem.rows_out, 1)
        hi_to(act, N_SGV + 5)
        for c in range(SGC):
            hi_to(act, N_SGV + 4 * c + 8)
            for tt in range(TT):
                act.wait_ge(unit_used, N_SGV + 4 * c + 4)
                act.activation(G_V[:, tt, c * 512:(c + 1) * 512], ps[:, VB[c % 3] + tt, :],
                               ACT.Gelu_apprx_tanh,
                               accum_out=lns[:, L_SUM + 6 * tt + c:L_SUM + 6 * tt + c + 1]).then_inc(g_sem.v, 1)
            hi_to(act, N_SGV + 4 * c + 9)

        def moments(tt):
            act.wait_ge(g_sem.stat, 2)
            for c in range(SGC):
                if tt or c:
                    act.wait_ge(g_sem.square, SGC * tt + c)
                act.activation(G_PR[:, 0:2, :].rearrange("p a b -> p (a b)"), G_V[:, tt, c * 512:(c + 1) * 512],
                               ACT.Square, bias=lns[:, L_NEG + tt:L_NEG + tt + 1],
                               accum_out=lns[:, L_SQ + 6 * tt + c:L_SQ + 6 * tt + c + 1]).then_inc(g_sem.square, 1)

        def pair(p, i, split):
            split(0)
            act.wait_ge(unit_used, N_SGU + 2 * p + 2 + 6 * i)
            dst = G_U[:, 2 * p:2 * p + 2, :] if isinstance(i, int) else G_U[:, bass.ds(2 * p + 6 * i, 2), :]
            act.activation(dst.rearrange("p a b -> p (a b)"), ps[:, UB[p % 3], :],
                           ACT.Gelu_apprx_tanh).then_inc(g_sem.u, 1)
            split(1)

        def vn(j, i=0):
            if j >= 3:
                act.wait_ge(g_sem.mixed, j - 2 + 6 * i)
            for tt in range(TT):
                src = G_V[:, tt, j * P:(j + 1) * P] if isinstance(i, int) else \
                    G_V[:, tt, bass.ds(j * P + 6 * P * i, P)]
                act.activation(G_VN[:, j % 3, tt, :], src, ACT.Identity,
                               bias=lns[:, L_SHIFT + tt:L_SHIFT + tt + 1],
                               scale=lns[:, L_INV + tt:L_INV + tt + 1]).then_inc(g_sem.vn, 1)

        def high(j, i=0):
            act.wait_ge(g_sem.product, j + 1 + 6 * i)
            if j >= 3:
                act.wait_ge(unit_used, N_SGO + j - 2 + 6 * i)
            act.activation(a_hi[:, KT + j % 3, :], G_PR[:, j % 3, :], ACT.Copy).then_inc(g_sem.hi, 1)

        def straight_pair(p):
            pair(p, 0, lambda j: hi_to(act, N_SGU + 2 * p + 6 + j))

        moments(0)
        straight_pair(0)
        moments(1)
        straight_pair(1)
        act.wait_ge(g_sem.stat, 4)
        act.activation(lns[:, L_ROOT:L_ROOT + 2], lns[:, L_VAR:L_VAR + 2], ACT.Sqrt).then_inc(g_sem.root, 1)
        act.wait_ge(g_sem.stat, 6)
        for j in range(3):
            vn(j)
        straight_pair(2)
        with act.Fori(0, SGT // 6 - 2) as i:
            for p in range(3, 6):
                pair(p, i, lambda j, p=p: hi_of(act, N_SGU + 2 * p + 6 + j, i))
        act_at[0] = N_SGO
        for p in range(SGT // 2 - 3, SGT // 2):
            straight_pair(p)
            if p == SGT // 2 - 3:
                high(0)
        vn(3)
        high(1)
        with act.Fori(0, 3) as i:
            for j in range(1, 7):
                vn(j + 3, i)
                high(j + 1, i)
                hi_of(act, N_SGO + j + 5, i)
        act_at[0] = N_SGO + 24
        for j in range(19, SGT):
            if j + 3 < SGT:
                vn(j + 3)
            if j + 1 < SGT:
                high(j + 1)
            hi_to(act, N_SGO + j + 5)

    def sgu_dve(dve):
        lo_to(dve, N_SGV + 4 * SGC - 1 + 6)
        dve.wait_ge(g_sem.v, 2 * SGC)
        dve.tensor_reduce(lns[:, L_TOT:L_TOT + 2], lns[:, L_SUM:L_SUM + 12].rearrange("p (a b) -> p a b", a=2),
                          AX.X, ALU.add).then_inc(g_sem.stat, 1)
        dve.wait_ge(g_sem.stat, 1)
        dve.tensor_scalar(lns[:, L_NEG:L_NEG + 2], lns[:, L_TOT:L_TOT + 2], -1.0 / SG, None,
                          ALU.mult).then_inc(g_sem.stat, 1)
        lo_to(dve, N_SGU + 9)
        dve.wait_ge(g_sem.square, 12)
        dve.tensor_reduce(lns[:, L_VSUM:L_VSUM + 2], lns[:, L_SQ:L_SQ + 12].rearrange("p (a b) -> p a b", a=2),
                          AX.X, ALU.add).then_inc(g_sem.stat, 1)
        dve.wait_ge(g_sem.stat, 3)
        dve.tensor_scalar(lns[:, L_VAR:L_VAR + 2], lns[:, L_VSUM:L_VSUM + 2], 1.0 / SG, EPS,
                          ALU.mult, ALU.add).then_inc(g_sem.stat, 1)
        dve.wait_ge(g_sem.root, 1)
        dve.reciprocal(lns[:, L_INV:L_INV + 2], lns[:, L_ROOT:L_ROOT + 2]).then_inc(g_sem.stat, 1)
        dve.wait_ge(g_sem.stat, 5)
        dve.tensor_tensor(lns[:, L_SHIFT:L_SHIFT + 2], lns[:, L_INV:L_INV + 2], lns[:, L_NEG:L_NEG + 2],
                          ALU.mult).then_inc(g_sem.stat, 1)
        lo_to(dve, N_SGU + 11)

        def gate(j, i=0):
            b = j % 3
            c = C_LN + 2 * j
            g = cols[:, c:c + 1] if isinstance(i, int) else cols[:, bass.ds(c + 12 * i, 1)]
            u = G_U[:, j, :] if isinstance(i, int) else \
                G_U[:, bass.ds(j + 6 * i, 1), :].rearrange("p a t -> p (a t)")
            dve.wait_ge(g_sem.mixed, j + 1 + 6 * i)
            dve.wait_ge(g_sem.affine, 2 * j + 2 + 12 * i)
            if j >= 3:
                dve.wait_ge(g_sem.lo, j - 2 + 6 * i)
            dve.scalar_tensor_tensor(G_PR[:, b, :].rearrange("p (c t) -> p c t", c=TT),
                                     ps[:, 4 + b, 0:SEQ].rearrange("p (c t) -> p c t", c=TT), g,
                                     G_AFF[:, b:b + 1, :].to_broadcast([P, TT, P]), ALU.mult,
                                     ALU.add).then_inc(g_sem.gated, 1)
            dve.wait_ge(g_sem.gated, j + 1 + 6 * i)
            dve.tensor_tensor(G_PR[:, b, :], G_PR[:, b, :], u, ALU.mult).then_inc(g_sem.product, 1)

        def low(j, i=0):
            dve.wait_ge(g_sem.hi, j + 1 + 6 * i)
            dve.tensor_tensor(a_lo[:, KT + j % 3, :], G_PR[:, j % 3, :],
                              a_hi[:, KT + j % 3, :].bitcast(F32), ALU.subtract).then_inc(g_sem.lo, 1)

        with dve.Fori(0, SGT // 6 - 2) as i:
            for n in range(12, 18):
                lo_of(dve, N_SGU + n, i)
        dve_at[0] = N_SGO
        gate(0)
        gate(1)
        lo_to(dve, N_SGO + 1)
        low(0)
        gate(2)
        lo_to(dve, N_SGO + 5)
        low(1)
        with dve.Fori(0, 3) as i:
            for j in range(1, 7):
                gate(j + 2, i)
                lo_of(dve, N_SGO + j + 5, i)
                low(j + 1, i)
        dve_at[0] = N_SGO + 24
        for j in range(19, SGT):
            if j + 2 < SGT:
                gate(j + 2)
            lo_to(dve, N_SGO + j + 5)
            if j + 1 < SGT:
                low(j + 1)

    def sgu_pool(pool):
        def affine(j):
            b, c, g = j % 3, C_LN + 2 * j + 1, j // 3
            if j >= 3:
                pool.wait_ge(g_sem.gated, j - 2)
            pool.tensor_tensor(G_AFF[:, b, :], G_R[:, g, :], cols[:, c:c + 1].to_broadcast([P, P]),
                               ALU.mult).then_inc(g_sem.affine, 1)
            pool.wait_ge(g_sem.affine, 2 * j + 1)
            pool.tensor_tensor(G_AFF[:, b, :], G_AFF[:, b, :], misc[:, M_BS + g * P:M_BS + (g + 1) * P],
                               ALU.add).then_inc(g_sem.affine, 1)

        pool.wait_ge(g_sem.rows_out, 1)
        for j in range(SGT):
            affine(j)

    DT_STEP, DT_SUMS = 2, 4
    S_X, S_B, S_F = cut(6144, TT, D), cut(8192, TT, 256), cut(8704, 4, SEQ)
    S_T, S_XDD, S_ST = cut(9728, 2, 512), cut(10752, 512), cut(11264, 2, 512)
    S_E, S_LA, S_CB = cut(12288, 4, 512), cut(14336, 2, 512), cut(15360, 2, 2, P)
    S_CV, S_SL = cut(12288, 2, SEQ), cut(12800, 2, SEQ)
    S_Z = cut(12288, TT, D)
    x_sem = signals("xbc", "copied conv silu turned moved")

    def xbc_dst(j):
        return S_SL[:, j % 2, :] if j < 8 else S_F[:, j - 8, :]

    def x_unit(j):
        return N_MIX + 2 * j

    def x_bank(j):
        return 4 + j % 2 if j else 0

    def mixer_in_pe(pe, pre, q):
        def turn(j):
            pe.wait_ge(x_sem.silu, j + 1)
            if j >= 2:
                pe.wait_ge(x_sem.moved, j - 1)
            for tt in range(TT):
                mm = pe.transpose(ps[:, 6 + j % 2, tt * P:(tt + 1) * P],
                                  xbc_dst(j)[:, tt * P:(tt + 1) * P], ident)
            mm.then_inc(x_sem.turned, 1)

        for j in range(XT):
            if j >= 2:
                pe.wait_ge(x_sem.copied, j - 1)
            features(pe, x_unit(j), ps[:, x_bank(j), 0:SEQ], pre=None if j else pre)
            if j == 0:
                dt_pe(pe)
            if 1 <= j < XT - 1:
                turn(j - 1)
            if j == DT_SUMS:
                dt_sums_pe(pe)
            if j < QKT:
                if j >= 2:
                    pe.wait_ge(q.qk, j - 1)
                features(pe, x_unit(j) + 1, ps[:, 2 + j % 2, 0:SEQ])
            else:
                if j == QKT:
                    pe.wait_ge(d_sem.decay, 1)
                tokens(pe, x_unit(j) + 1, [ps[:, 0, 0:256], ps[:, 1, 0:256]], 4 * (j - QKT), 4, 256)

    def mixer_in_act(act):
        def move(j):
            act.wait_ge(x_sem.turned, j + 1)
            dst = S_X[:, :, j * P:(j + 1) * P] if j < 8 else S_B[:, :, (j - 8) * P:(j - 7) * P]
            act.activation(dst, ps[:, 6 + j % 2, 0:SEQ].rearrange("p (a b) -> p a b", a=TT),
                           ACT.Copy).then_inc(x_sem.moved, 1)

        for j in range(XT):
            hi_to(act, x_unit(j) + 5)
            act.wait_ge(unit_used, x_unit(j) + 1)
            if j >= 2:
                act.wait_ge(x_sem.conv, 5 * (j - 1))
            act.activation(pad[:, j % 2, 2:2 + SEQ], ps[:, x_bank(j), 0:SEQ], ACT.Copy).then_inc(x_sem.copied, 1)
            if 2 <= j < XT:
                move(j - 2)
            hi_to(act, x_unit(j) + 6)
            if j == DT_STEP:
                dt_act(act)
            if j == DT_SUMS + 1:
                decay_act(act)
            act.wait_ge(x_sem.conv, 5 * j + 5)
            if 2 <= j < 8:
                act.wait_ge(x_sem.turned, j - 1)
            act.activation(xbc_dst(j), S_CV[:, j % 2, :], ACT.Silu).then_inc(x_sem.silu, 1)

    def mixer_in_dve(dve, q):
        for j in range(XT):
            lo_to(dve, x_unit(j) + 5)
            c = C_XBC + 6 * j
            b = j % 2
            dve.wait_ge(x_sem.copied, j + 1)
            if j >= 2:
                dve.wait_ge(x_sem.silu, j - 1)
            dve.tensor_scalar(S_CV[:, b, :], pad[:, b, 0:SEQ], cols[:, c:c + 1], cols[:, c + 5:c + 6],
                              ALU.mult, ALU.add).then_inc(x_sem.conv, 1)
            for k in range(1, 5):
                dve.wait_ge(x_sem.conv, 5 * j + k)
                dve.scalar_tensor_tensor(S_CV[:, b, :], pad[:, b, k:k + SEQ], cols[:, c + k:c + k + 1],
                                         S_CV[:, b, :], ALU.mult, ALU.add).then_inc(x_sem.conv, 1)
            lo_to(dve, x_unit(j) + 6)
            if j == DT_STEP:
                dt_dve(dve)
            if j < QKT:
                dve.wait_ge(unit_used, x_unit(j) + 2)
                dst = A_Q[:, j, :] if j < QT else A_K[:, j - QT, :]
                dve.tensor_scalar(dst, ps[:, 2 + j % 2, 0:SEQ], DH ** -0.5 if j < QT else 1.0, None,
                                  ALU.mult).then_inc(q.qk, 1)
        dve.wait_ge(unit_used, N_Z)
        dve.tensor_copy(A_V[:, :, :], ps[:, 0:2, 0:256]).then_inc(q.v, TT)

    dts = sb("dts", [P, 12, 64])
    ex = sb("ex", [P, 4, HEADS])
    ea = sb("ea", [P, 32])
    d_sem = signals("dt", "w_hi w_lo product step exp ln sums decay")
    V_A, V_NEG, V_E, V_U, V_L, V_D, V_EQ, V_D2, V_RD, V_T, V_DT, V_DA = range(12)

    def dt_pe(pe):
        pe.wait_ge(d_sem.w_lo, 1)
        for tt in range(TT):
            t = slice(tt * P, (tt + 1) * P)
            for k in range(KT):
                mm = three(pe, ps[:, 1, 32 * tt:32 * tt + 32], a_hi[:, k, t], a_lo[:, k, t],
                           wdt_hi[:, k, :], wdt_lo[:, k, :], k == 0, k == KT - 1)
        mm.then_inc(d_sem.product, 1)

    def dt_sums_pe(pe):
        pe.wait_ge(d_sem.step, 12)
        da = dts[:, V_DA, :].rearrange("p (a b) -> p a b", a=TT)
        for n, (m, c, d) in enumerate(((gt, 0, 0), (lt, 1, 1), (ge, 0, 1), (le, 1, 0))):
            mm = pe.matmul(ps[:, 1, 128 + 16 * n:144 + 16 * n], m, da[:, c, 16 * d:16 * d + 16],
                           start=True, stop=True)
        mm.then_inc(d_sem.sums, 1)

    def dt_act(act):
        act.wait_ge(d_sem.step, 2)
        act.activation(dts[:, V_E, :], dts[:, V_NEG, :], ACT.Exp).then_inc(d_sem.exp, 1)
        act.activation(ea[:, :], misc[:, M_ALOG:M_ALOG + 32], ACT.Exp).then_inc(d_sem.exp, 1)
        act.wait_ge(d_sem.step, 3)
        act.activation(dts[:, V_L, :], dts[:, V_U, :], ACT.Ln).then_inc(d_sem.ln, 1)

    def decay_act(act):
        act.wait_ge(d_sem.sums, 1)
        act.activation(ex[:, :, :].rearrange("p a b -> p (a b)"), ps[:, 1, 128:192], ACT.Exp).then_inc(d_sem.decay, 1)

    def dt_dve(dve):
        v = lambda k: dts[:, k, :]
        two = lambda k: v(k).rearrange("p (a b) -> p a b", a=TT)
        row32 = lambda t, o: t[:, o:o + 32].rearrange("p (a b) -> p a b", a=1).to_broadcast([P, TT, 32])
        step = [0]

        def then(ins):
            ins.then_inc(d_sem.step, 1)
            step[0] += 1
            dve.wait_ge(d_sem.step, step[0])

        dve.wait_ge(d_sem.product, 1)
        then(dve.tensor_tensor(two(V_A), ps[:, 1, 0:64].rearrange("p (a b) -> p a b", a=TT), row32(misc, M_DTB), ALU.add))
        then(dve.scalar_tensor_tensor(v(V_NEG), v(V_A), -1.0, v(V_A), ALU.mult, ALU.min))
        dve.wait_ge(d_sem.exp, 2)
        then(dve.tensor_scalar(v(V_U), v(V_E), 1.0, None, ALU.add))
        then(dve.tensor_scalar(v(V_D), v(V_U), 1.0, None, ALU.subtract))
        then(dve.tensor_scalar(v(V_EQ), v(V_U), 1.0, None, ALU.is_equal))
        then(dve.tensor_tensor(v(V_D2), v(V_D), v(V_EQ), ALU.add))
        then(dve.reciprocal(v(V_RD), v(V_D2)))
        then(dve.tensor_tensor(v(V_T), v(V_E), v(V_RD), ALU.mult))
        dve.wait_ge(d_sem.ln, 1)
        then(dve.tensor_tensor(v(V_D), v(V_L), v(V_EQ), ALU.add))
        then(dve.tensor_tensor(v(V_T), v(V_T), v(V_D), ALU.mult))
        then(dve.scalar_tensor_tensor(v(V_DT), v(V_A), 0.0, v(V_T), ALU.max, ALU.add))
        then(dve.scalar_tensor_tensor(two(V_DA), two(V_DT), -1.0, row32(ea, 0), ALU.mult, ALU.mult))

    s_sem = signals("ssd", "la diff exp m pair cb cb_out decayed xdd state state_out off scaled skipped t y comb")
    decayed = sb("decayed", [P, 2, 8])

    def heads_bc(v, n, width):
        return v.rearrange("p (h a) -> p h a", a=1).to_broadcast([P, n, width])

    def eight(v):
        return v.rearrange("p (h e) -> p h e", h=8)

    def y_of(n):
        return ybuf[:, n % 2, (n // 2) * 512:(n // 2 + 1) * 512]

    def x_of(n):
        return S_X[:, n % 2, (n // 2) * 512:(n // 2 + 1) * 512]

    def ssd_pool(pool):
        pool.wait_ge(d_sem.step, 12)
        for b in range(16):
            k, q, d = b // 4, b // 2 % 2, b % 2
            g, c = k // 2, k % 2
            if b >= 2:
                pool.wait_ge(s_sem.diff, b - 1)
            o = 32 * c + 16 * d + 8 * g + 4 * q
            mask = (gt, lt)[d].rearrange("p (a b) -> p a b", a=1).to_broadcast([P, 4, P])
            pool.tensor_tensor(S_LA[:, b % 2, :].rearrange("p (h t) -> p h t", h=4), mask,
                               heads_bc(dts[:, V_DA, o:o + 4], 4, P), ALU.mult).then_inc(s_sem.la, 1)
            if b % 2 and 3 <= b <= 9:
                n = (b - 3) // 2
                pool.wait_ge(x_sem.moved, XT - 2)
                pool.tensor_tensor(eight(y_of(n)), eight(x_of(n)),
                                   heads_bc(misc[:, M_SKIP + 8 * (n // 2):M_SKIP + 8 * (n // 2) + 8], 8, DH),
                                   ALU.mult).then_inc(s_sem.skipped, 1)

    def ssd_pe(pe):
        def diff(b):
            pe.wait_ge(s_sem.la, b + 1)
            if b >= 2:
                pe.wait_ge(s_sem.exp, b - 1)
            for h in range(4):
                mm = pe.matmul(ps[:, 4 + b % 2, h * P:(h + 1) * P], S_LA[:, b % 2, h * P:(h + 1) * P],
                               (le, ge)[b % 2], start=True, stop=True)
            mm.then_inc(s_sem.diff, 1)

        def products(k):
            g, c = k // 2, k % 2
            t = slice(c * P, (c + 1) * P)
            if k >= 1:
                pe.wait_ge(s_sem.cb_out, 2 * k)
            pe.matmul(ps[:, 6, 0:P], S_F[:, g, t], S_F[:, 2 + g, t], start=True,
                      stop=True).then_inc(s_sem.cb, 1)

        def diagonal(j):
            k, q = j // 2, j % 2
            c = k % 2
            pe.wait_ge(s_sem.pair, j + 1)
            if k >= 2:
                pe.wait_ge(s_sem.t, c + 1)
            for h in range(4):
                o = (4 * q + h) * DH
                mm = pe.matmul(ps[:, c, o:o + DH], S_E[:, 2 * (j % 2), h * P:(h + 1) * P],
                               x_of(k)[:, o:o + DH], start=True, stop=True)
            mm.then_inc(s_sem.y, 1)

        def state(k):
            g, c = k // 2, k % 2
            pe.wait_ge(s_sem.xdd, k + 1)
            if k >= 1:
                pe.wait_ge(s_sem.state_out, k)
            pe.matmul(ps[:, 7, :], S_B[:, c, g * P:(g + 1) * P], S_XDD, start=True,
                      stop=True).then_inc(s_sem.state, 1)

        def off(k):
            g, c = k // 2, k % 2
            pe.wait_ge(s_sem.state_out, k + 1)
            if g:
                pe.wait_ge(s_sem.scaled, 2 - c)
            pe.matmul(ps[:, 2 + (1 - c), :], S_F[:, 2 + g, (1 - c) * P:(2 - c) * P], S_ST[:, c, :],
                      start=True, stop=True).then_inc(s_sem.off, 1)

        pe.wait_ge(at2.v, TT)
        for k in range(4):
            products(k)
            diff(4 * k)
            diff(4 * k + 1)
            state(k)
            diff(4 * k + 2)
            if k:
                diagonal(2 * k - 1)
            diff(4 * k + 3)
            off(k)
            diagonal(2 * k)
        diagonal(7)

    def ssd_act(act):
        act.wait_ge(x_sem.silu, XT)
        for k in range(4):
            g = k // 2
            for b in range(4 * k, 4 * k + 4):
                act.wait_ge(s_sem.diff, b + 1)
                if b >= 4:
                    act.wait_ge(s_sem.y, b // 2 - 1)
                act.activation(S_E[:, b % 4, :], ps[:, 4 + b % 2, :], ACT.Exp).then_inc(s_sem.exp, 1)
                if b % 4 == 1:
                    act.wait_ge(s_sem.state, k + 1)
                    if k >= 2:
                        act.wait_ge(s_sem.off, k - 1)
                    act.activation(S_ST[:, k % 2, :], ps[:, 7, :], ACT.Copy).then_inc(s_sem.state_out, 1)
            if k % 2:
                for n in (2 * g, 2 * g + 1):
                    act.wait_ge(s_sem.off, 2 * g + 2 - n % 2)
                    if n >= 2:
                        act.wait_ge(s_sem.comb, n - 1)
                    for h in range(8):
                        o = slice(h * DH, (h + 1) * DH)
                        ins = act.activation(S_T[:, n % 2, o], ps[:, 2 + n % 2, o], ACT.Copy,
                                             scale=ex[:, 2 + n % 2, 8 * g + h:8 * g + h + 1])
                    ins.then_inc(s_sem.scaled, 1)

    def ssd_dve(dve):
        def outputs(g):
            for n in (2 * g, 2 * g + 1):
                dve.wait_ge(s_sem.y, 2 * n + 2)
                dve.wait_ge(s_sem.scaled, n + 1)
                dve.tensor_tensor(S_T[:, n % 2, :], S_T[:, n % 2, :], ps[:, n % 2, :], ALU.add).then_inc(s_sem.t, 1)
            for n in (2 * g, 2 * g + 1):
                dve.wait_ge(s_sem.t, n + 1)
                dve.wait_ge(s_sem.skipped, n + 1)
                dve.tensor_tensor(y_of(n), y_of(n), S_T[:, n % 2, :], ALU.add).then_inc(s_sem.comb, 1)

        dve.wait_ge(d_sem.decay, 1)
        for k in range(4):
            g, c = k // 2, k % 2
            o = 48 * c + 8 * g
            if k >= 2:
                dve.wait_ge(s_sem.xdd, k - 1)
            dve.tensor_tensor(decayed[:, k % 2, :], dts[:, V_DT, o:o + 8], ex[:, c, 8 * g:8 * g + 8],
                              ALU.mult).then_inc(s_sem.decayed, 1)
            dve.wait_ge(s_sem.decayed, k + 1)
            if k:
                dve.wait_ge(s_sem.state, k)
            dve.tensor_tensor(eight(S_XDD), eight(x_of(k)), heads_bc(decayed[:, k % 2, :], 8, DH),
                              ALU.mult).then_inc(s_sem.xdd, 1)
            dve.wait_ge(s_sem.cb, k + 1)
            if k >= 2:
                dve.wait_ge(s_sem.m, 4 * (k - 1))
            for d in range(2):
                dve.tensor_tensor(S_CB[:, k % 2, d, :], ps[:, 6, 0:P], (le, ge)[d], ALU.mult).then_inc(s_sem.cb_out, 1)
            dve.wait_ge(s_sem.cb_out, 2 * k + 2)
            for q in range(2):
                for d in range(2):
                    b = 4 * k + 2 * q + d
                    dve.wait_ge(s_sem.exp, b + 1)
                    for h in range(4):
                        e = S_E[:, b % 4, h * P:(h + 1) * P]
                        t = 32 * c + 16 * d + 8 * g + 4 * q + h
                        ins = dve.scalar_tensor_tensor(e, e, dts[:, V_DT, t:t + 1], S_CB[:, k % 2, d, :],
                                                       ALU.mult, ALU.mult)
                    ins.then_inc(s_sem.m, 1)
                dve.wait_ge(s_sem.m, 4 * k + 2 * q + 2)
                dve.tensor_tensor(S_E[:, 2 * q, :], S_E[:, 2 * q, :], S_E[:, 2 * q + 1, :],
                                  ALU.add).then_inc(s_sem.pair, 1)
                if k == 2 and q == 0:
                    outputs(0)
        outputs(1)

    z_sem = signals("z", "silu gated")

    def z_pe(pe, c, k):
        tokens(pe, N_Z + 4 * c + k, [ps[:, 4 + 2 * c, :], ps[:, 5 + 2 * c, :]], 2 * k, 2, 512)

    def z_act(act, c):
        for tt in range(TT):
            act.wait_ge(unit_used, N_Z + 4 * c + 4)
            act.activation(S_Z[:, tt, c * 512:(c + 1) * 512], ps[:, 4 + 2 * c + tt, :],
                           ACT.Silu).then_inc(z_sem.silu, 1)

    def z_dve(dve):
        dve.wait_ge(z_sem.silu, 4)
        for tt in range(TT):
            dve.tensor_tensor(ybuf[:, tt, :], ybuf[:, tt, :], S_Z[:, tt, :], ALU.mult).then_inc(z_sem.gated, 1)

    def wo2(pe, k):
        if k >= KT:
            pe.wait_ge(at2.lo, (k - KT) // 2 + 1)
        accumulate(pe, N_WO2 + k, k, k == 0, k == 2 * KT - 1)

    MIX_TURN, WO2_FROM = 7, 9

    def attn2_pe(pe):
        at = attn_pe(pe, at2, False)
        pe.wait_ge(s_sem.exp, 16)
        pe.wait_ge(s_sem.state_out, 4)
        pe.wait_ge(s_sem.cb_out, 8)
        pe.wait_ge(at2.qk, QKT)
        for g in range(3):
            for k in range(2):
                z_pe(pe, g // 2, 2 * (g % 2) + k)
            if g == 0:
                pe.wait_ge(s_sem.comb, 4)
            for r in range(REP):
                at.scores(g, r)
        z_pe(pe, 1, 2)
        pe.wait_ge(z_sem.silu, 2)
        at.turn(0)
        z_pe(pe, 1, 3)
        for h in range(HEADS):
            if h == MIX_TURN:
                pe.wait_ge(at2.biased, HEADS)
                turn_pe(pe, mix, 0)
            if h == WO2_FROM:
                pe.wait_ge(mix.lo, KT * (mix.n + 1))
            if WO2_FROM <= h < HEADS - 1:
                wo2(pe, h - WO2_FROM)
            if h + 1 < HEADS:
                at.turn(h + 1)
            if h < 2:
                at.scores(3, 2 * h)
                at.scores(3, 2 * h + 1)
            if h == 0:
                pe.wait_ge(z_sem.silu, 4)
            at.values(h)
        for k in range(HEADS - 1 - WO2_FROM, 2 * KT):
            wo2(pe, k)

    def attn2_act(act):
        at = attn_act(act, at2, False)
        hi_to(act, N_Z + 7)
        at.exponentials(0)
        z_act(act, 0)
        at.exponentials(1)
        at.copy(0)
        z_act(act, 1)
        at.copy(1)
        norm_squares(act, mix, lambda tt: ybuf[:, tt, :], lambda tt: (z_sem.gated, tt + 1), 8)
        norm_root(act, mix, 8)
        at.copy(2)
        at.exponentials(2, [0])
        at.copy(3)
        at.exponentials(2, [1])
        at.copy(4)
        at.high(0)
        at.exponentials(2, [2, 3])
        for h in range(5, MIX_TURN + 1):
            at.copy(h)
        hi_to(act, N_WO2 + 1)
        halves_act(act, mix, 6, 0, range(4))
        at.copy(MIX_TURN + 1)
        halves_act(act, mix, 6, 0, range(4, KT))
        at.exponentials(3, [0, 1])
        at.copy(MIX_TURN + 2)
        at.exponentials(3, [2, 3])
        at.high(1)
        for h in range(MIX_TURN + 3, HEADS - REP):
            at.copy(h)
        hi_to(act, N_WO2 + 4)
        at.high(2)
        for h in range(HEADS - REP, HEADS):
            at.copy(h)
            hi_to(act, N_WO2 + h - (HEADS - REP) + 5)
        at.high(3)

    def attn2_dve(dve):
        at = attn_dve(dve, at2, False, M_SINK2)
        at.maxima(0)
        lo_to(dve, N_Z + 7)
        at.maxima(1)
        at.divide(0)
        at.maxima(2)
        at.divide(1)
        z_dve(dve)
        norm_dve(dve, mix, 8)
        scale_dve(dve, mix, 8, ybuf)
        at.maxima(3)
        at.low(0)
        at.divide(2)
        lo_to(dve, N_WO2 + 1)
        halves_dve(dve, mix, 6, 0)
        at.divide(3)
        at.low(1)
        lo_to(dve, N_WO2 + 4)
        at.low(2)
        lo_to(dve, N_WO2 + 8)
        at.low(3)

    M_PR, M_RL = cut(3072, 3, SEQ), cut(3840, 3, SEQ)
    m_sem = signals("mlp", "relu square hi lo")

    def m_up(t):
        return N_MLP + 2 * t - 1 if t else N_MLP

    def m_down(t):
        return N_MLP + 2 * MT - 1 if t == MT - 1 else N_MLP + 2 + 2 * t

    def mlp_in_pe(pe, t, i=0):
        if t >= 3:
            pe.wait_ge(m_sem.relu, t - 2 + 3 * i)
        features(pe, m_up(t), ps[:, 4 + t % 3, 0:SEQ], i)

    def mlp_pe(pe, pre):
        features(pe, m_up(0), ps[:, 0, 0:SEQ], pre=pre)
        for t in (1, 2, 3, 4):
            mlp_in_pe(pe, t)
            pe.wait_ge(m_sem.lo, t)
            accumulate(pe, m_down(t - 1), KT + (t - 1) % 3, t == 1, False)
        with pe.Fori(0, (MT - 5) // 3) as i:
            for t in (5, 6, 7):
                mlp_in_pe(pe, t, i)
                pe.wait_ge(m_sem.lo, t + 3 * i)
                accumulate(pe, m_down(t - 1), KT + (t - 1) % 3, False, False, i)
        pe.wait_ge(m_sem.lo, MT)
        accumulate(pe, m_down(MT - 1), KT + (MT - 1) % 3, False, True)

    def mlp_act(act):
        def step(t, i, split):
            act.wait_ge(unit_used, m_up(t) + 1 + RING * i)
            if t >= 3:
                act.wait_ge(m_sem.square, t - 2 + 3 * i)
            act.activation(M_RL[:, t % 3, :], ps[:, 4 + t % 3 if t else 0, 0:SEQ], ACT.Relu).then_inc(m_sem.relu, 1)
            split(0)
            act.wait_ge(m_sem.square, t + 1 + 3 * i)
            if t >= 3:
                act.wait_ge(unit_used, m_down(t - 3) + 1 + RING * i)
            act.activation(a_hi[:, KT + t % 3, :], M_PR[:, t % 3, :], ACT.Copy).then_inc(m_sem.hi, 1)
            split(1)
        mlp_steps(act, step, hi_of, hi_to, act_at)

    def mlp_dve(dve):
        def step(t, i, split):
            dve.wait_ge(m_sem.relu, t + 1 + 3 * i)
            dve.tensor_tensor(M_PR[:, t % 3, :], M_RL[:, t % 3, :], M_RL[:, t % 3, :],
                              ALU.mult).then_inc(m_sem.square, 1)
            split(0)
            dve.wait_ge(m_sem.hi, t + 1 + 3 * i)
            dve.tensor_tensor(a_lo[:, KT + t % 3, :], M_PR[:, t % 3, :], a_hi[:, KT + t % 3, :].bitcast(F32),
                              ALU.subtract).then_inc(m_sem.lo, 1)
            split(1)
        mlp_steps(dve, step, lo_of, lo_to, dve_at)

    def mlp_steps(eng, step, half_of, half_to, at):
        half_to(eng, N_MLP + 5)
        step(0, 0, lambda j: half_to(eng, N_MLP + 6) if j == 0 else None)
        for t in range(1, 5):
            step(t, 0, lambda j, t=t: half_to(eng, m_up(t) + 6 + j))
        with eng.Fori(0, 8) as i:
            for t in (5, 6, 7):
                step(t, i, lambda j, t=t: half_of(eng, m_up(t) + 6 + j, i))
        at[0] = UNITS - 1
        for t in range(29, MT):
            step(t, 0, lambda j, t=t: half_to(eng, UNITS - 1))

    first, mix = Norm(0, *pre_sems), Norm(5, *pre_sems)
    updates = [update(n, Norm(k, *pre_sems)) for n, k in enumerate((1, 2, 3, 4, 6, 7))]
    ffn = [ffn_sems("ffn0"), ffn_sems("ffn1")]
    at1, at2 = attn_sems("attn1"), attn_sems("attn2")
    x_rows, out_rows = (v.rearrange("(t p) d -> p t d", p=P) for v in (x_in, out))

    with nc.Block() as block:

        @block.sync
        def _(sp):
            for tt in range(TT):
                sp.dma_start(x[:, tt, :], x_rows[:, tt, :]).then_inc(x_loaded[tt], 16)
            for s in range(RING):
                sp.dma_start(raw[:, s, :], w[s]).then_inc(raw_loaded[s], 16)
            with sp.Fori(0, UNITS // RING - 1) as i:
                for s in range(RING):
                    sp.wait_ge(lo_done, s + 1 + RING * i)
                    sp.dma_start(raw[:, s, :], w[bass.ds(i * RING + RING + s, 1)].rearrange("a p n -> p (a n)")
                                 ).then_inc(raw_loaded[s], 16)
            for tt in range(TT):
                sp.wait_ge(add_sems.added, 5 * TT + tt + 1)
                sp.dma_start(out_rows[:, tt, :], x[:, tt, :]).then_inc(out_done, 16)
            sp.wait_ge(out_done, 16 * TT)

        @block.gpsimd
        def _(pool):
            def load_row(r):
                pool.dma_start(row[:, r % 2, :], rows_in[r:r + 1, :].to_broadcast([P, D])).then_inc(row_loaded[r % 2], 16)

            def updated(u):
                pool.wait_ge(add_sems.added, TT * (u + 1))

            pool.memset(pad[:], 0.0).then_inc(pad_ready, 1)
            attn_pool(pool, at1, True, range(2))
            for view, src in ((wdt[:], wdt_in), (tab[:, P:T_D1], tables_in[:, P:T_D1]),
                              (tab[:, T_D2:], tables_in[:, T_D2:]),
                              (misc[:, M_BS:], misc_in[:, M_BS:].to_broadcast([P, MISC - M_BS]))):
                pool.dma_start(view, src).then_inc(late_loaded, 16)
            load_row(0)
            load_row(1)
            pool.dma_start(G_WS, ws_in).then_inc(ws_loaded, 16)
            attn_pool(pool, at1, True, range(2, KV_HEADS))
            pool.wait_ge(late_loaded, 64)
            pool.wait_ge(ws_loaded, 16)
            pool.tensor_tensor(G_WS, G_WS, le.rearrange("p (a b) -> p a b", a=1).to_broadcast([P, GROUPS, P]),
                               ALU.mult).then_inc(g_sem.masked, 1)
            pool.wait_ge(updates[0].biased, TT)
            load_row(2)
            updated(0)
            load_row(3)
            updated(1)
            load_row(4)
            sgu_pool(pool)
            updated(2)
            load_row(5)
            updated(3)
            load_row(6)
            ssd_pool(pool)
            attn_pool(pool, at2, False)
            updated(4)

        @block.scalar
        def _(act):
            act.dma_start(ident, tables_in[:, T_ID:T_ID + P]).then_inc(ident_loaded, 16)
            act.dma_start(cols[:], cols_in).then_inc(cols_loaded, 16)
            act.preload_act_table(ACT.Sqrt)
            norm_act(act, first, lambda tt: x[:, tt, :], lambda tt: (x_loaded[tt], 16), 8)
            hi_to(act, 1)
            act.wait_ge(cols_loaded, 16)
            halves_act(act, first, 0)
            act.dma_start(tab[:, T_D1:T_D2], tables_in[:, T_D1:T_D2]).then_inc(early_loaded, 16)
            act.dma_start(misc[:, 0:M_BS], misc_in[:, 0:M_BS].to_broadcast([P, M_BS])).then_inc(early_loaded, 16)
            hi_to(act, 5)
            attn1_act(act)
            act.wait_ge(late_loaded, 64)
            act.activation(wdt_hi[:], wdt[:], ACT.Copy).then_inc(d_sem.w_hi, 1)
            hi_to(act, N_FFN0 - 1)
            update_act(act, updates[0], N_FFN0 - 1, 1, True, ACT.Gelu_apprx_tanh)
            act.wait_ge(pad_ready, 1)
            ffn_act(act, ffn[0], N_FFN0)
            update_act(act, updates[1], N_SGV - 1, 2, False, ACT.Gelu_apprx_tanh)
            sgu_act(act)
            update_act(act, updates[2], N_FFN1 - 1, 3, False, ACT.Gelu_apprx_tanh)
            ffn_act(act, ffn[1], N_FFN1)
            update_act(act, updates[3], N_MIX - 1, 4, False, ACT.Silu)
            mixer_in_act(act)
            hi_to(act, N_Z + 5)
            ssd_act(act)
            attn2_act(act)
            hi_to(act, N_MLP - 1)
            update_act(act, updates[4], N_MLP - 1, 5, False, ACT.Relu)
            mlp_act(act)
            update_act(act, updates[5], UNITS - 1, None, False, None)

        @block.vector
        def _(dve):
            norm_dve(dve, first, 8)
            scale_dve(dve, first, 8, x)
            lo_to(dve, 1)
            dve.wait_ge(cols_loaded, 16)
            halves_dve(dve, first, 0)
            attn1_dve(dve)
            dve.wait_ge(d_sem.w_hi, 1)
            dve.tensor_tensor(wdt_lo[:], wdt[:], wdt_hi[:].bitcast(F32), ALU.subtract).then_inc(d_sem.w_lo, 1)
            lo_to(dve, N_FFN0 - 1)
            update_dve(dve, updates[0], N_FFN0 - 1, 1, 1, 0)
            ffn_dve(dve, ffn[0], N_FFN0, 0)
            update_dve(dve, updates[1], N_SGV - 1, 2, 2, None)
            sgu_dve(dve)
            update_dve(dve, updates[2], N_FFN1 - 1, 3, 3, None)
            ffn_dve(dve, ffn[1], N_FFN1, 1)
            update_dve(dve, updates[3], N_MIX - 1, 4, 4, None)
            mixer_in_dve(dve, at2)
            lo_to(dve, N_Z + 5)
            ssd_dve(dve)
            attn2_dve(dve)
            lo_to(dve, N_MLP - 1)
            update_dve(dve, updates[4], N_MLP - 1, 5, 5, None)
            mlp_dve(dve)
            update_dve(dve, updates[5], UNITS - 1, None, 6, None)

        @block.tensor
        def _(pe):
            keep_warm(pe, WARM_FIRST, ident_loaded, 16)
            for tt in range(TT):
                keep_warm(pe, WARM_FIRST, first.sum, tt + 1)
            turn_pe(pe, first)

            attn1_pe(pe)
            keep_warm_update(pe, updates[0])
            turn_pe(pe, updates[0].pre)
            ffn_pe(pe, ffn[0], N_FFN0, updates[0].pre)
            keep_warm_update(pe, updates[1])
            turn_pe(pe, updates[1].pre)
            sgu_pe(pe, updates[1].pre)
            keep_warm_update(pe, updates[2])
            turn_pe(pe, updates[2].pre)
            ffn_pe(pe, ffn[1], N_FFN1, updates[2].pre)
            keep_warm_update(pe, updates[3])
            turn_pe(pe, updates[3].pre)
            mixer_in_pe(pe, updates[3].pre, at2)
            ssd_pe(pe)
            attn2_pe(pe)
            keep_warm_update(pe, updates[4])
            turn_pe(pe, updates[4].pre)
            mlp_pe(pe, updates[4].pre)


def head_order():
    order = []
    for t in range(QT):
        for half in range(2):
            h = REP * (2 * (t // REP) + half) + t % REP
            order += range(h * DH, (h + 1) * DH)
    return np.array(order)


def as_features(m):
    k, n = m.shape
    return m.reshape(KT, P, n // P, P).transpose(2, 1, 0, 3).reshape(n // P, P, KT * P)


def as_tokens(m, width):
    k, n = m.shape
    nk = UNIT // width
    v = m.reshape(KT // nk, nk, P, n // width, width).transpose(3, 0, 2, 1, 4)
    return v.reshape(-1, P, UNIT)


def as_rows(m):
    return m.reshape(-1, P, D)


def interleave(head, groups, tail):
    return np.concatenate([head, np.stack(groups, 1).reshape(-1, P, UNIT), tail])


def ffn_units(w_in, w_out):
    g, u, o = as_features(w_in[:, :FT * P]), as_features(w_in[:, FT * P:]), as_rows(w_out)
    return interleave(np.stack([g[0], u[0]]), [g[1:], u[1:], o[:-1]], o[-1:])


def qkv_units(q, k, v):
    return np.concatenate([as_features(q[:, head_order()]), as_features(k), as_tokens(v, 256)])


def tiles(v):
    return v.reshape(-1, P).T


def tables():
    p, f = np.arange(P)[:, None], np.arange(P)[None, :]
    masks = [p == f, p <= f, p > f, p >= f, p < f, p >= 0 * f]
    own = np.where(p >= f, p - f, FAR)
    before = np.where(f > p, p + P - f, FAR)
    near = []
    for b in range(TT):
        dist = np.abs(p + b * P - np.arange(SEQ)[None, :])
        near.append(np.where(dist <= P, dist, FAR))
    return np.concatenate([*masks, own, before, own, *near], 1).astype(np.float32)


def kernel(**inputs):
    from concourse import bacc
    from concourse.bass_utils import run_bass_kernel_spmd

    v = {k: np.asarray(a) for k, a in inputs.items()}
    arrays = layouts(v)
    nc = bacc.Bacc("TRN2", target_bir_lowering=False, num_devices=1)
    aps = {n: nc.dram_tensor("in_" + n, a.shape, F32, kind="ExternalInput").ap() for n, a in arrays.items()}
    out = nc.dram_tensor("out", (SEQ, D), F32, kind="ExternalOutput").ap()
    build(nc, *(aps[n] for n in ("w", "x", "cols", "misc", "tables", "rows", "ws", "wdt")), out)
    r = run_bass_kernel_spmd(nc, [{"in_" + n: a for n, a in arrays.items()}], core_ids=[0])
    return r.results[0]["out"].reshape(1, SEQ, D)


def layouts(v):
    order = head_order()
    qkv, win2 = v["attn_w_qkv"][0], v["w_in_2"][0]
    z, xbc, dt, q2, k2, v2 = np.split(win2, np.cumsum([D, XT * P, 32, QT * P, 256]), 1)
    wout2 = v["w_out_2"][0]
    up, down = as_features(v["w_up_2"][0]), as_rows(v["w_down_2"][0])
    w = np.concatenate([
        qkv_units(qkv[:, :D], qkv[:, D:D + 256], qkv[:, D + 256:])[QK_ORDER + [QKT, QKT + 1]],
        as_rows(v["attn_w_o"][0]),
        ffn_units(v["ffn_w_in"][0], v["ffn_w_out"][0]),
        as_tokens(v["sgu_w_in"][0][:, SG:], 512),
        as_features(v["sgu_w_in"][0][:, :SG]),
        as_rows(v["sgu_w_out"][0]),
        ffn_units(v["ffn_w_in"][1], v["ffn_w_out"][1]),
        np.stack([as_features(xbc), qkv_units(q2, k2, v2)], 1).reshape(-1, P, UNIT),
        as_tokens(z, 512),
        as_rows(wout2),
        interleave(up[:1], [up[1:], down[:-1]], down[-1:]),
    ])
    bq = v["attn_b_qkv"][0]
    gains = [v["norm_mix_pre"][0], v["norm_ffn_pre"][0], v["norm_mix_pre"][1], v["norm_ffn_pre"][1],
             v["norm_mix_pre_2"][0], v["norm_mlp_pre_2"][0], v["ssm_norm_2"][0]]
    conv = np.concatenate([v["ffn_conv_w"], v["ffn_conv_b"][:, None]], 1)
    conv = conv.reshape(2, 4, FT, P).transpose(3, 0, 2, 1).reshape(P, -1)
    xc = np.concatenate([v["conv_w_2"][0], v["conv_b_2"]], 0).reshape(6, XT, P).transpose(2, 1, 0).reshape(P, -1)
    ln = np.stack([v["sgu_ln_g"][0], v["sgu_ln_b"][0]]).reshape(2, SGT, P).transpose(2, 1, 0).reshape(P, -1)
    bqk = np.concatenate([tiles(bq[:D][order]), tiles(bq[D:D + 256])], 1)[:, QK_ORDER]
    cols = np.concatenate([*(tiles(g) for g in gains), bqk, conv, xc, ln], 1)
    misc = np.concatenate([v["attn_sinks"][0], v["attn_sink_2"][0], bq[D + 256:], v["dt_bias_2"].ravel(),
                           v["a_log_2"].ravel(), v["d_skip_2"].ravel(), v["sgu_b_s"].ravel()])[None]
    rows = np.stack([v["attn_b_o"][0], v["norm_mix_post"][0], v["norm_ffn_post"][0], v["norm_mix_post"][1],
                     v["norm_ffn_post"][1], v["norm_mix_post_2"][0], v["norm_mlp_post_2"][0]])
    ws = v["sgu_w_s"][0].transpose(2, 0, 1)
    wdt = dt.reshape(KT, P, 32).transpose(1, 0, 2)
    arrays = dict(w=w, x=v["x"][0], cols=cols, misc=misc, tables=tables(), rows=rows, ws=ws, wdt=wdt)
    return {k: np.ascontiguousarray(a) for k, a in arrays.items()}
```
